# Optimizing a Trainium2 kernel written in Bass

```python
import math
import jax, jax.numpy as jnp
from jax import lax
import numpy as np

D_MODEL = 1024
BATCH = 1
SEQ = 256
DEPTH = 1

CHUNK = 64
Q_BLOCK = 128
POOL_WINDOWS = (2, 4, 8, 16)
N_POOL_GROUPS = len(POOL_WINDOWS)
POOL_GROUP_DIM = D_MODEL // 8
POOL_DIM = N_POOL_GROUPS * POOL_GROUP_DIM
N_HEADS = 8
HEAD_DIM = D_MODEL // 16
V_HEAD_DIM = 2 * HEAD_DIM
QK_DIM = N_HEADS * 2 * HEAD_DIM
V_DIM = N_HEADS * V_HEAD_DIM
IN_DIM = POOL_DIM + 2 * QK_DIM + V_DIM
D_FF = 4 * D_MODEL
N_BRANCHES = 2
EPS = 1e-6


def rmsnorm(x, g):
    xf = x.astype(jnp.float32)
    y = xf * lax.rsqrt(jnp.mean(xf * xf, axis=-1, keepdims=True) + EPS)
    return (y * g.astype(jnp.float32)).astype(x.dtype)

def head_rmsnorm(x, g):
    xf = x.astype(jnp.float32)
    return xf * lax.rsqrt(jnp.mean(xf * xf, axis=-1, keepdims=True) + EPS) * g.astype(jnp.float32)

def alibi_slopes(n):
    return jnp.asarray(np.array([2.0 ** (-8.0 * (i + 1) / n) for i in range(n)], dtype=np.float32))

def pool_mixer(u, w_grp, scale):
    B, S, _ = u.shape
    uf = u.astype(jnp.float32).reshape(B, S, N_POOL_GROUPS, POOL_GROUP_DIM)
    csum = jnp.pad(jnp.cumsum(uf, axis=1), ((0, 0), (1, 0), (0, 0), (0, 0)))
    t = jnp.arange(S)
    pooled = []
    for g, w in enumerate(POOL_WINDOWS):
        lo = jnp.maximum(t + 1 - w, 0)
        win_sum = csum[:, 1:, g] - csum[:, lo, g]
        cnt = (t + 1 - lo).astype(jnp.float32)
        pooled.append(win_sum / cnt[None, :, None])
    mixed = jnp.stack(pooled, axis=2) - uf
    y = jnp.einsum('bsgc,gcd->bsgd', mixed, w_grp.astype(jnp.float32))
    return (y.reshape(B, S, POOL_DIM) * scale.astype(jnp.float32)).astype(u.dtype)

def diff_attention(q, k, v, g_q, g_k, lam, g_sub, lambda_init):
    B, S = q.shape[0], q.shape[1]
    qn = head_rmsnorm(q, g_q) * (HEAD_DIM ** -0.5)
    kn = head_rmsnorm(k, g_k)
    vf = v.astype(jnp.float32)
    lam = lam.astype(jnp.float32)
    slopes = alibi_slopes(N_HEADS)
    pos = jnp.arange(S)
    key_chunk = pos // CHUNK
    nb = S // Q_BLOCK
    q_blocks = qn.reshape(B, nb, Q_BLOCK, N_HEADS, 2, HEAD_DIM).transpose(1, 0, 2, 3, 4, 5)
    q_pos = pos.reshape(nb, Q_BLOCK)
    neg = jnp.finfo(jnp.float32).min

    def block(args):
        qblk, qp = args
        s = jnp.einsum('bqhid,bkhid->bihqk', qblk, kn)
        dist = jnp.abs(qp[:, None] - pos[None, :]).astype(jnp.float32)
        bias = -slopes[:, None, None] * dist
        allowed = key_chunk[None, :] <= (qp // CHUNK)[:, None]
        s = jnp.where(allowed, s + bias, neg)
        p = jax.nn.softmax(s, axis=-1)
        a = p[:, 0] - lam * p[:, 1]
        return jnp.einsum('bhqk,bkhe->bqhe', a, vf)

    o = lax.map(block, (q_blocks, q_pos))
    o = o.transpose(1, 0, 2, 3, 4).reshape(B, S, N_HEADS, V_HEAD_DIM)
    o = head_rmsnorm(o, g_sub) * (1.0 - lambda_init)
    return o.reshape(B, S, V_DIM).astype(v.dtype)

def first_inputs(seed: int = 0) -> dict:
    key = jax.random.key(seed)
    ks = jax.random.split(key, 20)
    f32 = jnp.float32

    def nrm(k, shape, fan_in):
        return jax.random.normal(k, shape, f32) * (fan_in ** -0.5)

    def gain(k, shape):
        return 1.0 + 0.05 * jax.random.normal(k, shape, f32)

    return {
        "x": jax.random.normal(ks[0], (BATCH, SEQ, D_MODEL), f32),
        "g_mix": gain(ks[1], (DEPTH, D_MODEL)),
        "w_in": nrm(ks[2], (DEPTH, D_MODEL, IN_DIM), D_MODEL),
        "w_pool_grp": nrm(ks[3], (DEPTH, N_POOL_GROUPS, POOL_GROUP_DIM, POOL_GROUP_DIM), POOL_GROUP_DIM),
        "pool_scale": gain(ks[4], (DEPTH, POOL_DIM)),
        "g_q": gain(ks[5], (DEPTH, HEAD_DIM)),
        "g_k": gain(ks[6], (DEPTH, HEAD_DIM)),
        "lambda_qk": 0.1 * jax.random.normal(ks[7], (DEPTH, 4, HEAD_DIM), f32),
        "g_sub": gain(ks[8], (DEPTH, V_HEAD_DIM)),
        "w_branch_pool": nrm(ks[9], (DEPTH, POOL_DIM, D_MODEL), POOL_DIM),
        "w_branch_attn": nrm(ks[10], (DEPTH, V_DIM, D_MODEL), V_DIM),
        "w_gate": nrm(ks[11], (DEPTH, D_MODEL, N_BRANCHES * D_MODEL), D_MODEL),
        "b_gate": 0.01 * jax.random.normal(ks[12], (DEPTH, N_BRANCHES * D_MODEL), f32),
        "w_out": nrm(ks[13], (DEPTH, D_MODEL, D_MODEL), D_MODEL),
        "g_ffn": gain(ks[14], (DEPTH, D_MODEL)),
        "w_up": nrm(ks[15], (DEPTH, D_MODEL, D_FF), D_MODEL),
        "w_down": nrm(ks[16], (DEPTH, D_FF, D_MODEL), D_FF),
    }

def first_block(x, g_mix, w_in, w_pool_grp, pool_scale, g_q, g_k, lambda_qk, g_sub,
              w_branch_pool, w_branch_attn, w_gate, b_gate, w_out, g_ffn, w_up, w_down):
    B, S, _ = x.shape
    for l in range(DEPTH):
        lambda_init = 0.8 - 0.6 * math.exp(-0.3 * l)
        h = rmsnorm(x, g_mix[l])
        z = h @ w_in[l]
        u_pool = z[..., :POOL_DIM]
        q = z[..., POOL_DIM:POOL_DIM + QK_DIM].reshape(B, S, N_HEADS, 2, HEAD_DIM)
        k = z[..., POOL_DIM + QK_DIM:POOL_DIM + 2 * QK_DIM].reshape(B, S, N_HEADS, 2, HEAD_DIM)
        v = z[..., POOL_DIM + 2 * QK_DIM:].reshape(B, S, N_HEADS, V_HEAD_DIM)

        y_pool = pool_mixer(u_pool, w_pool_grp[l], pool_scale[l])
        lq = lambda_qk[l].astype(jnp.float32)
        lam = jnp.exp(jnp.sum(lq[0] * lq[1])) - jnp.exp(jnp.sum(lq[2] * lq[3])) + lambda_init
        y_attn = diff_attention(q, k, v, g_q[l], g_k[l], lam, g_sub[l], lambda_init)

        gates = jax.nn.sigmoid(h @ w_gate[l] + b_gate[l])
        merged = (gates[..., :D_MODEL] * (y_pool @ w_branch_pool[l])
                  + gates[..., D_MODEL:] * (y_attn @ w_branch_attn[l]))
        x = x + merged @ w_out[l]

        h2 = rmsnorm(x, g_ffn[l])
        x = x + jnp.square(jax.nn.relu(h2 @ w_up[l])) @ w_down[l]
    return x


GRID_W = 64
CTX_LEN = 256
MLA_HEADS = 8
MLA_NOPE = 64
MLA_ROPE = 32
MLA_QK = MLA_NOPE + MLA_ROPE
MLA_V = 64
Q_LORA = 384
KV_LORA = 256
NA_HEADS = 8
NA_DIM = 64
NA_WIN_H = 8
NA_WIN_W = 16
MIX_WIDTH = MLA_HEADS * MLA_V + NA_HEADS * NA_DIM
Q_COLS = Q_LORA + NA_HEADS * NA_DIM
KV_COLS = KV_LORA + MLA_ROPE + 2 * NA_HEADS * NA_DIM
N_GROUPS = 4
EXPERTS_PER_GROUP = 4
N_EXPERTS = N_GROUPS * EXPERTS_PER_GROUP
TOP_K_IN_GROUP = 2
D_EXPERT = 512
ROPE_THETA = 10000.0
NORM_EPS = 1e-6
MASK_VALUE = -1e30


def rmsnorm_2(x, g):
    xf = x.astype(jnp.float32)
    y = xf * lax.rsqrt(jnp.mean(xf * xf, axis=-1, keepdims=True) + NORM_EPS)
    return (y * g.astype(jnp.float32)).astype(x.dtype)

def adaln(cond, w_mod, b_mod):
    return jnp.split(jax.nn.silu(cond) @ w_mod + b_mod, 6, axis=-1)

def modulate(h, shift, scale):
    return h * (1 + scale) + shift

def axial_rope_tables(row, col, dtype):
    half = MLA_ROPE // 2
    inv_freq = ROPE_THETA ** (-jnp.arange(0, half, 2, dtype=jnp.float32) / half)
    ang = jnp.concatenate([row.astype(jnp.float32)[:, None] * inv_freq,
                           col.astype(jnp.float32)[:, None] * inv_freq], axis=-1)
    return jnp.cos(ang).astype(dtype), jnp.sin(ang).astype(dtype)

def apply_rope(x, cos, sin):
    x1, x2 = jnp.split(x, 2, axis=-1)
    c, s = cos[:, None, :], sin[:, None, :]
    return jnp.concatenate([x1 * c - x2 * s, x1 * s + x2 * c], axis=-1)

def mixer_queries(pq, q_a_g, w_uq):
    B, L, _ = pq.shape
    q_lat, na_q = jnp.split(pq, [Q_LORA], axis=-1)
    q_mla = (rmsnorm_2(q_lat, q_a_g) @ w_uq).reshape(B, L, MLA_HEADS, MLA_QK)
    return q_mla, na_q.reshape(B, L, NA_HEADS, NA_DIM)

def mixer_keys_values(pkv, kv_a_g, w_ukv):
    B, L, _ = pkv.shape
    kv_lat, k_rope, na_k, na_v = jnp.split(
        pkv, [KV_LORA, KV_LORA + MLA_ROPE, KV_LORA + MLA_ROPE + NA_HEADS * NA_DIM], axis=-1)
    kv = (rmsnorm_2(kv_lat, kv_a_g) @ w_ukv).reshape(B, L, MLA_HEADS, MLA_NOPE + MLA_V)
    k_nope, v_mla = jnp.split(kv, [MLA_NOPE], axis=-1)
    return (k_nope, k_rope, v_mla,
            na_k.reshape(B, L, NA_HEADS, NA_DIM), na_v.reshape(B, L, NA_HEADS, NA_DIM))

def mla_keys(k_nope, k_rope_b):
    return jnp.concatenate([k_nope, jnp.broadcast_to(k_rope_b, k_nope.shape[:3] + (MLA_ROPE,))], axis=-1)

def dense_attention(q, k, v):
    s = jnp.einsum('bqhd,bkhd->bhqk', q, k).astype(jnp.float32) * (q.shape[-1] ** -0.5)
    p = jax.nn.softmax(s, axis=-1).astype(v.dtype)
    return jnp.einsum('bhqk,bkhd->bqhd', p, v)

def mla_latent_attention(q, k, v, k_ctx, v_ctx):
    B, N, H, Dq = q.shape
    k_all = jnp.concatenate([k_ctx, k], axis=1)
    v_all = jnp.concatenate([v_ctx, v], axis=1)
    q_blocks = jnp.moveaxis(q.reshape(B, N // Q_BLOCK, Q_BLOCK, H, Dq), 1, 0)
    out = lax.map(lambda qb: dense_attention(qb, k_all, v_all), q_blocks)
    return jnp.moveaxis(out, 0, 1).reshape(B, N, H, v.shape[-1])

def neighbourhood_attention(q, k, v, k_ctx, v_ctx, rel_bias):
    B, N, H, Dh = q.shape
    rows = N // GRID_W
    kh = min(NA_WIN_H, rows)
    kw = NA_WIN_W
    scale = Dh ** -0.5
    qg = jnp.moveaxis(q.reshape(B, rows, GRID_W, H, Dh), 1, 0)
    kg = k.reshape(B, rows, GRID_W, H, Dh)
    vg = v.reshape(B, rows, GRID_W, H, Dh)
    col = jnp.arange(GRID_W)
    col_start = jnp.clip(col - kw // 2, 0, GRID_W - kw)
    col_in = (col[None, :] >= col_start[:, None]) & (col[None, :] < col_start[:, None] + kw)
    bias_cols = rel_bias[:, :, col[None, :] - col[:, None] + (NA_WIN_W - 1)]

    def one_row(args):
        r, qr = args
        start = jnp.clip(r - kh // 2, 0, rows - kh)
        kr = lax.dynamic_slice_in_dim(kg, start, kh, axis=1)
        vr = lax.dynamic_slice_in_dim(vg, start, kh, axis=1)
        bias = bias_cols[:, start + jnp.arange(kh) - r + (NA_WIN_H - 1)]
        s = jnp.einsum('bqhd,bjkhd->bhqjk', qr, kr).astype(jnp.float32) * scale
        s = s + jnp.transpose(bias, (0, 2, 1, 3)).astype(jnp.float32)[None]
        s = jnp.where(col_in[None, None, :, None, :], s, MASK_VALUE).reshape(B, H, GRID_W, kh * GRID_W)
        s_ctx = jnp.einsum('bqhd,bchd->bhqc', qr, k_ctx).astype(jnp.float32) * scale
        p = jax.nn.softmax(jnp.concatenate([s, s_ctx], axis=-1), axis=-1).astype(v.dtype)
        p_win = p[..., :kh * GRID_W].reshape(B, H, GRID_W, kh, GRID_W)
        p_ctx = p[..., kh * GRID_W:]
        return (jnp.einsum('bhqjk,bjkhd->bqhd', p_win, vr)
                + jnp.einsum('bhqc,bchd->bqhd', p_ctx, v_ctx))

    out = lax.map(one_row, (jnp.arange(rows), qg))
    return jnp.moveaxis(out, 0, 1).reshape(B, N, H, Dh)

def hierarchical_moe(h, w_rg, b_rg, w_re, b_re, w_gate, w_up, w_down):
    B, L, D = h.shape
    t = h.reshape(B * L, D)
    T = t.shape[0]
    g_logits = (t @ w_rg + b_rg).astype(jnp.float32)
    g_prob = jax.nn.softmax(g_logits, axis=-1)
    g_sel = jnp.argmax(g_logits, axis=-1)
    g_w = jnp.take_along_axis(g_prob, g_sel[:, None], axis=-1)
    e_logits = (t @ w_re + b_re).astype(jnp.float32).reshape(T, N_GROUPS, EXPERTS_PER_GROUP)
    e_logits = jnp.take_along_axis(e_logits, g_sel[:, None, None], axis=1)[:, 0]
    top_p, top_i = lax.top_k(jax.nn.softmax(e_logits, axis=-1), TOP_K_IN_GROUP)
    top_p = top_p / jnp.sum(top_p, axis=-1, keepdims=True)
    within = jnp.sum(jax.nn.one_hot(top_i, EXPERTS_PER_GROUP, dtype=jnp.float32) * top_p[..., None], axis=1)
    combine = (jax.nn.one_hot(g_sel, N_GROUPS, dtype=jnp.float32)[:, :, None]
               * (g_w * within)[:, None, :]).astype(h.dtype)
    wg = w_gate.reshape(N_GROUPS, EXPERTS_PER_GROUP, D, D_EXPERT)
    wu = w_up.reshape(N_GROUPS, EXPERTS_PER_GROUP, D, D_EXPERT)
    wd = w_down.reshape(N_GROUPS, EXPERTS_PER_GROUP, D_EXPERT, D)

    def one_group(args):
        wg_g, wu_g, wd_g, comb_g = args
        hid = jax.nn.silu(jnp.einsum('td,edf->tef', t, wg_g)) * jnp.einsum('td,edf->tef', t, wu_g)
        return jnp.einsum('tef,efd->td', hid * comb_g[:, :, None], wd_g)

    y = jnp.sum(lax.map(one_group, (wg, wu, wd, jnp.moveaxis(combine, 1, 0))), axis=0)
    return y.reshape(B, L, D)

def second_inputs(seed: int = 0) -> dict:
    key = jax.random.key(seed)
    ks = jax.random.split(key, 24)
    D = D_MODEL

    def nrm(k, shape, scale):
        return jax.random.normal(k, shape, jnp.float32) * scale

    return {
        'x': nrm(ks[0], (BATCH, SEQ, D), 1.0),
        'c': nrm(ks[1], (BATCH, D), 1.0),
        'ctx': nrm(ks[2], (BATCH, CTX_LEN, D), 1.0),
        'c_ctx': nrm(ks[3], (D,), 1.0),
        'w_mod': nrm(ks[4], (DEPTH, D, 6 * D), 0.5 * D ** -0.5),
        'b_mod': nrm(ks[5], (DEPTH, 6 * D), 0.02),
        'norm_attn_g': 1.0 + nrm(ks[6], (DEPTH, D), 0.02),
        'norm_ffn_g': 1.0 + nrm(ks[7], (DEPTH, D), 0.02),
        'w_in': nrm(ks[8], (DEPTH, D, Q_COLS + KV_COLS), D ** -0.5),
        'q_a_norm_g': 1.0 + nrm(ks[9], (DEPTH, Q_LORA), 0.02),
        'kv_a_norm_g': 1.0 + nrm(ks[10], (DEPTH, KV_LORA), 0.02),
        'w_uq': nrm(ks[11], (DEPTH, Q_LORA, MLA_HEADS * MLA_QK), Q_LORA ** -0.5),
        'w_ukv': nrm(ks[12], (DEPTH, KV_LORA, MLA_HEADS * (MLA_NOPE + MLA_V)), KV_LORA ** -0.5),
        'na_rel_bias': nrm(ks[13], (DEPTH, NA_HEADS, 2 * NA_WIN_H - 1, 2 * NA_WIN_W - 1), 0.5),
        'w_out': nrm(ks[14], (DEPTH, MIX_WIDTH, D), MIX_WIDTH ** -0.5),
        'w_router_group': nrm(ks[15], (DEPTH, D, N_GROUPS), D ** -0.5),
        'b_router_group': nrm(ks[16], (DEPTH, N_GROUPS), 0.01),
        'w_router_expert': nrm(ks[17], (DEPTH, D, N_EXPERTS), D ** -0.5),
        'b_router_expert': nrm(ks[18], (DEPTH, N_EXPERTS), 0.01),
        'w_gate': nrm(ks[19], (DEPTH, N_EXPERTS, D, D_EXPERT), D ** -0.5),
        'w_up': nrm(ks[20], (DEPTH, N_EXPERTS, D, D_EXPERT), D ** -0.5),
        'w_down': nrm(ks[21], (DEPTH, N_EXPERTS, D_EXPERT, D), D_EXPERT ** -0.5),
        'final_norm_g': 1.0 + nrm(ks[22], (D,), 0.02),
    }

def second_block(x, c, ctx, c_ctx, w_mod, b_mod, norm_attn_g, norm_ffn_g, w_in, q_a_norm_g, kv_a_norm_g,
              w_uq, w_ukv, na_rel_bias, w_out, w_router_group, b_router_group, w_router_expert,
              b_router_expert, w_gate, w_up, w_down, final_norm_g):
    B, N, D = x.shape
    pos = jnp.arange(N)
    cos, sin = axial_rope_tables(pos // GRID_W, pos % GRID_W, x.dtype)
    for l in range(DEPTH):
        sh1, sc1, g1, sh2, sc2, g2 = [m[:, None, :] for m in adaln(c, w_mod[l], b_mod[l])]
        csh1, csc1, cg1, csh2, csc2, cg2 = adaln(c_ctx, w_mod[l], b_mod[l])
        hx = modulate(rmsnorm_2(x, norm_attn_g[l]), sh1, sc1)
        hc = modulate(rmsnorm_2(ctx, norm_attn_g[l]), csh1, csc1)

        kn_c, kr_c, v_c, nk_c, nv_c = mixer_keys_values(hc @ w_in[l][:, Q_COLS:], kv_a_norm_g[l], w_ukv[l])
        k_c = mla_keys(kn_c, kr_c[:, :, None, :])

        proj = hx @ w_in[l]
        q_m, nq = mixer_queries(proj[..., :Q_COLS], q_a_norm_g[l], w_uq[l])
        kn, kr, v_m, nk, nv = mixer_keys_values(proj[..., Q_COLS:], kv_a_norm_g[l], w_ukv[l])
        q_m = jnp.concatenate([q_m[..., :MLA_NOPE], apply_rope(q_m[..., MLA_NOPE:], cos, sin)], axis=-1)
        k_m = mla_keys(kn, apply_rope(kr[:, :, None, :], cos, sin))
        o_mla = mla_latent_attention(q_m, k_m, v_m, k_c, v_c)
        o_na = neighbourhood_attention(nq, nk, nv, nk_c, nv_c, na_rel_bias[l])
        mixed = jnp.concatenate([o_mla.reshape(B, N, -1), o_na.reshape(B, N, -1)], axis=-1) @ w_out[l]

        if l < DEPTH - 1:
            Bc, C = ctx.shape[:2]
            q_c, nq_c = mixer_queries(hc @ w_in[l][:, :Q_COLS], q_a_norm_g[l], w_uq[l])
            mixed_c = jnp.concatenate([dense_attention(q_c, k_c, v_c).reshape(Bc, C, -1),
                                       dense_attention(nq_c, nk_c, nv_c).reshape(Bc, C, -1)], axis=-1) @ w_out[l]
            ctx = ctx + cg1 * mixed_c
            hc2 = modulate(rmsnorm_2(ctx, norm_ffn_g[l]), csh2, csc2)
            ctx = ctx + cg2 * hierarchical_moe(hc2, w_router_group[l], b_router_group[l], w_router_expert[l],
                                               b_router_expert[l], w_gate[l], w_up[l], w_down[l])

        x = x + g1 * mixed
        hx2 = modulate(rmsnorm_2(x, norm_ffn_g[l]), sh2, sc2)
        x = x + g2 * hierarchical_moe(hx2, w_router_group[l], b_router_group[l], w_router_expert[l],
                                      b_router_expert[l], w_gate[l], w_up[l], w_down[l])
    return rmsnorm_2(x, final_norm_g)


def setup_inputs(seed=0):
    out = dict(first_inputs(seed))
    for name, value in second_inputs(seed + 1).items():
        if name != "x":
            out[name + "_2"] = value
    return out


def reference(
    x, g_mix, w_in, w_pool_grp, pool_scale, g_q, g_k, lambda_qk, g_sub, w_branch_pool,
    w_branch_attn, w_gate, b_gate, w_out, g_ffn, w_up, w_down, c_2, ctx_2, c_ctx_2, w_mod_2,
    b_mod_2, norm_attn_g_2, norm_ffn_g_2, w_in_2, q_a_norm_g_2, kv_a_norm_g_2, w_uq_2, w_ukv_2,
    na_rel_bias_2, w_out_2, w_router_group_2, b_router_group_2, w_router_expert_2,
    b_router_expert_2, w_gate_2, w_up_2, w_down_2, final_norm_g_2,
):
    x = first_block(
        x, g_mix, w_in, w_pool_grp, pool_scale, g_q, g_k, lambda_qk, g_sub, w_branch_pool,
        w_branch_attn, w_gate, b_gate, w_out, g_ffn, w_up, w_down,
    )
    return second_block(
        x, c_2, ctx_2, c_ctx_2, w_mod_2, b_mod_2, norm_attn_g_2, norm_ffn_g_2, w_in_2,
        q_a_norm_g_2, kv_a_norm_g_2, w_uq_2, w_ukv_2, na_rel_bias_2, w_out_2, w_router_group_2,
        b_router_group_2, w_router_expert_2, b_router_expert_2, w_gate_2, w_up_2, w_down_2,
        final_norm_g_2,
    )


_drawn_inputs = setup_inputs


def setup_inputs(seed=0):
    import zlib

    import numpy as np

    out = dict(_drawn_inputs(seed))
    spreads = {}
    factors = {'b_gate': 8.0,
     'ctx_2': 3.628,
     'b_mod_2': 5.407,
     'norm_attn_g_2': 8.0,
     'norm_ffn_g_2': 8.0,
     'q_a_norm_g_2': 8.0,
     'kv_a_norm_g_2': 8.0,
     'w_uq_2': 4.327,
     'na_rel_bias_2': 8.0,
     'b_router_group_2': 8.0,
     'b_router_expert_2': 31.8,
     'final_norm_g_2': 9.056}
    for name, (base, spread) in spreads.items():
        noise = np.random.default_rng([zlib.crc32(name.encode()), seed]).standard_normal(out[name].shape)
        drawn = base * np.exp(spread * noise) if base else spread * noise
        out[name] = __import__('jax').numpy.asarray(drawn.astype(out[name].dtype))
    for name, factor in factors.items():
        out[name] = (out[name] * factor).astype(out[name].dtype)
    return out
```

```python
from contextlib import ExitStack

import numpy as np
import concourse.bass as bass
from concourse import mybir

F32 = mybir.dt.float32
F32R = mybir.dt.float32r
ALU = mybir.AluOpType
ACT = mybir.ActivationFunctionType
AX = mybir.AxisListType

P = 128
S = 256
ST = S // P
D = 1024
KD = D // P
NB = 512
EPS = 1e-6
HEADS = 8
POOL_WINDOWS = (2, 4, 8, 16)
POOL_DIM = 512
D_FF = 4096
LAMBDA_INIT = 0.8 - 0.6 * float(np.exp(-0.3 * 0))
CHUNK = 64
CTX = 256
TT = (S + CTX) // P
Q_LORA, KV_LORA, ROPE, NOPE = 384, 256, 32, 64
QK = NOPE + ROPE
GRID_W, WIN_W = 64, 16
N_GROUPS, PER_GROUP = 4, 4
N_EXPERTS = N_GROUPS * PER_GROUP
D_EXPERT = 512
SLOTS = 128
BIG = -1e30

PIECE = 1024
N_PIECES = 4
N_RAW = 5

X_AT, B_AT, C_AT, D_AT, E_AT, G_AT, T_AT, M_AT, Z_AT = 0, 2048, 4096, 6144, 8192, 10240, 14336, 16384, 17408
ARENA = 18432
K_IDENT, K_DIST, K_SLOPE = 0, 128, 640
K_TRI, K_IOTA, K_ROPE, K_COLMASK, K_ONES = 128, 640, 768, 832, 896
K_COLS, K_SEL = 1664, 1792
K_MHALF = 1922
K_LAM = 1986

COLS = [("g_mix", 8), ("g_ffn", 8), ("norm_attn_g", 8), ("pool_scale", 4), ("g_q", 1), ("g_k", 1),
        ("g_sub", 1), ("q_a_g", 3), ("kv_a_g", 2), ("c", 8), ("c_ctx", 8)]
COL0, _at = {}, 0
for _n, _w in COLS:
    COL0[_n] = _at
    _at += _w
N_COLS = _at


def unit_table():
    t = []
    t += [("w_in", n, 8, 512, 1) for n in range(7)]
    t += [("w_gate", n, 8, 512, 1) for n in range(4)]
    t += [("w_bp", 0, 4, 512, 2)]
    t += [("w_ba", n, 4, 512, 2) for n in range(2)]
    t += [("w_out", n, 8, 512, 1) for n in range(2)]
    for n in range(2):
        t += [("w_up", n, 8, 512, 1)]
    for n in range(2, 10):
        t += [("w_down", n - 2, 4, 512, 2)]
        if n < 8:
            t += [("w_up", n, 8, 512, 1)]
    return t


def block_two_units():
    t = [("w_in2kv", 0, 8, 288, 1), ("w_in2k", 0, 8, 512, 1), ("w_in2v", 0, 8, 512, 1),
         ("w_in2q", 0, 8, 384, 1), ("w_in2nq", 0, 8, 512, 1)]
    t += [("w_uq", 0, 3, 384, 2)]
    t += [("w_ukv", n, 2, 512, 1) for n in range(2)]
    t += [("w_mod", n, 8, 512, 1) for n in (4, 5)]
    t += [("w_out2", n, 8, 512, 1) for n in range(2)]
    t += [("w_mod", n, 8, 512, 1) for n in (6, 7, 8, 9)]
    t += [("w_mod", n, 8, 512, 1) for n in (10, 11)]
    for e in range(N_EXPERTS):
        t += [("wg", e, 8, 512, 1), ("wu", e, 8, 512, 1)]
        if e > 0:
            t += [("wd", e - 1, 4, 512, 2)]
    t += [("wd", N_EXPERTS - 1, 4, 512, 2)]
    return t


UNITS = [("w_mod", n, 8, 512, 1) for n in range(4)] + unit_table() + block_two_units()


class Lane:

    def __init__(self, name, sem):
        self.name, self.sem, self.count, self.ops, self.seen = name, sem, 0, [], {}

    def __call__(self, fn, *after, mark=True):
        self.ops.append((self.needed(after), fn, self.sem if mark else None, 1))
        if mark:
            self.count += 1
            return (self.sem, self.count)
        return None

    def needed(self, after):
        out = []
        for m in flat(after):
            if self.seen.get(id(m[0]), 0) < m[1]:
                self.seen[id(m[0])] = m[1]
                out.append(m)
        return out

    def dma(self, fn, line, *after):
        self.ops.append((self.needed(after), fn, line.sem, 16))
        line.count += 16
        return (line.sem, line.count)

    def now(self):
        return (self.sem, self.count) if self.count else None

    def only_if(self, flag, least, ready, section):
        self.ops.append((self.needed([ready]), (flag, least, section), None, 0))

    def play(self, eng):
        for waits, fn, sem, by in self.ops:
            for s, v in waits:
                eng.wait_ge(s, v)
            if isinstance(fn, tuple):
                flag, least, section = fn
                value = eng.value_load(flag)
                with eng.If(value >= least):
                    section.play(eng)
                continue
            ins = fn(eng)
            if sem is not None:
                ins.then_inc(sem, by)


def flat(x):
    if x is None:
        return
    if isinstance(x, tuple) and len(x) == 2 and isinstance(x[1], int):
        yield x
        return
    for y in x:
        yield from flat(y)


class Line:
    def __init__(self, sem):
        self.sem, self.count = sem, 0


class Bank:

    def __init__(self, ap):
        self.ap, self.free = ap, None


class Piece:

    def __init__(self, name, n, load, raw0, cols, blocks):
        self.name, self.n, self.load, self.raw0, self.cols, self.blocks = name, n, load, raw0, cols, blocks
        self.split = None
        self.used = None


class Split:

    def __init__(self, hi, lo):
        self.hi, self.lo, self.ready = hi, lo, None


class Stop(Exception):
    pass


class Program:
    def __init__(self, nc, ctx, dram, upto=None, probe=None):
        self.nc, self.ctx, self.dram, self.upto, self.probe = nc, ctx, dram, upto, probe
        sem = lambda n: ctx.enter_context(nc.semaphore(n))
        self.lines = []
        self.pe, self.dve, self.act, self.pool, self.sp = (
            Lane(n, sem("done_" + n)) for n in ("pe", "dve", "act", "pool", "sp"))
        sb = lambda n, w, dt=F32: ctx.enter_context(nc.sbuf_tensor(n, [P, w], dt))
        self.raw = sb("raw_weights", N_RAW * 2 * PIECE)
        self.whi = sb("weights_hi", N_PIECES * PIECE, F32R)
        self.wlo = sb("weights_lo", N_PIECES * PIECE, F32R)
        self.R = sb("split_arena", 12800, F32R)
        self.F = [[0, sb("arena_x", B_AT)], [B_AT, None], [D_AT, sb("arena", ARENA - D_AT)]]
        self.K = sb("constants", 2048)
        self.stats = sb("stats", 1024)
        self.middle = ctx.enter_context(ExitStack())
        self.F[1][1] = self.middle.enter_context(nc.sbuf_tensor("arena_middle", [P, D_AT - B_AT], F32))
        self.stat_at = 0
        ps = ctx.enter_context(nc.psum_tensor("psum", [P, 8, NB], F32))
        self.ps = ps
        self.banks = [Bank(ps[:, i, :]) for i in range(8)]
        self.raw_lines = [self.newline(f"raw_{i}") for i in range(N_RAW)]
        self.plan_weights()

    def newline(self, name):
        self.lines.append(Line(self.ctx.enter_context(self.nc.semaphore(name))))
        return self.lines[-1]

    def stat(self, n):
        a = self.stats[:, self.stat_at:self.stat_at + n]
        self.stat_at += n
        assert self.stat_at <= 1024
        return a

    def middle_for_splits(self):
        self.middle.close()
        self.F[1][1] = self.middle.enter_context(self.nc.sbuf_tensor("arena_middle_split", [P, D_AT - B_AT], F32R))

    def f(self, at, *dims):
        n = int(np.prod(dims))
        first, arena = [a for a in self.F if a[0] <= at][-1]
        v = arena[:, at - first:at - first + n]
        return split_dims(v, dims)

    def r(self, at, *dims):
        n = int(np.prod(dims))
        return split_dims(self.R[:, at:at + n], dims)

    def k(self, at, *dims):
        n = int(np.prod(dims))
        return split_dims(self.K[:, at:at + n], dims)

    def plan_weights(self):
        self.loads, self.pieces = [], []
        for name, n, kt, w, chunks in UNITS:
            total = kt * w * chunks
            blocks = [(k, c, (k * chunks + c) * w, w) for k in range(kt) for c in range(chunks)]
            per = PIECE // w if chunks == 1 else chunks
            cut = [blocks[i:i + per] for i in range(0, len(blocks), per)]
            for i in range(0, len(cut), 2):
                pair = cut[i:i + 2]
                c0 = pair[0][0][2]
                c1 = pair[-1][-1][2] + w
                load = dict(name=name, n=n, c0=c0, c1=c1, pieces=[], mark=None)
                for bl in pair:
                    pc = Piece(name, n, len(self.loads), bl[0][2] - c0, len(bl) * w,
                               [(k, c, at - bl[0][2], w) for k, c, at, w in bl])
                    load["pieces"].append(pc)
                    self.pieces.append(pc)
                self.loads.append(load)
            assert total == blocks[-1][2] + w
        self.next_piece = self.next_split = self.next_load = 0

    def feed(self):
        while True:
            moved = False
            i = self.next_load
            if i < len(self.loads):
                old = self.loads[i - N_RAW]["pieces"] if i >= N_RAW else []
                if all(p.split for p in old):
                    ld = self.loads[i]
                    dst = self.raw[:, (i % N_RAW) * 2 * PIECE:(i % N_RAW) * 2 * PIECE + ld["c1"] - ld["c0"]]
                    src = self.dram[ld["name"]][ld["n"], :, ld["c0"]:ld["c1"]]
                    ld["mark"] = self.sp.dma(lambda e, d=dst, s=src: e.dma_start(d, s), self.raw_lines[i % N_RAW],
                                             [p.split for p in old])
                    self.next_load += 1
                    moved = True
            j = self.next_split
            if j < len(self.pieces) and j < self.next_piece + N_PIECES:
                pc = self.pieces[j]
                ld = self.loads[pc.load]
                if ld["mark"] is not None:
                    old = self.pieces[j - N_PIECES].used if j >= N_PIECES else None
                    slot = (j % N_PIECES) * PIECE
                    pc.hi = self.whi[:, slot:slot + pc.cols]
                    pc.lo = self.wlo[:, slot:slot + pc.cols]
                    r0 = (pc.load % N_RAW) * 2 * PIECE + pc.raw0
                    raw = self.raw[:, r0:r0 + pc.cols]
                    hi = self.act(lambda e, o=pc.hi, i=raw: e.activation(o, i, ACT.Copy), ld["mark"], old)
                    lo = self.dve(lambda e, o=pc.lo, i=raw, h=pc.hi: e.tensor_tensor(o, i, h.bitcast(F32), ALU.subtract),
                                  ld["mark"], old, hi)
                    pc.split = [hi, lo]
                    self.next_split += 1
                    moved = True
            if not moved:
                return

    def take(self, name, n):
        self.feed()
        pc = self.pieces[self.next_piece]
        assert (pc.name, pc.n) == (name, n), ((pc.name, pc.n), (name, n))
        assert pc.split
        return pc

    def gemm(self, name, n, kt, lhs, tiles, out, banks, k0=0, first=True, last=True, after=None):
        started = set()
        npieces = sum(1 for p in self.pieces if (p.name, p.n) == (name, n))
        mark = None
        for i in range(npieces):
            pc = self.take(name, n)
            wait = [pc.split, lhs.ready, after, [b.free for b in banks]]
            for t in tiles:
                for k, c, at, w in pc.blocks:
                    o = out(t, c)
                    st = first and k == 0
                    en = last and k == kt - 1
                    ah, al = lhs.hi(k0 + k, t), lhs.lo(k0 + k, t)
                    wh, wl = pc.hi[:, at:at + w], pc.lo[:, at:at + w]
                    self.pe(lambda e, o=o, a=ah, b=wh, s=st: e.matmul(o, a, b, start=s, stop=False), wait, mark=False)
                    wait = None
                    self.pe(lambda e, o=o, a=ah, b=wl: e.matmul(o, a, b, start=False, stop=False), mark=False)
                    final = t == tiles[-1] and (k, c, at, w) == pc.blocks[-1]
                    mark = self.pe(lambda e, o=o, a=al, b=wh, z=en: e.matmul(o, a, b, start=False, stop=z), mark=final)
            pc.used = mark
            self.next_piece += 1
            if i < npieces - 1:
                self.feed()
                yield None
        self.last_gemm = mark
        yield mark

    def run(self, gen, between=None):
        m = None
        for i, m in enumerate(gen):
            for step in (between or {}).get(i, ()):
                step()
        return m

    def rstd(self, ss, out, n, *after):
        w = ss.shape[-1]
        t = self.stat(w)
        a = self.pool(lambda e: e.tensor_scalar(t, ss, 1.0 / n, EPS, ALU.mult, ALU.add), *after)
        return self.pool(lambda e: e.tensor_tensor(out, t, self.minus_half[:, 0:w], ALU.pow), a, self.const_ready)

    def row_norm(self, src, tiles, dst, scratch, *after):
        ss, rs = self.stat(tiles), self.stat(tiles)
        ms = []
        for t in range(tiles):
            i, o, acc = src(t), scratch(t), ss[:, t:t + 1]
            if t % 2 == 0:
                ms.append(self.act(lambda e, i=i, o=o, acc=acc: e.activation(o, i, ACT.Square, accum_out=acc), *after))
            else:
                ms.append(self.dve(lambda e, i=i, o=o, acc=acc: e.scalar_tensor_tensor(
                    out=o, in0=i, scalar=1.0, in1=i, op0=ALU.mult, op1=ALU.mult, accum_out=acc), *after))
        m = self.rstd(ss, rs, D, ms)
        return [self.dve(lambda e, i=src(t), o=dst(t), r=rs[:, t:t + 1]: e.tensor_scalar(o, i, r, None, ALU.mult), m, *after)
                for t in range(tiles)]

    def transpose_in(self, src, ready, nk, tiles, dst, banks, scale=None, bias=None, tmp=None, toks=None):
        ident = self.ident
        width = tiles * P
        per = NB // width
        marks = []
        for j in range(0, nk, per):
            b = banks[(j // per) % len(banks)]
            ks = list(range(j, min(j + per, nk)))
            for k in ks:
                for t in range(tiles):
                    o = b.ap[:, (k - j) * width + t * P:(k - j) * width + (t + 1) * P]
                    m = self.pe(lambda e, o=o, i=src(t, k): e.transpose(o, i, ident), ready, b.free, self.const_ready,
                                mark=(k == ks[-1] and t == tiles - 1))
            hs, ls = [], []
            if scale is None:
                o = b.ap[:, 0:len(ks) * width]
                hi, lo = dst.hi_span(j, len(ks)), dst.lo_span(j, len(ks))
                h = self.act(lambda e, o=o, hi=hi: e.activation(hi, o, ACT.Copy), m)
                l = self.dve(lambda e, o=o, hi=hi, lo=lo: e.tensor_tensor(lo, o, hi.bitcast(F32), ALU.subtract), m, h)
                hs.append(h)
                ls.append(l)
            elif bias is None:
                for k in ks:
                    o = b.ap[:, (k - j) * width:(k - j + 1) * width]
                    hs.append(self.act(lambda e, o=o, k=k: e.activation(dst.hi_span(k, 1), o, ACT.Copy, scale=scale(k)), m, ls))
                for k in ks:
                    o = b.ap[:, (k - j) * width:(k - j + 1) * width]
                    ls.append(self.dve(lambda e, o=o, k=k: e.scalar_tensor_tensor(
                        out=dst.lo_span(k, 1), in0=o, scalar=scale(k), in1=dst.hi_span(k, 1).bitcast(F32),
                        op0=ALU.mult, op1=ALU.subtract), m, hs))
            else:
                for k in ks:
                    o = b.ap[:, (k - j) * width:(k - j + 1) * width]
                    tm = tmp(k)
                    v = self.dve(lambda e, o=o, k=k, tm=tm: e.tensor_scalar(tm, o, scale(k), bias(k), ALU.mult, ALU.add), m)
                    h = self.act(lambda e, k=k, tm=tm: e.activation(dst.hi_span(k, 1), tm, ACT.Copy), v)
                    l = self.dve(lambda e, k=k, tm=tm: e.tensor_tensor(
                        dst.lo_span(k, 1), tm, dst.hi_span(k, 1).bitcast(F32), ALU.subtract), v, h)
                    hs.append(v)
                    ls.append([l, h])
            b.free = [hs[-1], ls[-1]]
            marks.append([hs, ls])
        dst.ready = marks
        return marks

    def split_view(self, at, nk, toks, arena=None):
        r = arena or self.r
        hi, lo = r(at, nk, toks), r(at + nk * toks, nk, toks)
        s = Split(lambda k, t: hi[:, k, t * P:(t + 1) * P], lambda k, t: lo[:, k, t * P:(t + 1) * P])
        s.hi_span = lambda k, n: r(at + k * toks, n * toks)
        s.lo_span = lambda k, n: r(at + nk * toks + k * toks, n * toks)
        return s

    def load(self, dst, src, *after, lane=None):
        return (lane or self.pool).dma(lambda e: e.dma_start(dst, src), self.newline(f"load_{len(self.lines)}"), *after)

    def everyone(self):
        return [m for m in (self.pe.now(), self.dve.now(), self.act.now(), self.pool.now()) if m]

    def checkpoint(self, name, ap, marks):
        if self.upto == name:
            self.store = (ap, marks)
            raise Stop()


def split_dims(v, dims):
    if len(dims) == 1:
        return v
    if len(dims) == 2:
        return v.rearrange("p (a b) -> p a b", a=dims[0])
    return v.rearrange("p (a b c) -> p a b c", a=dims[0], b=dims[1])



def begin(p):
    d = p.dram
    p.ident = p.k(K_IDENT, P)
    p.minus_half = p.k(K_MHALF, 62)
    x = p.f(X_AT, ST, D)
    p.x = x
    p.x_in = p.load(x, d["x"].rearrange("(t q) d -> q t d", q=P), lane=p.sp)
    cols_in = p.load(p.k(K_COLS, N_COLS), d["cols"], lane=p.act)
    ident_in = p.load(p.k(K_IDENT, P), d["ident"], lane=p.act)
    sel_in = p.load(p.k(K_SEL, 130), d["sel"], lane=p.act)
    lam_in = p.load(p.f(T_AT, 4, 64), d["lambda_rows"], lane=p.act)
    dist_in = p.load(p.k(K_DIST, ST, S), d["dist"], lane=p.act)
    slope_in = p.load(p.k(K_SLOPE, HEADS, P), d["slopes"], lane=p.act)
    p.attn_consts = [dist_in, slope_in]
    half = p.dve(lambda e: e.memset(p.minus_half, -0.5))
    p.const_ready = [half, ident_in, cols_in]
    p.col = lambda name, k: p.k(K_COLS + COL0[name] + k, 1)
    p.sel_in = sel_in
    p.feed()

    cs = p.r(11776, KD, P)
    zero = p.dve(lambda e: e.memset(cs.bitcast(F32), 0.0))
    c16 = p.k(K_COLS + COL0["c"], 16)
    sil = p.stat(16)
    a = p.act(lambda e: e.activation(sil, c16, ACT.Silu), cols_in)
    marks = []
    for j in range(2):
        hi, lo, v = cs[:, :, 2 * j], cs[:, :, 2 * j + 1], sil[:, 8 * j:8 * j + 8]
        h = p.dve(lambda e, hi=hi, v=v: e.tensor_copy(hi, v), a, zero)
        marks.append(p.dve(lambda e, hi=hi, lo=lo, v=v: e.tensor_tensor(lo, v, hi.bitcast(F32), ALU.subtract), h))
    p.cs = Split(lambda k, t: cs[:, k, :], None)
    p.cs.ready = marks

    rows = p.f(T_AT, 4, 64)
    prod = p.f(T_AT + 256, 2, 64)
    pair = rows.rearrange("p (a b) c -> p a b c", b=2)
    m = p.dve(lambda e: e.tensor_tensor(prod, pair[:, :, 0, :], pair[:, :, 1, :], ALU.mult), lam_in)
    sums, ex = p.stat(2), p.stat(2)
    m = p.dve(lambda e: e.tensor_reduce(sums, prod, AX.X, ALU.add), m)
    m = p.act(lambda e: e.activation(ex, sums, ACT.Exp), m)
    p.neg_lam = p.k(K_LAM, 1)
    m = p.dve(lambda e: e.tensor_tensor(p.neg_lam, ex[:, 1:2], ex[:, 0:1], ALU.subtract), m)
    p.sub_gain = p.k(K_LAM + 1, 1)
    p.sub_ready = p.dve(lambda e: e.tensor_scalar(p.sub_gain, p.col("g_sub", 0), 1.0 - LAMBDA_INIT, None, ALU.mult), cols_in)
    p.lam_ready = p.dve(lambda e: e.tensor_scalar(p.neg_lam, p.neg_lam, 1.0, -LAMBDA_INIT, ALU.mult, ALU.add), m)
    p.mod_f = p.stat(64).rearrange("p (k two) -> p k two", two=2)
    p.mod_rows = [p.f(Z_AT + 512 * i, NB) for i in range(2)]
    p.mod_n = 0
    p.mod_rows_free = [None, None]


def modulation(p, n, banks, dst=None, gain=None, after=None):
    row = p.mod_rows[p.mod_n % 2]
    prior = p.mod_rows_free[p.mod_n % 2]
    b_in = p.load(row[4:5, :], p.dram["b_mod"][n:n + 1, :], prior, lane=p.pool)
    acc, out = banks
    started = False
    for i in range(4):
        pc = p.take("w_mod", n)
        for k, c, at, w in pc.blocks:
            a = p.cs.hi(k, 0)
            p.pe(lambda e, a=a, b=pc.hi[:, at:at + w], s=(k == 0): e.matmul(acc.ap, a, b, start=s, stop=False),
                 pc.split, p.cs.ready, acc.free, mark=False)
            last = (k, c, at, w) == pc.blocks[-1]
            m = p.pe(lambda e, a=a, b=pc.lo[:, at:at + w], z=(k == KD - 1): e.matmul(acc.ap, a, b, start=False, stop=z),
                     mark=last)
        pc.used = m
        p.next_piece += 1
        if i < 3:
            p.feed()
            yield
    ev = p.act(lambda e: e.activation(row[0:4, :], acc.ap[0:4, :], ACT.Copy), m, prior)
    acc.free = ev
    if n < 4:
        sel2 = p.k(K_SEL + 128, 2)
        for j in range(4):
            m = p.pe(lambda e, j=j: e.matmul(out.ap[:, 2 * j:2 * j + 2], row[0:5, j * P:(j + 1) * P], sel2[0:5, :],
                                             start=True, stop=True), ev, b_in, p.sel_in, out.free, mark=j == 3)
        f = p.mod_f[:, 4 * n:4 * n + 4, :]
        o = out.ap[:, 0:8].rearrange("p (k two) -> p k two", two=2)
        r = p.mod_f_ready = p.dve(lambda e: e.tensor_copy(f, o), m)
    else:
        selb = p.k(K_SEL, P)
        m = p.pe(lambda e: e.matmul(out.ap, selb[0:5, :], row[0:5, :], start=True, stop=True),
                 ev, b_in, p.sel_in, out.free)
        if gain is None:
            r = p.act(lambda e: e.activation(dst, out.ap, ACT.Copy), m, after)
        else:
            r = p.dve(lambda e: e.scalar_tensor_tensor(out=dst, in0=out.ap, scalar=1.0, in1=gain,
                                                       op0=ALU.add, op1=ALU.mult), m, after)
    out.free = r
    p.mod_rows_free[p.mod_n % 2] = m
    p.mod_n += 1
    p.mod_ready = r
    yield


def segment_stats(p, bank, m, z, sq, ss, segs, seglen):
    n = segs * seglen
    a = p.act(lambda e: e.activation(z, bank.ap[:, 0:n], ACT.Copy), m)
    b = p.act(lambda e: e.activation(sq[0], bank.ap[:, 0:n], ACT.Square), m, sq[1])
    bank.free = b
    r = p.dve(lambda e: e.tensor_reduce(ss, sq[0].rearrange("p (s c) -> p s c", s=segs), AX.X, ALU.add), b)
    return a, r


def block_one(p):
    B = p.banks
    F = p.f
    xn = F(B_AT, ST, D)
    nrm = p.row_norm(lambda t: p.x[:, t, :], ST, lambda t: xn[:, t, :], lambda t: F(C_AT + t * D, D), p.x_in)
    for n in range(2):
        p.run(modulation(p, n, [B[n], B[6]]))
    hT = p.split_view(0, KD, S)
    p.transpose_in(lambda t, k: xn[:, t, k * P:(k + 1) * P], nrm, KD, ST, hT, [B[4], B[5], B[7]],
                   scale=lambda k: p.col("g_mix", k))
    for n in range(2, 4):
        p.run(modulation(p, n, [B[n - 2], B[6]]))
    p.checkpoint("hT", p.R[:, 0:2048].bitcast(F32), p.everyone())

    pool_m = F(G_AT + 2048, 4, ST, S)
    grp_w = F(E_AT, 4, P)
    pm_in = p.load(pool_m, p.dram["pool_m"], lane=p.act)
    gw_in = p.load(grp_w, p.dram["w_grp"], lane=p.act)

    def project(n, bs):
        return p.run(p.gemm("w_in", n, KD, hT, (0, 1), lambda t, c: bs[t].ap, bs))

    U = F(G_AT, ST, NB)
    m = project(0, B[0:2])
    for t in range(ST):
        B[t].free = ev = p.act(lambda e, t=t: e.activation(U[:, t, :], B[t].ap, ACT.Copy), m)
    u_ready = ev

    sqs = [[F(T_AT + 512 * i, NB), None] for i in range(2)]
    ss_q, ss_k, rs_q, rs_k = (p.stat(32) for _ in range(4))
    zq, zk = F(B_AT, ST, D), F(C_AT, ST, D)
    qT, kT = F(D_AT, HEADS, S), None
    norm_marks = {}
    turn = 0
    for what, z, ss, rs, chunks in (("q", zq, ss_q, rs_q, (1, 2)), ("k", zk, ss_k, rs_k, (3, 4))):
        marks = []
        for i, n in enumerate(chunks):
            turn += 1
            bs = B[2 * (turn % 2):2 * (turn % 2) + 2]
            m = project(n, bs)
            for t in range(ST):
                s = ss[:, t * 16 + i * 8:t * 16 + i * 8 + 8]
                zz = z[:, t, i * NB:(i + 1) * NB]
                a, r = segment_stats(p, bs[t], m, zz, sqs[t], s, 8, 64)
                sqs[t][1] = r
                marks += [a, r]
            if what == "q" and i == 0:
                pool_mix(p, U, u_ready, pool_m, grp_w, [pm_in, gw_in])
        rm = p.rstd(ss, rs, 64, marks)
        for t in range(ST):
            zt = z[:, t, :].rearrange("p (s c) -> p s c", s=16)
            rb = rs[:, t * 16:t * 16 + 16].unsqueeze(2).to_broadcast([P, 16, 64])
            norm_marks[what, t] = p.dve(lambda e, zt=zt, rb=rb: e.tensor_tensor(zt, zt, rb, ALU.mult), rm, marks)
    qT, kT = F(D_AT, HEADS, S), F(E_AT, HEADS, S)
    v = F(B_AT, ST, D)

    def heads_in(z, marks, dst, g, extra, after=None):
        out = []
        for j in range(0, HEADS, 2):
            b = B[4 + (j // 2) % 4]
            for h in (j, j + 1):
                for t in range(ST):
                    o = b.ap[:, (h - j) * S + t * P:(h - j) * S + (t + 1) * P]
                    m = p.pe(lambda e, o=o, i=z[:, t, h * P:(h + 1) * P]: e.transpose(o, i, p.ident),
                             marks, b.free, mark=(h == j + 1 and t == 1))
            d = dst[:, j:j + 2, :].rearrange("p a b -> p (a b)")
            b.free = r = p.dve(lambda e, d=d, b=b: e.tensor_scalar(d, b.ap, p.col(g, 0), extra, ALU.mult, ALU.mult), m, after)
            out.append(r)
        return out

    mq = heads_in(zq, [norm_marks["q", 0], norm_marks["q", 1]], qT, "g_q", 64 ** -0.5)
    q_moved = p.pe.now()
    mv = []
    m = project(5, B[0:2])
    for t in range(ST):
        B[t].free = r = p.act(lambda e, t=t: e.activation(v[:, t, 0:NB], B[t].ap, ACT.Copy), m, q_moved)
        mv.append(r)
    mk = heads_in(zk, [norm_marks["k", 0], norm_marks["k", 1]], kT, "g_k", 1.0, p.pool_mixed)
    k_moved = p.pe.now()
    m = project(6, B[2:4])
    for t in range(ST):
        B[2 + t].free = r = p.act(lambda e, t=t: e.activation(v[:, t, NB:D], B[2 + t].ap, ACT.Copy), m)
        mv.append(r)
    p.checkpoint("qT", p.f(D_AT, 2048), [p.everyone()])

    gz = F(G_AT, ST, 2048)
    gate_bias = [F(Z_AT + NB * i, NB) for i in range(2)]
    bias_line = [p.newline(f"gate_bias_{i}") for i in range(2)]
    bias_used = [list(p.mod_rows_free)] * 2

    def gates():
        for n in range(4):
            bs = B[2 * (n % 2):2 * (n % 2) + 2]
            gb = gate_bias[n % 2]
            gb_in = p.pool.dma(lambda e, gb=gb, n=n: e.dma_start(gb, p.dram["b_gate"][:, n * NB:(n + 1) * NB]),
                               bias_line[n % 2], bias_used[n % 2])
            yield from p.gemm("w_gate", n, KD, hT, (0, 1), lambda t, c: bs[t].ap, bs)
            for t in range(ST):
                bs[t].free = r = p.dve(lambda e, t=t, bs=bs, n=n, gb=gb: e.tensor_tensor(
                    gz[:, t, n * NB:(n + 1) * NB], bs[t].ap, gb, ALU.add),
                    p.last_gemm, gb_in, p.pool_mixed)
                p.gz_ready.append(r)
            bias_used[n % 2] = r

    p.gz_ready = []
    background = gates()
    attn_out = diff_attention(p, qT, kT, v, [mq, mk, mv, p.attn_consts, p.lam_ready], background, k_moved)
    yaT = attn_out
    p.attention_done = p.everyone()

    sig = []
    for t in range(ST):
        for c in range(2):
            g = gz[:, t, c * D:(c + 1) * D]
            sig.append(p.act(lambda e, g=g: e.activation(g, g, ACT.Sigmoid), p.gz_ready))
    m = p.run(p.gemm("w_bp", 0, 4, p.ypT, (0, 1), lambda t, c: B[2 * t + c].ap, B[0:4]))
    merged = F(B_AT, ST, D)
    part = F(C_AT, ST, D)
    mm = []
    for t in range(ST):
        for c in range(2):
            B[2 * t + c].free = r = p.dve(lambda e, t=t, c=c: e.tensor_tensor(
                merged[:, t, c * NB:(c + 1) * NB], B[2 * t + c].ap, gz[:, t, c * NB:(c + 1) * NB], ALU.mult), m, sig)
            mm.append(r)
    for n in range(2):
        m = p.run(p.gemm("w_ba", n, 4, yaT, (0, 1), lambda t, c: B[4 + 2 * t + c].ap, B[4:8] if n == 0 else [],
                         k0=4 * n, first=(n == 0), last=(n == 1)))
    ready = []
    for c in range(2):
        for t in range(ST):
            pt = part[:, t, c * NB:(c + 1) * NB]
            mg = merged[:, t, c * NB:(c + 1) * NB]
            B[4 + 2 * t + c].free = r = p.dve(lambda e, t=t, c=c, pt=pt: e.tensor_tensor(
                pt, B[4 + 2 * t + c].ap, gz[:, t, D + c * NB:D + (c + 1) * NB], ALU.mult), m, sig, mm)
            ready.append(p.dve(lambda e, pt=pt, mg=mg: e.tensor_tensor(mg, mg, pt, ALU.add), r))
    p.na_bias_free = ready
    mT = p.split_view(0, KD, S)
    p.transpose_in(lambda t, k: merged[:, t, k * P:(k + 1) * P], ready, KD, ST, mT, B[0:4])
    xs = []
    for n in range(2):
        bs = B[4 + 2 * n:6 + 2 * n]
        m = p.run(p.gemm("w_out", n, KD, mT, (0, 1), lambda t, c: bs[t].ap, bs))
        for t in range(ST):
            xx = p.x[:, t, n * NB:(n + 1) * NB]
            bs[t].free = r = p.dve(lambda e, xx=xx, b=bs[t]: e.tensor_tensor(xx, b.ap, xx, ALU.add), m)
            xs.append(r)
    p.checkpoint("x1", p.f(X_AT, 2048), [p.everyone()])

    xn = F(C_AT, ST, D)
    nrm = p.row_norm(lambda t: p.x[:, t, :], ST, lambda t: xn[:, t, :], lambda t: F(B_AT + t * D, D), xs, p.pe.now())
    h2 = p.split_view(0, KD, S)
    p.transpose_in(lambda t, k: xn[:, t, k * P:(k + 1) * P], nrm, KD, ST, h2, B[0:4], scale=lambda k: p.col("g_ffn", k))
    hid = [F(D_AT + 1024 * i, ST, NB) for i in range(2)]
    hidT = [p.split_view(4096 + 2048 * i, 4, S) for i in range(2)]
    state = {"made": [None] * 2, "hid_free": [None] * 2}

    def up(n):
        bs = B[4:6]
        m = p.run(p.gemm("w_up", n, KD, h2, (0, 1), lambda t, c: bs[t].ap, bs))
        h, out = hid[n % 2], []
        for t in range(ST):
            bs[t].free = a = p.act(lambda e, t=t, h=h: e.activation(h[:, t, :], bs[t].ap, ACT.Relu), m, state["hid_free"][n % 2])
            out.append(p.dve(lambda e, t=t, h=h: e.tensor_tensor(h[:, t, :], h[:, t, :], h[:, t, :], ALU.mult), a))
        state["made"][n % 2] = out

    def turn_in(n):
        h = hid[n % 2]
        ht = hidT[n % 2]
        p.transpose_in(lambda t, k: h[:, t, k * P:(k + 1) * P], state["made"][n % 2], 4, ST, ht, B[6:8])
        state["hid_free"][n % 2] = p.pe.now()

    up(0)
    up(1)
    over = p.attention_done
    p.late_consts = [p.load(p.k(K_TRI, ST, S), p.dram["tri"], over), p.load(p.k(K_IOTA, P), p.dram["iota"], over),
                     p.load(p.k(K_ROPE, ST, 2, 16), p.dram["rope"], over),
                     p.load(p.k(K_COLMASK, GRID_W), p.dram["col_mask"], over)]
    xc = F(E_AT, ST, D)
    c_in = p.load(xc, p.dram["ctx"].rearrange("(t q) d -> q t d", q=P), over)
    p.ctx_normed = p.row_norm(lambda t: xc[:, t, :], ST, lambda t: xc[:, t, :], lambda t: F(G_AT + t * D, D), c_in, ready)
    for n in range(8):
        turn_in(n)
        m = p.run(p.gemm("w_down", n, 4, hidT[n % 2], (0, 1), lambda t, c: B[2 * t + c].ap,
                         B[0:4] if n == 0 else [], first=(n == 0), last=(n == 7)))
        if n + 2 < 8:
            up(n + 2)
    xs = []
    for t in range(ST):
        for c in range(2):
            xx = p.x[:, t, c * NB:(c + 1) * NB]
            B[2 * t + c].free = r = p.dve(lambda e, xx=xx, b=B[2 * t + c]: e.tensor_tensor(xx, b.ap, xx, ALU.add), m)
            xs.append(r)
    p.x_ready = xs
    p.checkpoint("x2", p.f(X_AT, 2048), [p.everyone()])


def pool_mix(p, U, ready, pool_m, grp_w, ins):
    B = p.banks
    mix = p.f(E_AT + 512, 4, S)
    marks = []
    for g in range(4):
        b = B[4 + g // 2]
        for kt in range(ST):
            m = p.pe(lambda e, g=g, kt=kt, b=b: e.matmul(
                b.ap[:, (g % 2) * S:(g % 2 + 1) * S], U[:, kt, g * P:(g + 1) * P], pool_m[:, g, kt, :],
                start=kt == 0, stop=kt == 1), ready, ins, b.free, mark=(kt == 1 and g % 2 == 1))
        if g % 2 == 1:
            d = mix[:, g - 1:g + 1, :].rearrange("p a b -> p (a b)")
            b.free = r = p.dve(lambda e, d=d, b=b: e.tensor_copy(d, b.ap), m)
            marks.append(r)
    yp = p.split_view(8192, 4, S)
    out = []
    for g in range(4):
        b = B[6 + g // 2]
        o = b.ap[:, (g % 2) * S:(g % 2 + 1) * S]
        m = p.pe(lambda e, g=g, o=o: e.matmul(o, grp_w[:, g, :], mix[:, g, :], start=True, stop=True),
                 marks, ins, b.free, mark=g % 2 == 1)
        if g % 2 == 1:
            hs = []
            for q in (g - 1, g):
                oo = b.ap[:, (q % 2) * S:(q % 2 + 1) * S]
                hs.append(p.act(lambda e, q=q, oo=oo: e.activation(yp.hi_span(q, 1), oo, ACT.Copy, scale=p.col("pool_scale", q)), m))
            for q in (g - 1, g):
                oo = b.ap[:, (q % 2) * S:(q % 2 + 1) * S]
                r = p.dve(lambda e, q=q, oo=oo: e.scalar_tensor_tensor(
                    out=yp.lo_span(q, 1), in0=oo, scalar=p.col("pool_scale", q), in1=yp.hi_span(q, 1).bitcast(F32),
                    op0=ALU.mult, op1=ALU.subtract), m, hs)
            b.free = r
            out += [hs, r]
    yp.ready = out
    p.ypT = yp
    p.pool_mixed = [p.pe.now(), out]


def diff_attention(p, qT, kT, v, ready, background, k_moved):
    B = p.banks
    dist = p.k(K_DIST, ST, S)
    slopes = p.k(K_SLOPE, HEADS, P)
    prob = [p.f(T_AT + 512 * i, 2, S) for i in range(3)]
    prob_free = [None] * 3
    aT = [p.f(T_AT + 1536 + 256 * i, ST, P) for i in range(2)]
    aT_free = [None] * 2
    Oh = p.f(M_AT, 2, NB)
    units = [(t, h) for t in range(ST) for h in range(HEADS)]
    st = {}
    neg_max, sums, inv = p.stat(32), p.stat(32), p.stat(32)
    ssq, rs = p.stat(16), p.stat(16)

    def scores(u):
        t, h = units[u]
        nk = (t + 1) * P
        for i in range(2):
            o = B[4 + i].ap[:, 0:nk]
            p.pe(lambda e, o=o, i=i: e.matmul(o, qT[64 * i:64 * i + 64, h, t * P:(t + 1) * P], kT[64 * i:64 * i + 64, h, 0:nk],
                                              start=True, stop=False), ready, B[4].free, B[5].free, mark=False)
            m = p.pe(lambda e, o=o: e.matmul(o, slopes[:, h, :], dist[:, t, 0:nk], start=False, stop=True), mark=i == 1)
        nm, rs_, iv = (s[:, 2 * u:2 * u + 2] for s in (neg_max, sums, inv))
        both = p.ps[:, 4:6, 0:nk]
        r = p.dve(lambda e: e.tensor_reduce(nm, both, AX.X, ALU.max, negate=True), m)
        w = prob[u % 3]
        ex = []
        for i in range(2):
            ex.append(p.act(lambda e, i=i: e.activation(w[:, i, 0:nk], B[4 + i].ap[:, 0:nk], ACT.Exp, bias=nm[:, i:i + 1],
                                                        accum_out=rs_[:, i:i + 1]), r, prob_free[u % 3]))
        B[4].free = B[5].free = ex
        m = p.dve(lambda e: e.reciprocal(iv, rs_), ex)
        m = p.dve(lambda e: e.tensor_tensor(iv[:, 1:2], iv[:, 1:2], p.neg_lam, ALU.mult), m)
        m2 = p.dve(lambda e: e.tensor_scalar(w[:, 0, 0:nk], w[:, 0, 0:nk], iv[:, 0:1], None, ALU.mult), m, ex)
        st[u] = p.dve(lambda e: e.scalar_tensor_tensor(out=w[:, 0, 0:nk], in0=w[:, 1, 0:nk], scalar=iv[:, 1:2],
                                                       in1=w[:, 0, 0:nk], op0=ALU.mult, op1=ALU.add), m, m2)

    def weigh(u):
        t, h = units[u]
        w, a, b = prob[u % 3], aT[u % 2], B[6]
        for kt in range(t + 1):
            m = p.pe(lambda e, kt=kt: e.transpose(b.ap[:, kt * P:(kt + 1) * P], w[:, 0, kt * P:(kt + 1) * P], p.ident),
                     st[u], b.free, mark=kt == t)
        prob_free[u % 3] = m
        b.free = ev = p.act(lambda e: e.activation(a[:, 0:t + 1, :].rearrange("p a b -> p (a b)"), b.ap[:, 0:(t + 1) * P], ACT.Copy),
                            m, aT_free[u % 2])
        ob = B[7]
        for kt in range(t + 1):
            m = p.pe(lambda e, kt=kt: e.matmul(ob.ap[:, (h % 4) * P:(h % 4 + 1) * P], a[:, kt, :], v[:, kt, h * P:(h + 1) * P],
                                               start=kt == 0, stop=kt == t), ev, ob.free, mark=kt == t)
        aT_free[u % 2] = m
        if h % 4 == 3:
            q = t * 2 + h // 4
            s = ssq[:, 4 * q:4 * q + 4]
            z = p.o_all[:, t, (h // 4) * NB:(h // 4 + 1) * NB]
            a2 = p.act(lambda e: e.activation(z, ob.ap, ACT.Copy), m, p.o_free)
            sq = Oh[:, q % 2, :]
            b2 = p.act(lambda e: e.activation(sq, ob.ap, ACT.Square), m, st.get(("sq", q - 2)))
            ob.free = b2
            r = p.dve(lambda e: e.tensor_reduce(s, sq.rearrange("p (s c) -> p s c", s=4), AX.X, ALU.add), b2)
            st["sq", q] = r
            rm = p.rstd(s, rs[:, 4 * q:4 * q + 4], P, r)
            zz = z.rearrange("p (s c) -> p s c", s=4)
            rb = rs[:, 4 * q:4 * q + 4].unsqueeze(2).to_broadcast([P, 4, P])
            st["o", q] = p.dve(lambda e: e.tensor_tensor(zz, zz, rb, ALU.mult), rm, a2)

    p.o_all = p.f(C_AT, ST, D)
    p.o_free = k_moved
    for u in range(len(units) + 2):
        if u < len(units):
            scores(u)
        next(background, None)
        if u >= 2:
            weigh(u - 2)
    for _ in background:
        pass
    yaT = p.split_view(4096, KD, S)
    p.transpose_in(lambda t, k: p.o_all[:, t, k * P:(k + 1) * P], [[st["o", q] for q in range(4)], p.sub_ready], KD, ST, yaT,
                   [B[4], B[5], B[6]], scale=lambda k: p.sub_gain)
    return yaT


def block_two(p):
    B, F, K = p.banks, p.f, p.k
    x = p.x
    def coefficients(which):
        scale, shift = p.stat(8), p.mod_f[:, 0:8, which]
        m = p.dve(lambda e, s=scale, i=p.mod_f[:, 8:16, which], g=K(K_COLS + COL0["norm_attn_g"], 8):
                  e.scalar_tensor_tensor(out=s, in0=i, scalar=1.0, in1=g, op0=ALU.add, op1=ALU.mult), p.mod_f_ready)
        return scale, shift, m

    ax, bx, m_x = coefficients(0)
    ac, bc, m_c = coefficients(1)
    tmp = lambda k: F(T_AT + S * (k % 4), S)
    xn_c = F(E_AT, ST, D)
    hcT = p.split_view(4096, KD, S)
    xn = F(B_AT, ST, D)
    nrm = p.row_norm(lambda t: x[:, t, :], ST, lambda t: xn[:, t, :], lambda t: F(G_AT + 2048 + t * D, D), p.x_ready)
    p.transpose_in(lambda t, k: xn_c[:, t, k * P:(k + 1) * P], [p.ctx_normed, m_c], KD, ST, hcT, B[4:8],
                   scale=lambda k: ac[:, k:k + 1], bias=lambda k: bc[:, k:k + 1], tmp=tmp)
    hxT = p.split_view(0, KD, S)
    p.transpose_in(lambda t, k: xn[:, t, k * P:(k + 1) * P], [nrm, m_x], KD, ST, hxT, B[4:8],
                   scale=lambda k: ax[:, k:k + 1], bias=lambda k: bx[:, k:k + 1], tmp=tmp)
    both = Split(lambda k, t: hxT.hi(k, t) if t < ST else hcT.hi(k, t - ST),
                 lambda k, t: hxT.lo(k, t) if t < ST else hcT.lo(k, t - ST))
    both.ready = [hxT.ready, hcT.ready]

    ALL = tuple(range(TT))
    kvl = F(C_AT, TT, KV_LORA + ROPE)
    m = p.run(p.gemm("w_in2kv", 0, KD, both, ALL, lambda t, c: B[t].ap[:, 0:KV_LORA + ROPE], B[0:4]))
    ss_kv, rs_kv = p.stat(TT), p.stat(TT)
    moved, sq = [], []
    for t in ALL:
        a = p.act(lambda e, t=t: e.activation(kvl[:, t, :], B[t].ap[:, 0:KV_LORA + ROPE], ACT.Copy), m)
        B[t].free = b = p.act(lambda e, t=t: e.activation(F(T_AT + 1024 + 256 * (t % 2), KV_LORA), B[t].ap[:, 0:KV_LORA],
                                                          ACT.Square, accum_out=ss_kv[:, t:t + 1]), m, sq[-2:-1])
        moved.append(a)
        sq.append(b)
    rm = p.rstd(ss_kv, rs_kv, KV_LORA, sq)
    kvn = [p.dve(lambda e, t=t: e.tensor_scalar(kvl[:, t, 0:KV_LORA], kvl[:, t, 0:KV_LORA], rs_kv[:, t:t + 1], None, ALU.mult),
                 rm, moved) for t in ALL]

    nk, nkT, nv = F(D_AT, TT, NB), F(E_AT, 4, TT * P), F(G_AT, TT, NB)
    m = p.run(p.gemm("w_in2k", 0, KD, both, ALL, lambda t, c: B[4 + t].ap, B[4:8]))
    nk_in = []
    for t in ALL:
        B[4 + t].free = r = p.act(lambda e, t=t: e.activation(nk[:, t, :], B[4 + t].ap, ACT.Copy), m)
        nk_in.append(r)
    m = p.run(p.gemm("w_in2v", 0, KD, both, ALL, lambda t, c: B[t].ap, B[0:4]))
    nv_in = []
    for t in ALL:
        B[t].free = r = p.act(lambda e, t=t: e.activation(nv[:, t, :], B[t].ap, ACT.Copy), m)
        nv_in.append(r)

    def turn(src, ready, dst, banks, tiles, rows=P):
        b = banks
        for t in range(tiles):
            m = p.pe(lambda e, o=b.ap[0:rows, t * P:(t + 1) * P], i=src(t): e.transpose(o, i, p.ident), ready, b.free,
                     mark=t == tiles - 1)
        b.free = r = p.act(lambda e, o=dst, i=b.ap[0:rows, 0:tiles * P]: e.activation(o, i, ACT.Copy), m)
        return r

    nkT_in = [turn(lambda t, j=j: nk[:, t, j * P:(j + 1) * P], nk_in, nkT[:, j, :], B[4 + j], TT) for j in range(4)]
    kvT = p.split_view(9728, 2, TT * P)
    p.transpose_in(lambda t, k: kvl[:, t, k * P:(k + 1) * P], kvn, 2, TT, kvT, B[4:6], scale=lambda k: p.col("kv_a_g", k))

    zql = F(B_AT, ST, Q_LORA)
    m = p.run(p.gemm("w_in2q", 0, KD, hxT, (0, 1), lambda t, c: B[t].ap[:, 0:Q_LORA], B[0:2]))
    ss_q, rs_q = p.stat(ST), p.stat(ST)
    moved, sq = [], []
    for t in range(ST):
        moved.append(p.act(lambda e, t=t: e.activation(zql[:, t, :], B[t].ap[:, 0:Q_LORA], ACT.Copy), m))
        B[t].free = b = p.act(lambda e, t=t: e.activation(F(T_AT + 1024 + 512 * (t % 2), Q_LORA), B[t].ap[:, 0:Q_LORA],
                                                                 ACT.Square, accum_out=ss_q[:, t:t + 1]), m)
        sq.append(b)
    rm = p.rstd(ss_q, rs_q, Q_LORA, sq)
    qn = [p.dve(lambda e, t=t: e.tensor_scalar(zql[:, t, :], zql[:, t, :], rs_q[:, t:t + 1], None, ALU.mult), rm, moved)
          for t in range(ST)]
    nq, nqT = F(B_AT + 768, ST, NB), F(G_AT + 2048, 4, S)
    m = p.run(p.gemm("w_in2nq", 0, KD, hxT, (0, 1), lambda t, c: B[2 + t].ap, B[2:4]))
    nq_in = []
    for t in range(ST):
        B[2 + t].free = r = p.act(lambda e, t=t: e.activation(nq[:, t, :], B[2 + t].ap, ACT.Copy, scale=64 ** -0.5), m)
        nq_in.append(r)
    nqT_in = [turn(lambda t, j=j: nq[:, t, j * P:(j + 1) * P], nq_in, nqT[:, j, :], B[4 + j], ST) for j in range(4)]
    qlT = p.split_view(8192, 3, S)
    p.transpose_in(lambda t, k: zql[:, t, k * P:(k + 1) * P], qn, 3, ST, qlT, B[0:2], scale=lambda k: p.col("q_a_g", k))

    rope = K(K_ROPE, ST, 2, 16)

    def rotate(z, shape, tables, scratch, ready):
        x1, x2, c, s = z[0], z[1], tables[0], tables[1]
        if shape is not None:
            c, s = (v.unsqueeze(1).to_broadcast(shape) for v in (c, s))
        a, b, c2, d2 = scratch
        ms = [p.dve(lambda e, o=o, i=i, j=j: e.tensor_tensor(o, i, j, ALU.mult), ready, p.late_consts)
              for o, i, j in ((a, x1, c), (b, x2, s), (c2, x1, s), (d2, x2, c))]
        return [p.dve(lambda e: e.tensor_tensor(x1, a, b, ALU.subtract), ms),
                p.dve(lambda e: e.tensor_tensor(x2, c2, d2, ALU.add), ms)]

    kr_ready = []
    for t in range(ST):
        kr = kvl[:, t, KV_LORA:KV_LORA + ROPE]
        sc = [F(T_AT + 64 * t + 16 * i, 16) for i in range(4)]
        kr_ready += rotate((kr[:, 0:16], kr[:, 16:32]), None, (rope[:, t, 0, :], rope[:, t, 1, :]), sc,
                           [moved, p.everyone()] if t == 0 else [])

    mixed = F(B_AT, ST, D)
    bias = [F(G_AT + 3072 + 512 * i, ST, S) for i in range(2)]
    bias_lines = [p.newline(f"window_bias_{i}") for i in range(2)]
    bias_used = [p.na_bias_free, p.na_bias_free]
    col_mask = K(K_COLMASK, GRID_W)
    bias_ready = {}

    def window_bias(h):
        b = bias[h % 2]
        m = p.pool.dma(lambda e, b=b: e.dma_start(b, p.dram["rel_rows"][h]), bias_lines[h % 2], bias_used[h % 2])
        v = b.rearrange("p t (j c) -> p (t j) c", c=GRID_W)
        mask = col_mask.unsqueeze(1).to_broadcast([P, 8, GRID_W])
        bias_ready[h] = p.pool(lambda e, v=v, mask=mask: e.tensor_tensor(v, v, mask, ALU.add), m, p.late_consts)

    def na_scores(h, t, b, after):
        lo = 64 * (h % 2)
        p.pe(lambda e: e.matmul(b.ap, nqT[lo:lo + 64, h // 2, t * P:(t + 1) * P], nkT[lo:lo + 64, h // 2, :],
                                start=True, stop=False), nqT_in, nkT_in, after, mark=False)
        m = p.pe(lambda e: e.matmul(b.ap[:, 0:S], p.ident, bias[h % 2][:, t, :], start=False, stop=True), bias_ready[h])
        if t == ST - 1:
            bias_used[h % 2] = m
            if h + 2 < HEADS:
                window_bias(h + 2)
        return m

    window_bias(0)
    window_bias(1)
    nq_gone = p.pe.now()
    na_done = attend(p, na_scores, 1.0, lambda h, kt: nv[:, kt, h * 64:(h + 1) * 64], nv_in, mixed, 512,
                     iter(()), [nq_gone])

    qm = F(T_AT, ST, HEADS * QK)
    m = p.run(p.gemm("w_uq", 0, 3, qlT, (0, 1), lambda t, c: B[2 * t + c].ap[:, 0:4 * QK], B[0:4]))
    qm_in = []
    for t in range(ST):
        for c in range(2):
            B[2 * t + c].free = r = p.act(lambda e, t=t, c=c: e.activation(
                qm[:, t, c * 4 * QK:(c + 1) * 4 * QK], B[2 * t + c].ap[:, 0:4 * QK], ACT.Copy), m, na_done)
            qm_in.append(r)
    qh = qm.rearrange("p t (h d) -> p t h d", h=HEADS)
    q_ready = []
    for t in range(ST):
        sc = [F(M_AT + 512 * t + 128 * i, HEADS, 16) for i in range(4)]
        q_ready += rotate((qh[:, t, :, NOPE:NOPE + 16], qh[:, t, :, NOPE + 16:QK]), [P, HEADS, 16],
                          (rope[:, t, 0, :], rope[:, t, 1, :]), sc, qm_in)
    vm = F(E_AT, TT, NB)
    kT = F(G_AT, HEADS, TT * P)
    qT = F(D_AT, HEADS, S)
    kt_in, vm_in = [], []
    qT_in = []
    for j in range(0, HEADS, 2):
        b = B[4 + (j // 2) % 2]
        for h in (j, j + 1):
            for t in range(ST):
                m = p.pe(lambda e, o=b.ap[0:QK, (h - j) * S + t * P:(h - j) * S + (t + 1) * P], i=qh[:, t, h, :]:
                         e.transpose(o, i, p.ident), q_ready, b.free, mark=(h == j + 1 and t == 1))
        b.free = r = p.act(lambda e, o=qT[0:QK, j:j + 2, :].rearrange("p a b -> p (a b)"), i=b.ap[0:QK, :]:
                           e.activation(o, i, ACT.Copy), m)
        qT_in.append(r)
    q_gone = p.pe.now()
    kfull = [F(T_AT + 4 * QK * i, 4, QK) for i in range(4)]
    kfree = [None] * 4
    for n in range(2):
        bs = B[0:4]
        m = p.run(p.gemm("w_ukv", n, 2, kvT, ALL, lambda t, c: bs[t].ap, bs))
        for t in ALL:
            src = bs[t].ap.rearrange("p (h d) -> p h d", h=4)
            kd = kfull[t]
            a = p.act(lambda e, o=kd[:, :, 0:NOPE], i=src[:, :, 0:NOPE]: e.activation(o, i, ACT.Copy), m, q_gone, kfree[t])
            vd = vm[:, t, n * 256:(n + 1) * 256].rearrange("p (h d) -> p h d", h=4)
            bs[t].free = r = p.act(lambda e, o=vd, i=src[:, :, NOPE:P]: e.activation(o, i, ACT.Copy), m)
            vm_in.append(r)
            kr = kvl[:, t, KV_LORA:KV_LORA + ROPE].unsqueeze(1).to_broadcast([P, 4, ROPE])
            c = p.dve(lambda e, o=kd[:, :, NOPE:QK], i=kr: e.tensor_copy(o, i), kr_ready, kfree[t], q_gone)
            b = B[4 + t % 2]
            for h in range(4):
                mt = p.pe(lambda e, o=b.ap[0:QK, h * P:(h + 1) * P], i=kd[:, h, :]: e.transpose(o, i, p.ident),
                          a, c, b.free, mark=h == 3)
            kfree[t] = mt
            o = kT[0:QK, 4 * n:4 * n + 4, t * P:(t + 1) * P]
            b.free = r2 = p.dve(lambda e, o=o, i=b.ap[0:QK, :].rearrange("p (h q) -> p h q", h=4): e.tensor_copy(o, i), mt)
            kt_in.append(r2)

    def mla_scores(h, t, b, after):
        return p.pe(lambda e: e.matmul(b.ap, qT[0:QK, h, t * P:(t + 1) * P], kT[0:QK, h, :], start=True, stop=True),
                    qT_in, kt_in, after)

    g1 = F(M_AT, D)
    def g1_chunks():
        for n in (4, 5):
            yield from modulation(p, n, [B[4], B[5]], dst=g1[:, (n - 4) * NB:(n - 3) * NB], after=q_ready)
    bg = g1_chunks()
    mla_done = attend(p, mla_scores, float(QK) ** -0.5, lambda h, kt: vm[:, kt, h * 64:(h + 1) * 64], vm_in, mixed, 0,
                      bg, [kfree])
    for _ in bg:
        pass
    g1_ready = p.mod_ready
    p.checkpoint("mixed", p.f(B_AT, 2048), p.everyone())

    mT = p.split_view(0, KD, S)
    p.transpose_in(lambda t, k: mixed[:, t, k * P:(k + 1) * P], [na_done, mla_done], KD, ST, mT, B[0:4])
    shift2, scale2, gain2, g2 = (F(G_AT + D * i, D) for i in range(4))
    gain_in = p.load(gain2, p.dram["norm_ffn_g"], mla_done, lane=p.pool)
    xs = []
    for n in range(2):
        bs = B[4 + 2 * n:6 + 2 * n]
        m = p.run(p.gemm("w_out2", n, KD, mT, (0, 1), lambda t, c: bs[t].ap, bs))
        for t in range(ST):
            tp = F(T_AT + NB * t, NB)
            xx = x[:, t, n * NB:(n + 1) * NB]
            bs[t].free = r = p.dve(lambda e, b=bs[t], tp=tp, g=g1[:, n * NB:(n + 1) * NB]: e.tensor_tensor(tp, b.ap, g, ALU.mult),
                                   m, g1_ready)
            xs.append(p.dve(lambda e, tp=tp, xx=xx: e.tensor_tensor(xx, xx, tp, ALU.add), r))
    mixT_gone = p.pe.now()
    p.checkpoint("x3", p.f(X_AT, 2048), p.everyone())

    h = F(B_AT, ST, D)
    nrm = p.row_norm(lambda t: x[:, t, :], ST, lambda t: h[:, t, :], lambda t: F(C_AT + t * D, D), xs, mixT_gone)
    for n in (6, 7):
        p.run(modulation(p, n, [B[n - 6], B[2]], dst=shift2[:, (n - 6) * NB:(n - 5) * NB], after=mla_done))
    sh_ready = p.mod_ready
    for n in (8, 9):
        p.run(modulation(p, n, [B[n - 8], B[2]], dst=scale2[:, (n - 8) * NB:(n - 7) * NB],
                         gain=gain2[:, (n - 8) * NB:(n - 7) * NB], after=[mla_done, gain_in]))
    sc_ready = p.mod_ready
    hs = []
    for t in range(ST):
        a = p.dve(lambda e, t=t: e.tensor_tensor(h[:, t, :], h[:, t, :], scale2, ALU.mult), nrm, sc_ready)
        hs.append(p.dve(lambda e, t=t: e.tensor_tensor(h[:, t, :], h[:, t, :], shift2, ALU.add), a, sh_ready))
    p.checkpoint("hx2", p.f(B_AT, 2048), p.everyone())
    for n in (10, 11):
        p.run(modulation(p, n, [B[n - 10], B[2]], dst=g2[:, (n - 10) * NB:(n - 9) * NB], after=mla_done))
    g2_ready = p.mod_ready
    moe(p, h, hs, g2, g2_ready, mixT_gone)
    y, fin = F(T_AT, ST, D), F(D_AT, ST, D)
    gain = F(G_AT, D)
    fg_in = p.load(gain, p.dram["final_g"], hs, lane=p.pool)
    ys = []
    for t in range(ST):
        for c in range(2):
            a = p.dve(lambda e, t=t, c=c, b=p.y_banks[2 * t + c][2]: e.tensor_tensor(
                y[:, t, c * NB:(c + 1) * NB], b.ap, g2[:, c * NB:(c + 1) * NB], ALU.mult), p.y_ready, g2_ready)
        ys.append(p.dve(lambda e, t=t: e.tensor_tensor(y[:, t, :], y[:, t, :], x[:, t, :], ALU.add), a))
    nrm = p.row_norm(lambda t: y[:, t, :], ST, lambda t: fin[:, t, :], lambda t: F(G_AT + (1 + t) * D, D), ys, p.everyone())
    outs = [p.dve(lambda e, t=t: e.tensor_tensor(fin[:, t, :], fin[:, t, :], gain, ALU.mult), nrm, fg_in) for t in range(ST)]
    dst = p.nc.dram_tensor("out", [S, D], F32, kind="ExternalOutput").ap().rearrange("(t q) d -> q t d", q=P)
    for t in range(ST):
        p.load(dst[:, t, :], fin[:, t, :], outs[t], lane=p.sp if t else p.act)
    p.sp.ops.append((p.sp.needed([(l.sem, l.count) for l in p.lines if l.count]), lambda e: e.nop(), None, 0))


def attend(p, scores, scale, values, v_ready, out, col0, background, free):
    B = p.banks
    prob = [p.f(T_AT + 512 * i, NB) for i in range(2)]
    probT = [p.f(T_AT + 1024 + 512 * i, TT, P) for i in range(2)]
    units = [(h, t) for h in range(HEADS) for t in range(ST)]
    peak, neg, sums, inv = p.stat(16), p.stat(16), p.stat(16), p.stat(16)
    prob_free, probT_free, made = [free, free], [free, free], {}
    turned = {}
    acc = B[6:8]

    def first(u):
        h, t = units[u]
        b = B[u % 2]
        at = t * HEADS + h
        m = scores(h, t, b, b.free)
        pk, ng, sm = peak[:, at:at + 1], neg[:, at:at + 1], sums[:, at:at + 1]
        m = p.dve(lambda e: e.tensor_reduce(pk, b.ap, AX.X, ALU.max), m)
        m = p.dve(lambda e: e.tensor_scalar(ng, pk, -scale, None, ALU.mult), m)
        b.free = made[u] = p.act(lambda e, w=prob[u % 2]: e.activation(w, b.ap, ACT.Exp, bias=ng, scale=scale, accum_out=sm),
                                 m, prob_free[u % 2])

    def second(u):
        b, w = B[2 + u % 2], prob[u % 2]
        for kt in range(TT):
            m = p.pe(lambda e, kt=kt: e.transpose(b.ap[:, kt * P:(kt + 1) * P], w[:, kt * P:(kt + 1) * P], p.ident),
                     made[u], b.free, mark=kt == TT - 1)
        prob_free[u % 2] = m
        dst = probT[u % 2].rearrange("p a b -> p (a b)")
        if u % 4 < 3:
            r = p.act(lambda e: e.activation(dst, b.ap, ACT.Copy), m, probT_free[u % 2])
        else:
            r = p.dve(lambda e: e.tensor_copy(dst, b.ap), m, probT_free[u % 2])
        b.free = turned[u] = r

    def third(u):
        h, t = units[u]
        w = probT[u % 2]
        for kt in range(TT):
            m = p.pe(lambda e, kt=kt: e.matmul(acc[t].ap[:, h * 64:(h + 1) * 64], w[:, kt, :], values(h, kt),
                                               start=kt == 0, stop=kt == TT - 1),
                     turned[u], v_ready, acc[t].free, mark=kt == TT - 1)
        probT_free[u % 2] = m
        return m

    for u in range(len(units) + 2):
        if u < len(units):
            first(u)
        next(background, None)
        if 1 <= u <= len(units):
            second(u - 1)
        if u >= 2:
            m = third(u - 2)
    done = []
    r = p.dve(lambda e: e.reciprocal(inv, sums), made[len(units) - 1])
    for t in range(ST):
        o = out[:, t, col0:col0 + NB].rearrange("p (h d) -> p h d", h=HEADS)
        iv = inv[:, t * HEADS:(t + 1) * HEADS].unsqueeze(2).to_broadcast([P, HEADS, 64])
        acc[t].free = r2 = p.dve(lambda e, o=o, iv=iv, i=acc[t].ap.rearrange("p (h d) -> p h d", h=HEADS):
                                 e.tensor_tensor(o, i, iv, ALU.mult), m, r)
        done.append(r2)
    return done


def moe(p, h, h_ready, g2, g2_ready, gone):
    B, F, K = p.banks, p.f, p.k
    H_hi, H_lo = p.r(0, ST, D), p.r(2048, ST, D)
    Hm = []
    for t in range(ST):
        a = p.act(lambda e, t=t: e.activation(H_hi[:, t, :], h[:, t, :], ACT.Copy), h_ready, gone)
        Hm.append(p.dve(lambda e, t=t: e.tensor_tensor(H_lo[:, t, :], h[:, t, :], H_hi[:, t, :].bitcast(F32), ALU.subtract),
                        h_ready, a))
    hT = p.split_view(4096, KD, S)
    p.transpose_in(lambda t, k: h[:, t, k * P:(k + 1) * P], h_ready, KD, ST, hT, B[4:8])
    wr = F(E_AT, KD, 20)
    wr_hi, wr_lo = p.r(12288, KD, 20), p.r(12448, KD, 20)
    wr_in = p.load(wr, p.dram["w_router"], p.attention_done, lane=p.pool)
    br = F(E_AT + 160, 20)
    br_in = p.load(br, p.dram["b_router"], p.attention_done, lane=p.pool)
    a = p.dve(lambda e: e.tensor_copy(wr_hi, wr), wr_in)
    wm = p.dve(lambda e: e.tensor_tensor(wr_lo, wr, wr_hi.bitcast(F32), ALU.subtract), a)
    lg = F(E_AT + 192, ST, 20)
    b = B[3]
    lm = []
    for t in range(ST):
        o = b.ap[:, t * 32:t * 32 + 20]
        for k in range(KD):
            for i, (l, r) in enumerate(((hT.hi(k, t), wr_hi[:, k, :]), (hT.hi(k, t), wr_lo[:, k, :]), (hT.lo(k, t), wr_hi[:, k, :]))):
                m = p.pe(lambda e, o=o, l=l, r=r, s=(k == 0 and i == 0), z=(k == KD - 1 and i == 2):
                         e.matmul(o, l, r, start=s, stop=z), hT.ready, wm, b.free, mark=(t == ST - 1 and k == KD - 1 and i == 2))
    bb = br.unsqueeze(1).to_broadcast([P, ST, 20])
    b.free = m = p.dve(lambda e: e.tensor_tensor(lg, b.ap[:, 0:64].rearrange("p (t c) -> p t c", t=ST)[:, :, 0:20], bb, ALU.add), m, br_in)
    router_gone = p.pe.now()

    at = [E_AT + 256]

    def small(*dims):
        v = F(at[0], *dims)
        at[0] += int(np.prod(dims))
        return v

    def d(fn, *after):
        return p.dve(fn, *after)

    wide = lambda v: v.unsqueeze(2).to_broadcast([P, ST, 4])

    def peak_of(v, m):
        top, eq, cum, first = small(ST), small(ST, 4), small(ST, 5), small(ST, 4)
        m1 = d(lambda e: e.tensor_reduce(top, v, AX.X, ALU.max), m)
        z = d(lambda e: e.memset(cum, 0.0))
        m2 = d(lambda e: e.tensor_tensor(eq, v, wide(top), ALU.is_equal), m1)
        for i in range(4):
            m2 = d(lambda e, i=i: e.tensor_tensor(cum[:, :, i + 1], cum[:, :, i], eq[:, :, i], ALU.max), m2, z)
        return top, first, d(lambda e: e.tensor_tensor(first, cum[:, :, 1:5], cum[:, :, 0:4], ALU.subtract), m2)

    gl = lg[:, :, 0:4]
    gtop, gsel, m1 = peak_of(gl, m)
    diff, ex, gs, gw = small(ST, 4), small(ST, 4), small(ST), small(ST)
    m2 = d(lambda e: e.tensor_tensor(diff, gl, wide(gtop), ALU.subtract), m1)
    m2 = p.act(lambda e: e.activation(ex, diff, ACT.Exp), m2)
    m2 = d(lambda e: e.tensor_reduce(gs, ex, AX.X, ALU.add), m2)
    m2 = d(lambda e: e.reciprocal(gw, gs), m2)
    el = lg[:, :, 4:20].rearrange("p t (g e) -> p t g e", g=4)
    prod, es = small(ST, 4, 4), small(ST, 4)
    gb = gsel.unsqueeze(3).to_broadcast([P, ST, 4, 4])
    m3 = d(lambda e: e.tensor_tensor(prod, el, gb, ALU.mult), m1)
    m3 = d(lambda e: e.tensor_reduce(es, prod.rearrange("p t g e -> p t e g"), AX.X, ALU.add), m3)
    etop, _, m3 = peak_of(es, m3)
    ediff, ee = small(ST, 4), small(ST, 4)
    m3 = d(lambda e: e.tensor_tensor(ediff, es, wide(etop), ALU.subtract), m3)
    m3 = p.act(lambda e: e.activation(ee, ediff, ACT.Exp), m3)
    p1, f1, m4 = peak_of(ee, m3)
    rest = small(ST, 4)
    m4 = d(lambda e: e.scalar_tensor_tensor(out=rest, in0=f1, scalar=-2.0, in1=ee, op0=ALU.mult, op1=ALU.add), m4)
    p2, f2, m5 = peak_of(rest, m4)
    tot, inv, wgt, wi, sel2 = small(ST), small(ST), small(ST), small(ST, 4), small(ST, 4)
    m6 = d(lambda e: e.tensor_tensor(tot, p1, p2, ALU.add), m5)
    m6 = d(lambda e: e.reciprocal(inv, tot), m6)
    m6 = d(lambda e: e.tensor_tensor(wgt, inv, gw, ALU.mult), m6, m2)
    m7 = d(lambda e: e.tensor_tensor(wi, f2, wide(p2), ALU.mult), m5)
    a1 = small(ST, 4)
    m7b = d(lambda e: e.tensor_tensor(a1, f1, wide(p1), ALU.mult), m5)
    m7 = d(lambda e: e.tensor_tensor(wi, wi, a1, ALU.add), m7, m7b)
    m7 = d(lambda e: e.tensor_tensor(wi, wi, wide(wgt), ALU.mult), m7, m6)
    m8 = d(lambda e: e.tensor_tensor(sel2, f1, f2, ALU.add), m5)
    comb, chosen = small(ST, N_EXPERTS), small(ST, N_EXPERTS)
    c4, s4 = (v.rearrange("p t (g e) -> p t g e", g=4) for v in (comb, chosen))
    wb = wi.unsqueeze(2).to_broadcast([P, ST, 4, 4])
    sb2 = sel2.unsqueeze(2).to_broadcast([P, ST, 4, 4])
    comb_ready = d(lambda e: e.tensor_tensor(c4, gb, wb, ALU.mult), m7, m1)
    m8 = d(lambda e: e.tensor_tensor(s4, gb, sb2, ALU.mult), m8, m1)
    tri = K(K_TRI, ST, S)
    for t in range(ST):
        for kt in range(ST):
            m = p.pe(lambda e, t=t, kt=kt: e.matmul(b.ap[:, 64 + t * 16:80 + t * 16], tri[:, kt, t * P:(t + 1) * P], chosen[:, kt, :],
                                                    start=kt == 0, stop=kt == 1), m8, p.late_consts, b.free,
                     mark=(t == 1 and kt == 1))
    slot = small(ST, N_EXPERTS)
    b.free = m = d(lambda e: e.scalar_tensor_tensor(out=slot, in0=b.ap[:, 64:96].rearrange("p (t c) -> p t c", t=ST), scalar=1.0,
                                                    in1=chosen, op0=ALU.add, op1=ALU.mult), m, m8)
    slot_ready = d(lambda e: e.tensor_scalar(slot, slot, -1.0, None, ALU.add), m)
    ones = K(K_ONES, P)
    one = d(lambda e: e.memset(ones, 1.0), p.attention_done)
    for kt in range(ST):
        m = p.pe(lambda e, kt=kt: e.matmul(b.ap[:, 128:128 + N_EXPERTS], ones, chosen[:, kt, :], start=kt == 0, stop=kt == 1),
                 m8, one, b.free, mark=kt == 1)
    most, most_int = small(1), small(1).bitcast(mybir.dt.int32)
    b.free = m = d(lambda e: e.tensor_reduce(most, b.ap[:, 128:128 + N_EXPERTS], AX.X, ALU.max), m)
    flag_ready = d(lambda e: e.tensor_copy(most_int, most), m)
    assert at[0] <= G_AT

    p.middle_for_splits()
    iota = K(K_IOTA, P)
    Sel = p.r(11264, ST, 2 * P)
    SelT = [[p.r(11776 + 512 * i + 256 * j, ST, P) for j in range(2)] for i in range(2)]
    X = [p.split_view(4096, KD, 2 * P), p.split_view(B_AT, KD, 2 * P, arena=F)]
    Y = [p.r(8192 + D * i, D) for i in range(2)]
    hidT = p.split_view(10240, 4, P)
    silu = [F(D_AT + NB * i, NB) for i in range(2)]
    hid = [F(D_AT + 1024 + NB * i, NB) for i in range(2)]
    weight = p.stat(N_EXPERTS)
    y_banks = [(t, c, B[(2, 3, 6, 7)[2 * t + c]]) for t in range(ST) for c in range(2)]
    sel_free, selT_free, x_free = None, [router_gone] * 2, [router_gone, [router_gone, p.everyone()]]
    silu_free, hid_free, hidT_free, y_free = [None] * 2, [None] * 2, router_gone, router_gone
    sel_ready, x_parts, selT_ready, w_ready, hid_ready, Y_ready = {}, {}, {}, {}, {}, {}

    def choose(pair):
        sel_ready[pair] = [p.dve(lambda e, t=t, j=j: e.tensor_scalar(Sel[:, t, j * P:(j + 1) * P], iota,
                                                                    slot[:, t, 2 * pair + j:2 * pair + j + 1], None, ALU.is_equal),
                                 slot_ready, p.late_consts, sel_free) for t in range(ST) for j in range(2)]

    def gather(pair, part, b):
        x = X[pair % 2]
        for j in range(2):
            k = 2 * part + j
            terms = [(src, t) for src in (H_hi, H_lo) for t in range(ST)]
            for i, (src, t) in enumerate(terms):
                m = p.pe(lambda e, o=b.ap[:, j * 2 * P:(j + 1) * 2 * P], l=src[:, t, k * P:(k + 1) * P], r=Sel[:, t, :], i=i:
                         e.matmul(o, l, r, start=i == 0, stop=i == 3), sel_ready[pair], Hm, b.free, mark=(j == 1 and i == 3))
        hi, lo = x.hi_span(2 * part, 2), x.lo_span(2 * part, 2)
        a = p.act(lambda e: e.activation(hi, b.ap, ACT.Copy), m, x_free[pair % 2])
        b.free = l = p.dve(lambda e: e.tensor_tensor(lo, b.ap, hi.bitcast(F32), ALU.subtract), m, a)
        x_parts.setdefault(pair, []).append([a, l])

    def turn_choice(n, b):
        nonlocal sel_free
        s = Sel[:, :, (n % 2) * P:(n % 2 + 1) * P]
        sT = SelT[n // 2 % 2][n % 2]
        for t in range(ST):
            p.pe(lambda e, t=t: e.transpose(b.ap[:, t * P:(t + 1) * P], s[:, t, :].bitcast(F32), p.ident),
                 sel_ready[n // 2], b.free, mark=False)
        for t in range(ST):
            m = p.pe(lambda e, t=t: e.matmul(b.ap[:, S:S + 1], s[:, t, :].bitcast(F32), comb[:, t, n:n + 1],
                                             start=t == 0, stop=t == 1), comb_ready, mark=t == 1)
        sel_free = m
        w_ready[n] = p.act(lambda e: e.activation(weight[:, n:n + 1], b.ap[:, S:S + 1], ACT.Copy), m)
        b.free = selT_ready[n] = p.act(lambda e: e.activation(sT.rearrange("p a b -> p (a b)"), b.ap[:, 0:S], ACT.Copy),
                                       m, selT_free[n // 2 % 2])

    def turn_hid(n, b):
        h = hid[n % 2]
        p.transpose_in(lambda t, k: h[:, k * P:(k + 1) * P], [hid_ready[n], hidT_free], 4, 1, hidT, [b])
        hid_free[n % 2] = p.pe.now()

    def scatter(n):
        nonlocal y_free
        sT = SelT[n // 2 % 2][n % 2]
        for t, c, b in y_banks:
            for q in range(2):
                m = p.pe(lambda e, b=b, t=t, q=q, c=c: e.matmul(b.ap, sT[:, t, :], Y[q][:, c * NB:(c + 1) * NB],
                                                                start=(n == 0 and q == 0), stop=(n == N_EXPERTS - 1 and q == 1)),
                         selT_ready[n], Y_ready[n], b.free, mark=(b is B[7] and q == 1))
        y_free = m
        if n % 2 == 1:
            selT_free[n // 2 % 2] = m

    def tokens_of(n):
        x = X[n // 2 % 2]
        lhs = Split(lambda k, t: x.hi(k, n % 2), lambda k, t: x.lo(k, n % 2))
        lhs.ready = x_parts[n // 2]
        return lhs

    def down(n, between):
        nonlocal hidT_free
        m = p.run(p.gemm("wd", n, 4, hidT, (0,), lambda t, c: B[4 + c].ap, B[4:6]), between)
        hidT_free = m
        Y_ready[n] = []
        for c in range(2):
            hi, lo = Y[0][:, c * NB:(c + 1) * NB], Y[1][:, c * NB:(c + 1) * NB]
            a = p.act(lambda e, hi=hi, c=c: e.activation(hi, B[4 + c].ap, ACT.Copy), m, y_free)
            B[4 + c].free = l = p.dve(lambda e, hi=hi, lo=lo, c=c: e.tensor_tensor(lo, B[4 + c].ap, hi.bitcast(F32), ALU.subtract),
                                      m, a, y_free)
            Y_ready[n] += [a, l]

    choose(0)
    for part, bank in enumerate((B[4], B[5], B[0], B[1])):
        gather(0, part, bank)
    turn_choice(0, B[4])
    turn_choice(1, B[5])
    for n in range(N_EXPERTS):
        i, pair, odd = n % 2, n // 2 + 1, n % 2
        more = pair < N_EXPERTS // 2
        parts = (2, 3) if odd else (0, 1)
        steps = {j: [] for j in range(12)}
        if n >= 1:
            steps[0].append(lambda: turn_hid(n - 1, B[1]))
        if more and not odd:
            steps[1].append(lambda: choose(pair))
        if n >= 2:
            steps[2].append(lambda: scatter(n - 2))
        if more:
            steps[4].append(lambda: gather(pair, parts[0], B[4]))
            steps[6].append(lambda: gather(pair, parts[1], B[5]))
            if odd:
                steps[9].append(lambda: turn_choice(2 * pair, B[0]))
                steps[10].append(lambda: turn_choice(2 * pair + 1, B[1]))
        part_of = lambda first: {j: steps[first + j] for j in range(4)}
        lhs = tokens_of(n)
        mg = p.run(p.gemm("wg", n, KD, lhs, (0,), lambda t, c: B[0].ap, B[0:1]), part_of(0))
        B[0].free = a = p.act(lambda e, i=i: e.activation(silu[i], B[0].ap, ACT.Silu), mg, silu_free[i])
        mu = p.run(p.gemm("wu", n, KD, lhs, (0,), lambda t, c: B[1].ap, B[1:2]), part_of(4))
        if odd:
            x_free[n // 2 % 2] = mu
        B[1].free = hid_ready[n] = silu_free[i] = p.dve(
            lambda e, i=i, n=n: e.scalar_tensor_tensor(out=hid[i], in0=silu[i], scalar=weight[:, n:n + 1], in1=B[1].ap,
                                                       op0=ALU.mult, op1=ALU.mult), mu, a, w_ready[n], hid_free[i])
        if n >= 1:
            down(n - 1, part_of(8))
    last = N_EXPERTS - 1
    turn_hid(last, B[0])
    down(last, {2: [lambda: scatter(last - 1)]})
    p.y_banks = y_banks
    overflow(p, most_int[0:1, 0:1], flag_ready, H_hi, H_lo, comb, slot, slot_ready)
    scatter(last)
    p.y_ready = [y_free]


def overflow(p, flag, flag_ready, H_hi, H_lo, comb, slot, slot_ready):
    B, F = p.banks, p.f
    sem = lambda n: p.ctx.enter_context(p.nc.semaphore(n))
    pe, dve, act, pool, sp = (Lane(n, sem("over_" + n)) for n in ("pe", "dve", "act", "pool", "sp"))
    lines = [Line(sem(f"over_weights_{i}")) for i in range(3)]
    before = [p.pe.now(), p.dve.now(), p.act.now()]
    slot2 = p.stat(2 * N_EXPERTS).rearrange("p (t e) -> p t e", t=ST)
    weight = p.stat(1)
    X, Y = F(M_AT, KD, P), F(M_AT + D, D)
    sel, selT = F(T_AT, ST, P), F(T_AT + 256, ST, P)
    hid, silu, hidT = F(T_AT + 512, NB), F(T_AT + 1024, NB), F(T_AT + 1536, 4, P)
    raw = [p.raw[:, 0:4096], p.raw[:, 4096:8192]]
    iota = p.k(K_IOTA, P)
    state = {"m": dve(lambda e: e.tensor_scalar(slot2, slot, -float(SLOTS), None, ALU.add), before, slot_ready)}

    def expert(n):
        start = state["m"]
        wg_in = sp.dma(lambda e: e.dma_start(raw[0], p.dram["wg"][n]), lines[0], start)
        wu_in = sp.dma(lambda e: e.dma_start(raw[1], p.dram["wu"][n]), lines[1], start)
        ms = [dve(lambda e, t=t: e.tensor_scalar(sel[:, t, :], iota, slot2[:, t, n:n + 1], None, ALU.is_equal), start)
              for t in range(ST)]
        xs = []
        for half in range(2):
            bank = B[4 + half]
            for k in range(4 * half, 4 * half + 4):
                parts = [(src, t) for src in (H_hi, H_lo) for t in range(ST)]
                for j, (src, t) in enumerate(parts):
                    m = pe(lambda e, o=bank.ap[:, (k % 4) * P:(k % 4 + 1) * P], l=src[:, t, k * P:(k + 1) * P].bitcast(F32),
                           r=sel[:, t, :], j=j: e.matmul(o, l, r, start=j == 0, stop=j == 3), ms, start, mark=(j == 3 and k % 4 == 3))
            xs.append(act(lambda e, o=X[:, 4 * half:4 * half + 4, :].rearrange("p a b -> p (a b)"), i=bank.ap:
                          e.activation(o, i, ACT.Copy), m))
        for t in range(ST):
            pe(lambda e, t=t: e.transpose(B[0].ap[:, t * P:(t + 1) * P], sel[:, t, :], p.ident), mark=False)
        for t in range(ST):
            m = pe(lambda e, t=t: e.matmul(B[0].ap[:, S:S + 1], sel[:, t, :], comb[:, t, n:n + 1], start=t == 0, stop=t == 1),
                   mark=t == 1)
        w = act(lambda e: e.activation(weight, B[0].ap[:, S:S + 1], ACT.Copy), m)
        selT_in = act(lambda e: e.activation(selT.rearrange("p a b -> p (a b)"), B[0].ap[:, 0:S], ACT.Copy), m)
        mg = mu = None
        for k in range(KD):
            mg = pe(lambda e, k=k: e.matmul(B[0].ap, X[:, k, :], raw[0][:, k * NB:(k + 1) * NB], start=k == 0, stop=k == KD - 1),
                    xs, selT_in, wg_in, mark=k == KD - 1)
        for k in range(KD):
            mu = pe(lambda e, k=k: e.matmul(B[1].ap, X[:, k, :], raw[1][:, k * NB:(k + 1) * NB], start=k == 0, stop=k == KD - 1),
                    wu_in, mark=k == KD - 1)
        wd_in = sp.dma(lambda e: e.dma_start(raw[0], p.dram["wd"][n]), lines[2], mg)
        a = act(lambda e: e.activation(silu, B[0].ap, ACT.Silu), mg)
        r = dve(lambda e: e.scalar_tensor_tensor(out=hid, in0=silu, scalar=weight, in1=B[1].ap, op0=ALU.mult, op1=ALU.mult),
                a, w, mu)
        for k in range(4):
            m = pe(lambda e, k=k: e.transpose(B[4].ap[:, k * P:(k + 1) * P], hid[:, k * P:(k + 1) * P], p.ident), r, mark=k == 3)
        a = act(lambda e: e.activation(hidT.rearrange("p a b -> p (a b)"), B[4].ap, ACT.Copy), m)
        for c in range(2):
            for k in range(4):
                m = pe(lambda e, k=k, c=c: e.matmul(B[4 + c].ap, hidT[:, k, :], raw[0][:, (2 * k + c) * NB:(2 * k + c + 1) * NB],
                                                    start=k == 0, stop=k == 3), a, wd_in, mark=k == 3)
        ys = [act(lambda e, c=c: e.activation(Y[:, c * NB:(c + 1) * NB], B[4 + c].ap, ACT.Copy), m) for c in range(2)]
        for t, c, bank in p.y_banks:
            m = pe(lambda e, bank=bank, t=t, c=c: e.matmul(bank.ap, selT[:, t, :], Y[:, c * NB:(c + 1) * NB], start=False, stop=False),
                   ys, selT_in)
        state["m"] = [m, ys]

    for n in range(N_EXPERTS):
        expert(n)
    ends = [pe.now(), dve.now(), act.now()] + [(l.sem, l.count) for l in lines]
    for main, section in ((p.pe, pe), (p.dve, dve), (p.act, act), (p.sp, sp)):
        section.ops.append((section.needed(ends), lambda e: e.nop(), None, 0))
        main.only_if(flag, SLOTS + 1, flag_ready, section)


def shape_constants():
    f = np.float32
    t = np.arange(S)
    q = np.arange(P)
    out = {"ident": np.eye(P, dtype=f)}
    sel = np.zeros((P, 130), f)
    sel[[0, 1, 4], 0:P] = 1.0
    sel[[0, 1, 4], P] = 1.0
    sel[[2, 3, 4], P + 1] = 1.0
    out["sel"] = sel
    dist = -np.abs(t[:, None] - t[None, :]).astype(f)
    allowed = (t[None, :] // CHUNK) <= (t[:, None] // CHUNK)
    dist = np.where(allowed, dist, f(BIG)).astype(f)
    out["dist"] = np.ascontiguousarray(dist.reshape(ST, P, S).transpose(1, 0, 2))
    slopes = np.array([2.0 ** (-8.0 * (i + 1) / HEADS) for i in range(HEADS)], dtype=f)
    out["slopes"] = np.ascontiguousarray((np.eye(P, dtype=f)[:, None, :] * slopes[None, :, None]).astype(f))
    m = np.zeros((4, S, S), f)
    for g, w in enumerate(POOL_WINDOWS):
        lo = np.maximum(t + 1 - w, 0)
        for i in t:
            m[g, lo[i]:i + 1, i] = 1.0 / (i + 1 - lo[i])
            m[g, i, i] -= 1.0
    out["pool_m"] = np.ascontiguousarray(m.reshape(4, ST, P, S).transpose(2, 0, 1, 3))
    half = ROPE // 2
    freq = (10000.0 ** (-np.arange(0, half, 2, dtype=f) / half)).astype(f)
    ang = np.concatenate([(t // GRID_W).astype(f)[:, None] * freq, (t % GRID_W).astype(f)[:, None] * freq], axis=-1)
    rope = np.stack([np.cos(ang), np.sin(ang)]).astype(f)
    out["rope"] = np.ascontiguousarray(rope.reshape(2, ST, P, half).transpose(2, 1, 0, 3))
    col = np.arange(GRID_W)
    start = np.clip(col - WIN_W // 2, 0, GRID_W - WIN_W)
    inside = (col[None, :] >= start[:, None]) & (col[None, :] < start[:, None] + WIN_W)
    out["col_mask"] = np.where(inside, f(0), f(BIG))[q % GRID_W].astype(f)
    out["tri"] = np.ascontiguousarray((t[:, None] < t[None, :]).astype(f).reshape(ST, P, S).transpose(1, 0, 2))
    out["iota"] = np.tile(np.arange(P, dtype=f), (P, 1))
    return out


def by_chunk(w, n):
    k, cols = w.shape
    return np.ascontiguousarray(w.reshape(k // P, P, cols // n, n).transpose(2, 1, 0, 3)).reshape(cols // n, P, -1)


def by_rows(w, rows):
    k, cols = w.shape
    return np.ascontiguousarray(w.reshape(k // rows, rows // P, P, cols).transpose(0, 2, 1, 3)).reshape(k // rows, P, -1)


def lay_out(a):
    o = dict(shape_constants())
    o["x"] = a["x"][0]
    col = lambda v: v.reshape(-1, P).T
    vectors = {"g_mix": a["g_mix"][0], "g_ffn": a["g_ffn"][0], "norm_attn_g": a["norm_attn_g_2"][0],
               "pool_scale": a["pool_scale"][0], "g_q": np.concatenate([a["g_q"][0]] * 2), "g_k": np.concatenate([a["g_k"][0]] * 2),
               "g_sub": a["g_sub"][0], "q_a_g": a["q_a_norm_g_2"][0], "kv_a_g": a["kv_a_norm_g_2"][0],
               "c": a["c_2"][0], "c_ctx": a["c_ctx_2"]}
    o["cols"] = np.ascontiguousarray(np.concatenate([col(vectors[n]) for n, _ in COLS], axis=1))
    o["lambda_rows"] = a["lambda_qk"][0].reshape(1, 256)
    o["b_gate"] = a["b_gate"][0].reshape(1, -1)
    o["b_mod"] = a["b_mod_2"][0].reshape(12, NB)
    o["w_grp"] = np.ascontiguousarray(a["w_pool_grp"][0].transpose(1, 0, 2))
    o["w_in"] = by_chunk(a["w_in"][0], 512)
    o["w_gate"] = by_chunk(a["w_gate"][0], 512)
    o["w_bp"] = by_rows(a["w_branch_pool"][0], 512)
    o["w_ba"] = by_rows(a["w_branch_attn"][0], 512)
    o["w_out"] = by_chunk(a["w_out"][0], 512)
    o["w_up"] = by_chunk(a["w_up"][0], 512)
    o["w_down"] = by_rows(a["w_down"][0], 512)
    o["w_mod"] = by_chunk(a["w_mod_2"][0], 512)
    w = a["w_in_2"][0]
    c0 = Q_LORA + 512
    o["w_in2q"] = by_chunk(np.ascontiguousarray(w[:, 0:Q_LORA]), Q_LORA)
    o["w_in2nq"] = by_chunk(np.ascontiguousarray(w[:, Q_LORA:c0]), 512)
    o["w_in2kv"] = by_chunk(np.ascontiguousarray(w[:, c0:c0 + 288]), 288)
    o["w_in2k"] = by_chunk(np.ascontiguousarray(w[:, c0 + 288:c0 + 800]), 512)
    o["w_in2v"] = by_chunk(np.ascontiguousarray(w[:, c0 + 800:c0 + 1312]), 512)
    o["w_uq"] = by_rows(a["w_uq_2"][0], Q_LORA)
    o["w_ukv"] = by_chunk(a["w_ukv_2"][0], 512)
    o["w_out2"] = by_chunk(a["w_out_2"][0], 512)
    wg, wu, wd = a["w_gate_2"][0], a["w_up_2"][0], a["w_down_2"][0]
    o["wg"] = np.stack([by_chunk(wg[e], 512)[0] for e in range(N_EXPERTS)])
    o["wu"] = np.stack([by_chunk(wu[e], 512)[0] for e in range(N_EXPERTS)])
    o["wd"] = np.stack([by_rows(wd[e], 512)[0] for e in range(N_EXPERTS)])
    o["ctx"] = a["ctx_2"][0]
    o["norm_ffn_g"] = a["norm_ffn_g_2"][0].reshape(1, D)
    o["final_g"] = a["final_norm_g_2"].reshape(1, D)
    o["w_router"] = np.ascontiguousarray(np.concatenate([a["w_router_group_2"][0], a["w_router_expert_2"][0]], axis=1)
                                         .reshape(KD, P, 20).transpose(1, 0, 2))
    o["b_router"] = np.concatenate([a["b_router_group_2"][0], a["b_router_expert_2"][0]]).reshape(1, 20)
    rb = a["na_rel_bias_2"][0]
    pad = np.pad(rb, ((0, 0), (0, 0), (48, 48)))
    rows = np.stack([pad[:, :, 63 - q:127 - q] for q in range(GRID_W)], axis=1)
    tiles = [np.concatenate([rows[:, :, 7 - r:11 - r].reshape(HEADS, GRID_W, S) for r in (2 * t, 2 * t + 1)], axis=1)
             for t in range(ST)]
    o["rel_rows"] = np.ascontiguousarray(np.stack(tiles, axis=2))
    return {k: v if v.dtype == np.float32 and v.flags.c_contiguous else np.ascontiguousarray(v) for k, v in o.items()}


BROADCAST = ("lambda_rows", "b_gate", "norm_ffn_g", "final_g", "b_router")


def build(nc, arrays, upto=None):
    dram = {}
    for name, a in arrays.items():
        ap = nc.dram_tensor("in_" + name, list(a.shape), F32, kind="ExternalInput").ap()
        if name in BROADCAST:
            ap = ap.rearrange("a b -> (a b)").partition_broadcast(P)
        dram[name] = ap
    dram["lambda_rows"] = dram["lambda_rows"].rearrange("p (a b) -> p a b", a=4)
    with ExitStack() as ctx:
        p = Program(nc, ctx, dram, upto)
        try:
            begin(p)
            block_one(p)
            block_two(p)
        except Stop:
            ap, marks = p.store
            out = nc.dram_tensor("out", [P, ap.shape[-1]], F32, kind="ExternalOutput").ap()
            p.out_mark = p.load(out, ap, marks, lane=p.act)
            p.act.ops.append((p.act.needed([(l.sem, l.count) for l in p.lines if l.count]), lambda e: e.nop(), None, 0))
        block = ctx.enter_context(nc.Block())

        @block.sync
        def _(eng):
            p.sp.play(eng)

        @block.scalar
        def _(eng):
            p.act.play(eng)

        @block.vector
        def _(eng):
            p.dve.play(eng)

        @block.gpsimd
        def _(eng):
            p.pool.play(eng)

        @block.tensor
        def _(eng):
            p.pe.play(eng)


def kernel(**inputs):
    from concourse import bacc
    from concourse.bass_utils import run_bass_kernel_spmd

    arrays = lay_out({k: np.asarray(v) for k, v in inputs.items()})
    nc = bacc.Bacc("TRN2", target_bir_lowering=False, num_devices=1)
    build(nc, arrays)
    r = run_bass_kernel_spmd(nc, [{"in_" + k: v for k, v in arrays.items()}], core_ids=[0])
    return r.results[0]["out"].reshape(1, S, D)
```

```python
from contextlib import ExitStack

import numpy as np
import concourse.bass as bass
from concourse import mybir

F32 = mybir.dt.float32
F32R = mybir.dt.float32r
ALU = mybir.AluOpType
ACT = mybir.ActivationFunctionType
AX = mybir.AxisListType

P = 128
S = 256
ST = S // P
D = 1024
KD = D // P
NB = 512
EPS = 1e-6
HEADS = 8
POOL_WINDOWS = (2, 4, 8, 16)
POOL_DIM = 512
D_FF = 4096
LAMBDA_INIT = 0.8 - 0.6 * float(np.exp(-0.3 * 0))
CHUNK = 64
CTX = 256
TT = (S + CTX) // P
Q_LORA, KV_LORA, ROPE, NOPE = 384, 256, 32, 64
QK = NOPE + ROPE
GRID_W, WIN_W = 64, 16
N_GROUPS, PER_GROUP = 4, 4
N_EXPERTS = N_GROUPS * PER_GROUP
D_EXPERT = 512
SLOTS = 128
BIG = -1e30

PIECE = 1024
N_PIECES = 5
N_RAW = 4

X_AT, B_AT, C_AT, D_AT, E_AT, G_AT, T_AT, M_AT, Z_AT = 0, 2048, 4096, 6144, 8192, 10240, 14336, 16384, 17408
ARENA = 18432
K_IDENT, K_DIST, K_SLOPE = 0, 128, 640
K_TRI, K_IOTA, K_ROPE, K_COLMASK, K_ONES = 128, 640, 768, 832, 896
K_COLS, K_SEL = 1664, 1792
K_MHALF = 1922
K_MODROWS = 1024
K_LAM = 1986

COLS = [("g_mix", 8), ("g_ffn", 8), ("norm_attn_g", 8), ("pool_scale", 4), ("g_q", 1), ("g_k", 1),
        ("g_sub", 1), ("q_a_g", 3), ("kv_a_g", 2), ("c", 8), ("c_ctx", 8)]
COL0, _at = {}, 0
for _n, _w in COLS:
    COL0[_n] = _at
    _at += _w
N_COLS = _at


def mod_units(*chunks):
    return [("w_mod", n, 8, 512, 1) for n in chunks]


def block_one_units():
    t = []
    t += [("w_in", n, 8, 512, 1) for n in range(7)]
    t += [("w_gate", n, 8, 512, 1) for n in range(4)]
    t += [("w_bp", 0, 4, 512, 2)]
    t += [("w_ba", n, 4, 512, 2) for n in range(2)]
    t += mod_units(1, 2)
    t += [("w_out", n, 8, 512, 1) for n in range(2)]
    t += mod_units(3, 4)
    for n in range(2):
        t += [("w_up", n, 8, 512, 1)]
    for n in range(2, 10):
        t += [("w_down", n - 2, 4, 512, 2)]
        if n < 8:
            t += [("w_up", n, 8, 512, 1)]
    t += mod_units(5, 6, 7)
    return t


def block_two_units():
    t = [("w_in2kv", 0, 8, 288, 1), ("w_in2k", 0, 8, 512, 1), ("w_in2v", 0, 8, 512, 1),
         ("w_in2q", 0, 8, 384, 1), ("w_in2nq", 0, 8, 512, 1)]
    t += [("w_uq", 0, 3, 384, 2)]
    t += [("w_ukv", n, 2, 512, 1) for n in range(2)]
    t += mod_units(8, 9)
    t += [("w_out2", n, 8, 512, 1) for n in range(2)]
    t += mod_units(10, 11)
    for e in range(N_EXPERTS):
        t += [("wg", e, 8, 512, 1), ("wu", e, 8, 512, 1)]
        if e > 0:
            t += [("wd", e - 1, 4, 512, 2)]
    t += [("wd", N_EXPERTS - 1, 4, 512, 2)]
    return t


UNITS = mod_units(0) + block_one_units() + block_two_units()


class Lane:

    def __init__(self, name, sem):
        self.name, self.sem, self.count, self.ops, self.seen = name, sem, 0, [], {}

    def __call__(self, fn, *after, mark=True):
        self.ops.append((self.needed(after), fn, self.sem if mark else None, 1))
        if mark:
            self.count += 1
            return (self.sem, self.count)
        return None

    def needed(self, after):
        out = []
        for m in flat(after):
            if self.seen.get(id(m[0]), 0) < m[1]:
                self.seen[id(m[0])] = m[1]
                out.append(m)
        return out

    def dma(self, fn, line, *after):
        self.ops.append((self.needed(after), fn, line.sem, 16))
        line.count += 16
        return (line.sem, line.count)

    def now(self):
        return (self.sem, self.count) if self.count else None

    def only_if(self, flag, least, ready, section):
        self.ops.append((self.needed([ready]), (flag, least, section), None, 0))

    def play(self, eng):
        for waits, fn, sem, by in self.ops:
            for s, v in waits:
                eng.wait_ge(s, v)
            if isinstance(fn, tuple):
                flag, least, section = fn
                value = eng.value_load(flag)
                with eng.If(value >= least):
                    section.play(eng)
                continue
            ins = fn(eng)
            if sem is not None:
                ins.then_inc(sem, by)


def flat(x):
    if x is None:
        return
    if isinstance(x, tuple) and len(x) == 2 and isinstance(x[1], int):
        yield x
        return
    for y in x:
        yield from flat(y)


class Line:
    def __init__(self, sem):
        self.sem, self.count = sem, 0


class Bank:

    def __init__(self, ap):
        self.ap, self.free = ap, None


class Piece:

    def __init__(self, name, n, load, raw0, cols, blocks):
        self.name, self.n, self.load, self.raw0, self.cols, self.blocks = name, n, load, raw0, cols, blocks
        self.split = None
        self.used = None


class Split:

    def __init__(self, hi, lo):
        self.hi, self.lo, self.ready = hi, lo, None


class Stop(Exception):
    pass


class Program:
    def __init__(self, nc, ctx, dram, upto=None, probe=None):
        self.nc, self.ctx, self.dram, self.upto, self.probe = nc, ctx, dram, upto, probe
        sem = lambda n: ctx.enter_context(nc.semaphore(n))
        self.lines = []
        self.pe, self.dve, self.act, self.pool, self.sp = (
            Lane(n, sem("done_" + n)) for n in ("pe", "dve", "act", "pool", "sp"))
        sb = lambda n, w, dt=F32: ctx.enter_context(nc.sbuf_tensor(n, [P, w], dt))
        self.raw = sb("raw_weights", N_RAW * 2 * PIECE)
        self.whi = sb("weights_hi", N_PIECES * PIECE, F32R)
        self.wlo = sb("weights_lo", N_PIECES * PIECE, F32R)
        self.R = sb("split_arena", 12800, F32R)
        self.F = [[0, sb("arena_x", B_AT)], [B_AT, None], [D_AT, sb("arena", ARENA - D_AT)]]
        self.K = sb("constants", 2048)
        self.stats = sb("stats", 1024)
        self.middle = ctx.enter_context(ExitStack())
        self.F[1][1] = self.middle.enter_context(nc.sbuf_tensor("arena_middle", [P, D_AT - B_AT], F32))
        self.stat_at = 0
        ps = ctx.enter_context(nc.psum_tensor("psum", [P, 8, NB], F32))
        self.ps = ps
        self.banks = [Bank(ps[:, i, :]) for i in range(8)]
        self.raw_lines = [self.newline(f"raw_{i}") for i in range(N_RAW)]
        self.plan_weights()

    def newline(self, name):
        self.lines.append(Line(self.ctx.enter_context(self.nc.semaphore(name))))
        return self.lines[-1]

    def stat(self, n):
        a = self.stats[:, self.stat_at:self.stat_at + n]
        self.stat_at += n
        assert self.stat_at <= 1024
        return a

    def middle_for_splits(self):
        self.middle.close()
        self.F[1][1] = self.middle.enter_context(self.nc.sbuf_tensor("arena_middle_split", [P, D_AT - B_AT], F32R))

    def f(self, at, *dims):
        n = int(np.prod(dims))
        first, arena = [a for a in self.F if a[0] <= at][-1]
        v = arena[:, at - first:at - first + n]
        return split_dims(v, dims)

    def r(self, at, *dims):
        n = int(np.prod(dims))
        return split_dims(self.R[:, at:at + n], dims)

    def k(self, at, *dims):
        n = int(np.prod(dims))
        return split_dims(self.K[:, at:at + n], dims)

    def plan_weights(self):
        self.loads, self.pieces = [], []
        for name, n, kt, w, chunks in UNITS:
            total = kt * w * chunks
            blocks = [(k, c, (k * chunks + c) * w, w) for k in range(kt) for c in range(chunks)]
            per = PIECE // w if chunks == 1 else chunks
            cut = [blocks[i:i + per] for i in range(0, len(blocks), per)]
            for i in range(0, len(cut), 2):
                pair = cut[i:i + 2]
                c0 = pair[0][0][2]
                c1 = pair[-1][-1][2] + w
                load = dict(name=name, n=n, c0=c0, c1=c1, pieces=[], mark=None)
                for bl in pair:
                    pc = Piece(name, n, len(self.loads), bl[0][2] - c0, len(bl) * w,
                               [(k, c, at - bl[0][2], w) for k, c, at, w in bl])
                    load["pieces"].append(pc)
                    self.pieces.append(pc)
                self.loads.append(load)
            assert total == blocks[-1][2] + w
        self.next_piece = self.next_split = self.next_load = 0
        self.hold = False

    def feed(self, loads_only=False):
        while not self.hold:
            moved = False
            i = self.next_load
            if i < len(self.loads):
                old = self.loads[i - N_RAW]["pieces"] if i >= N_RAW else []
                if all(p.split for p in old):
                    ld = self.loads[i]
                    dst = self.raw[:, (i % N_RAW) * 2 * PIECE:(i % N_RAW) * 2 * PIECE + ld["c1"] - ld["c0"]]
                    src = self.dram[ld["name"]][ld["n"], :, ld["c0"]:ld["c1"]]
                    ld["mark"] = self.sp.dma(lambda e, d=dst, s=src: e.dma_start(d, s), self.raw_lines[i % N_RAW],
                                             [p.split for p in old])
                    self.next_load += 1
                    moved = True
            j = self.next_split
            if j < len(self.pieces) and j < self.next_piece + N_PIECES and not loads_only:
                pc = self.pieces[j]
                ld = self.loads[pc.load]
                if ld["mark"] is not None:
                    old = self.pieces[j - N_PIECES].used if j >= N_PIECES else None
                    slot = (j % N_PIECES) * PIECE
                    pc.hi = self.whi[:, slot:slot + pc.cols]
                    pc.lo = self.wlo[:, slot:slot + pc.cols]
                    r0 = (pc.load % N_RAW) * 2 * PIECE + pc.raw0
                    raw = self.raw[:, r0:r0 + pc.cols]
                    hi = self.act(lambda e, o=pc.hi, i=raw: e.activation(o, i, ACT.Copy), ld["mark"], old)
                    lo = self.dve(lambda e, o=pc.lo, i=raw, h=pc.hi: e.tensor_tensor(o, i, h.bitcast(F32), ALU.subtract),
                                  ld["mark"], old, hi)
                    pc.split = [hi, lo]
                    self.next_split += 1
                    moved = True
            if not moved:
                return

    def take(self, name, n):
        self.feed()
        pc = self.pieces[self.next_piece]
        assert (pc.name, pc.n) == (name, n), ((pc.name, pc.n), (name, n))
        assert pc.split
        return pc

    def gemm(self, name, n, kt, lhs, tiles, out, banks, k0=0, first=True, last=True, after=None):
        npieces = sum(1 for p in self.pieces if (p.name, p.n) == (name, n))
        mark = None
        for i in range(npieces):
            pc = self.take(name, n)
            wait = [pc.split, lhs.ready, after, [b.free for b in banks]]
            for t in tiles:
                for k, c, at, w in pc.blocks:
                    o = out(t, c)
                    st = first and k == 0
                    en = last and k == kt - 1
                    ah, al = lhs.hi(k0 + k, t), lhs.lo(k0 + k, t)
                    wh, wl = pc.hi[:, at:at + w], pc.lo[:, at:at + w]
                    self.pe(lambda e, o=o, a=ah, b=wh, s=st: e.matmul(o, a, b, start=s, stop=False), wait, mark=False)
                    wait = None
                    self.pe(lambda e, o=o, a=ah, b=wl: e.matmul(o, a, b, start=False, stop=False), mark=False)
                    final = t == tiles[-1] and (k, c, at, w) == pc.blocks[-1]
                    mark = self.pe(lambda e, o=o, a=al, b=wh, z=en: e.matmul(o, a, b, start=False, stop=z), mark=final)
            pc.used = mark
            self.next_piece += 1
            if i < npieces - 1:
                self.feed()
                yield None
        self.last_gemm = mark
        yield mark

    def run(self, gen, between=None):
        m = None
        for i, m in enumerate(gen):
            for step in (between or {}).get(i, ()):
                step()
        return m

    def rstd(self, ss, out, n, *after):
        w = ss.shape[-1]
        t = self.stat(w)
        a = self.pool(lambda e: e.tensor_scalar(t, ss, 1.0 / n, EPS, ALU.mult, ALU.add), *after)
        return self.pool(lambda e: e.tensor_tensor(out, t, self.minus_half[:, 0:w], ALU.pow), a, self.const_ready)

    def row_norm(self, src, tiles, dst, scratch, *after, meanwhile=()):
        ss, rs = self.stat(tiles), self.stat(tiles)
        ms = []
        for t in range(tiles):
            i, o, acc = src(t), scratch(t), ss[:, t:t + 1]
            if t % 2 == 0:
                ms.append(self.act(lambda e, i=i, o=o, acc=acc: e.activation(o, i, ACT.Square, accum_out=acc), *after))
            else:
                ms.append(self.dve(lambda e, i=i, o=o, acc=acc: e.scalar_tensor_tensor(
                    out=o, in0=i, scalar=1.0, in1=i, op0=ALU.mult, op1=ALU.mult, accum_out=acc), *after))
        m = self.rstd(ss, rs, D, ms)
        for step in meanwhile:
            step()
        return [self.dve(lambda e, i=src(t), o=dst(t), r=rs[:, t:t + 1]: e.tensor_scalar(o, i, r, None, ALU.mult), m, *after)
                for t in range(tiles)]

    def transpose_in(self, src, ready, nk, tiles, dst, banks, scale=None, bias=None, tmp=None, toks=None):
        ident = self.ident
        width = tiles * P
        per = NB // width
        marks = []
        for j in range(0, nk, per):
            b = banks[(j // per) % len(banks)]
            ks = list(range(j, min(j + per, nk)))
            for k in ks:
                for t in range(tiles):
                    o = b.ap[:, (k - j) * width + t * P:(k - j) * width + (t + 1) * P]
                    m = self.pe(lambda e, o=o, i=src(t, k): e.transpose(o, i, ident), ready, b.free, self.const_ready,
                                mark=(k == ks[-1] and t == tiles - 1))
            hs, ls = [], []
            if scale is None:
                o = b.ap[:, 0:len(ks) * width]
                hi, lo = dst.hi_span(j, len(ks)), dst.lo_span(j, len(ks))
                h = self.act(lambda e, o=o, hi=hi: e.activation(hi, o, ACT.Copy), m)
                l = self.dve(lambda e, o=o, hi=hi, lo=lo: e.tensor_tensor(lo, o, hi.bitcast(F32), ALU.subtract), m, h)
                hs.append(h)
                ls.append(l)
            elif bias is None:
                for k in ks:
                    o = b.ap[:, (k - j) * width:(k - j + 1) * width]
                    hs.append(self.act(lambda e, o=o, k=k: e.activation(dst.hi_span(k, 1), o, ACT.Copy, scale=scale(k)), m, ls))
                for k in ks:
                    o = b.ap[:, (k - j) * width:(k - j + 1) * width]
                    ls.append(self.dve(lambda e, o=o, k=k: e.scalar_tensor_tensor(
                        out=dst.lo_span(k, 1), in0=o, scalar=scale(k), in1=dst.hi_span(k, 1).bitcast(F32),
                        op0=ALU.mult, op1=ALU.subtract), m, hs))
            else:
                for k in ks:
                    o = b.ap[:, (k - j) * width:(k - j + 1) * width]
                    tm = tmp(k)
                    v = self.dve(lambda e, o=o, k=k, tm=tm: e.tensor_scalar(tm, o, scale(k), bias(k), ALU.mult, ALU.add), m)
                    hs.append(self.act(lambda e, k=k, tm=tm: e.activation(dst.hi_span(k, 1), tm, ACT.Copy), v))
                b.free = v
                for k, h in zip(ks, hs):
                    l = self.dve(lambda e, k=k, tm=tmp(k): e.tensor_tensor(
                        dst.lo_span(k, 1), tm, dst.hi_span(k, 1).bitcast(F32), ALU.subtract), v, h)
                ls.append(l)
            if bias is None:
                b.free = [hs[-1], ls[-1]]
            marks.append([hs, ls])
        dst.ready = marks
        return marks

    def split_view(self, at, nk, toks, arena=None):
        r = arena or self.r
        hi, lo = r(at, nk, toks), r(at + nk * toks, nk, toks)
        s = Split(lambda k, t: hi[:, k, t * P:(t + 1) * P], lambda k, t: lo[:, k, t * P:(t + 1) * P])
        s.hi_span = lambda k, n: r(at + k * toks, n * toks)
        s.lo_span = lambda k, n: r(at + nk * toks + k * toks, n * toks)
        return s

    def load(self, dst, src, *after, lane=None):
        return (lane or self.pool).dma(lambda e: e.dma_start(dst, src), self.newline(f"load_{len(self.lines)}"), *after)

    def everyone(self):
        return [m for m in (self.pe.now(), self.dve.now(), self.act.now(), self.pool.now()) if m]

    def checkpoint(self, name, ap, marks):
        if self.upto == name:
            self.store = (ap, marks)
            raise Stop()


def split_dims(v, dims):
    if len(dims) == 1:
        return v
    if len(dims) == 2:
        return v.rearrange("p (a b) -> p a b", a=dims[0])
    return v.rearrange("p (a b c) -> p a b c", a=dims[0], b=dims[1])



def begin(p):
    d = p.dram
    p.ident = p.k(K_IDENT, P)
    p.minus_half = p.k(K_MHALF, 62)
    x = p.f(X_AT, ST, D)
    p.x = x
    p.x_in = p.load(x, d["x"].rearrange("(t q) d -> q t d", q=P), lane=p.sp)
    cols_in = p.load(p.k(K_COLS, N_COLS), d["cols"], lane=p.act)
    ident_in = p.load(p.k(K_IDENT, P), d["ident"], lane=p.act)
    sel_in = p.load(p.k(K_SEL, 130), d["sel"], lane=p.act)
    lam_in = p.load(p.f(T_AT, 4, 64), d["lambda_rows"], lane=p.act)
    dist_in = p.load(p.k(K_DIST, ST, S), d["dist"], lane=p.act)
    slope_in = p.load(p.k(K_SLOPE, HEADS, P), d["slopes"], lane=p.act)
    p.attn_consts = [dist_in, slope_in]
    half = p.dve(lambda e: e.memset(p.minus_half, -0.5))
    p.const_ready = [half, ident_in, cols_in]
    p.col = lambda name, k: p.k(K_COLS + COL0[name] + k, 1)
    p.sel_in = sel_in
    p.cols_in, p.lam_in = cols_in, lam_in
    p.mod_f = p.stat(64).rearrange("p (k two) -> p k two", two=2)
    p.mod_rows_made, p.mod_bias_in = {}, {}
    p.feed(loads_only=True)


def conditions(p):
    cs = p.r(11776, KD, P)
    zero = p.dve(lambda e: e.memset(cs.bitcast(F32), 0.0))
    c16 = p.k(K_COLS + COL0["c"], 16)
    sil = p.stat(16)
    a = p.act(lambda e: e.activation(sil, c16, ACT.Silu), p.cols_in)
    marks = []
    for j in range(2):
        copies = cs.rearrange("p k (i c) -> p k i c", i=4)[:, :, 0:3, :]
        hi, lo = copies[:, :, :, 2 * j], copies[:, :, :, 2 * j + 1]
        v = sil[:, 8 * j:8 * j + 8].unsqueeze(2).to_broadcast([P, KD, 3])
        h = p.dve(lambda e, hi=hi, v=v: e.tensor_copy(hi, v), a, zero)
        marks.append(p.dve(lambda e, hi=hi, lo=lo, v=v: e.tensor_tensor(lo, v, hi.bitcast(F32), ALU.subtract), h))
    p.cs = Split(lambda k, t: cs[:, k, :], None)
    p.cs.ready = marks


def attention_scalars(p):
    p.slopes, p.dist = p.r(4096, HEADS, P), p.r(5120, ST, S)
    p.attn_consts = [p.dve(lambda e, o=o, i=i: e.tensor_copy(o, i), ready) for o, i, ready in (
        (p.slopes, p.k(K_SLOPE, HEADS, P), p.attn_consts[1]), (p.dist, p.k(K_DIST, ST, S), p.attn_consts[0]))]
    rows = p.f(T_AT, 4, 64)
    prod = p.f(T_AT + 256, 2, 64)
    pair = rows.rearrange("p (a b) c -> p a b c", b=2)
    m = p.dve(lambda e: e.tensor_tensor(prod, pair[:, :, 0, :], pair[:, :, 1, :], ALU.mult), p.lam_in)
    sums, ex = p.stat(2), p.stat(2)
    m = p.dve(lambda e: e.tensor_reduce(sums, prod, AX.X, ALU.add), m)
    m = p.act(lambda e: e.activation(ex, sums, ACT.Exp), m)
    p.neg_lam = p.k(K_LAM, 1)
    m = p.dve(lambda e: e.tensor_tensor(p.neg_lam, ex[:, 1:2], ex[:, 0:1], ALU.subtract), m)
    p.sub_gain = p.k(K_LAM + 1, 1)
    p.sub_ready = p.dve(lambda e: e.tensor_scalar(p.sub_gain, p.col("g_sub", 0), 1.0 - LAMBDA_INIT, None, ALU.mult), p.cols_in)
    p.lam_ready = p.dve(lambda e: e.tensor_scalar(p.neg_lam, p.neg_lam, 1.0, -LAMBDA_INIT, ALU.mult, ALU.add), m)


def mod_place(p, n):
    s = n if n < 4 else n - 4
    tile = p.f(Z_AT + NB, NB) if n < 4 else p.f(Z_AT + NB * (s // 3), NB) if s < 6 else p.k(K_MODROWS, NB)
    return tile, 32 * (s % 3), None if n < 3 else [p.mod_gone, p.attention_done]


def load_mod_bias(p, n):
    tile, base, free = mod_place(p, n)
    p.mod_bias_in[n] = p.load(tile[base + 4:base + 5, :], p.dram["b_mod"][n:n + 1, :], free, lane=p.pool)


def mod_row(p, n, acc):
    tile, base, free = mod_place(p, n)
    if n < 4:
        load_mod_bias(p, n)
    for i in range(4):
        pc = p.take("w_mod", n)
        for k, c, at, w in pc.blocks:
            a = p.cs.hi(k, 0)
            p.pe(lambda e, a=a, b=pc.hi[:, at:at + w], s=(k == 0): e.matmul(acc.ap, a, b, start=s, stop=False),
                 pc.split, p.cs.ready, acc.free, mark=False)
            last = (k, c, at, w) == pc.blocks[-1]
            m = p.pe(lambda e, a=a, b=pc.lo[:, at:at + w], z=(k == KD - 1): e.matmul(acc.ap, a, b, start=False, stop=z),
                     mark=last)
        pc.used = m
        p.next_piece += 1
        if i < 3:
            p.feed()
            yield
    acc.free = p.act(lambda e: e.activation(tile[base:base + 4, :], acc.ap[base:base + 4, :], ACT.Copy), m, free)
    p.mod_rows_made[n] = (tile[base:base + 5, :], base, [acc.free, p.mod_bias_in[n]] if n < 4 else [acc.free])
    yield


def mod_features(p, n, out):
    row, base, made = p.mod_rows_made[n]
    sel2 = p.k(K_SEL + 128, 2)[base:base + 5, :]
    for j in range(4):
        m = p.pe(lambda e, j=j: e.matmul(out.ap[:, 2 * j:2 * j + 2], row[:, j * P:(j + 1) * P], sel2,
                                         start=True, stop=True), made, p.sel_in, out.free, mark=j == 3)
    f = p.mod_f[:, 4 * n:4 * n + 4, :]
    o = out.ap[:, 0:8].rearrange("p (k two) -> p k two", two=2)
    out.free = p.mod_f_ready = p.dve(lambda e: e.tensor_copy(f, o), m)
    p.mod_gone = m


def mod_spread(p, n, out, dst, gain=None, after=None):
    row, base, made = p.mod_rows_made[n]
    selb = p.k(K_SEL, P)[base:base + 5, :]
    m = p.pe(lambda e: e.matmul(out.ap, selb, row, start=True, stop=True), made, p.mod_bias_in[n], p.sel_in, out.free)
    if gain is None:
        out.free = p.act(lambda e: e.activation(dst, out.ap, ACT.Copy), m, after)
    else:
        out.free = p.dve(lambda e: e.scalar_tensor_tensor(out=dst, in0=out.ap, scalar=1.0, in1=gain,
                                                          op0=ALU.add, op1=ALU.mult), m, after)
    return out.free


def adaln_coefficients(p, which):
    scale, shift = p.stat(8), p.mod_f[:, 0:8, which]
    m = p.dve(lambda e, s=scale, i=p.mod_f[:, 8:16, which], g=p.k(K_COLS + COL0["norm_attn_g"], 8):
              e.scalar_tensor_tensor(out=s, in0=i, scalar=1.0, in1=g, op0=ALU.add, op1=ALU.mult), p.mod_f_ready)
    return scale, shift, m


def segment_stats(p, bank, m, z, sq, ss, segs, seglen):
    n = segs * seglen
    a = p.act(lambda e: e.activation(z, bank.ap[:, 0:n], ACT.Copy), m)
    b = p.act(lambda e: e.activation(sq[0], bank.ap[:, 0:n], ACT.Square), m, sq[1])
    bank.free = b
    r = p.dve(lambda e: e.tensor_reduce(ss, sq[0].rearrange("p (s c) -> p s c", s=segs), AX.X, ALU.add), b)
    return a, r


def block_one(p):
    B = p.banks
    F = p.f
    xn = F(B_AT, ST, D)
    nrm = p.row_norm(lambda t: p.x[:, t, :], ST, lambda t: xn[:, t, :], lambda t: F(C_AT + t * D, D), p.x_in,
                     meanwhile=[lambda: conditions(p)])
    mod = mod_row(p, 0, B[0])
    next(mod)
    next(mod)
    hT = p.split_view(0, KD, S)
    p.transpose_in(lambda t, k: xn[:, t, k * P:(k + 1) * P], nrm, KD, ST, hT, B[4:8],
                   scale=lambda k: p.col("g_mix", k))
    p.run(mod)
    mod_features(p, 0, B[1])
    attention_scalars(p)
    p.checkpoint("hT", p.R[:, 0:2048].bitcast(F32), p.everyone())

    pool_m = F(G_AT + 2048, 4, ST, S)
    grp_w = F(E_AT, 4, P)
    pm_in = p.load(pool_m, p.dram["pool_m"], lane=p.act)
    gw_in = p.load(grp_w, p.dram["w_grp"], lane=p.act)

    def project(n, bs, between=None):
        return p.run(p.gemm("w_in", n, KD, hT, (0, 1), lambda t, c: bs[t].ap, bs), between)

    U = F(G_AT, ST, NB)
    m = project(0, B[0:2])
    for t in range(ST):
        B[t].free = ev = p.act(lambda e, t=t: e.activation(U[:, t, :], B[t].ap, ACT.Copy), m)
    u_ready = ev

    sqs = [[F(T_AT + 512 * i, NB), None] for i in range(2)]
    ss_q, ss_k, rs_q, rs_k = (p.stat(32) for _ in range(4))
    zq, zk = F(B_AT, ST, D), F(C_AT, ST, D)
    qT, kT = F(D_AT, HEADS, S), None
    norm_marks = {}
    turn, waiting = 0, None
    for what, z, ss, rs, chunks in (("q", zq, ss_q, rs_q, (1, 2)), ("k", zk, ss_k, rs_k, (3, 4))):
        marks = []
        for i, n in enumerate(chunks):
            turn += 1
            bs = B[2 * (turn % 2):2 * (turn % 2) + 2]
            m = project(n, bs, waiting)
            waiting = None
            for t in range(ST):
                s = ss[:, t * 16 + i * 8:t * 16 + i * 8 + 8]
                zz = z[:, t, i * NB:(i + 1) * NB]
                a, r = segment_stats(p, bs[t], m, zz, sqs[t], s, 8, 64)
                sqs[t][1] = r
                marks += [a, r]
            if what == "q" and i == 0:
                pool_mix(p, U, u_ready, pool_m, grp_w, [pm_in, gw_in])
        rm = p.rstd(ss, rs, 64, marks)

        def normalise(what=what, z=z, rs=rs, rm=rm, marks=marks):
            for t in range(ST):
                zt = z[:, t, :].rearrange("p (s c) -> p s c", s=16)
                rb = rs[:, t * 16:t * 16 + 16].unsqueeze(2).to_broadcast([P, 16, 64])
                norm_marks[what, t] = p.dve(lambda e, zt=zt, rb=rb: e.tensor_tensor(zt, zt, rb, ALU.mult), rm, marks)

        waiting = {1: [normalise]}
    qT, kT = F(D_AT, HEADS, S), F(E_AT, HEADS, S)
    v = F(B_AT, ST, D)

    def heads_in(z, marks, dst, g, extra, after=None):
        out = []
        for j in range(0, HEADS, 2):
            b = B[4 + (j // 2) % 4]
            for h in (j, j + 1):
                for t in range(ST):
                    o = b.ap[:, (h - j) * S + t * P:(h - j) * S + (t + 1) * P]
                    m = p.pe(lambda e, o=o, i=z[:, t, h * P:(h + 1) * P]: e.transpose(o, i, p.ident),
                             marks, b.free, mark=(h == j + 1 and t == 1))
            d = dst[:, j:j + 2, :].rearrange("p a b -> p (a b)")
            b.free = r = p.dve(lambda e, d=d, b=b: e.tensor_scalar(d, b.ap, p.col(g, 0), extra, ALU.mult, ALU.mult), m, after)
            out.append(r)
        return out

    mq = heads_in(zq, [norm_marks["q", 0], norm_marks["q", 1]], qT, "g_q", 64 ** -0.5)
    q_moved = p.pe.now()
    mv = []
    m = project(5, B[0:2], waiting)
    for t in range(ST):
        B[t].free = r = p.act(lambda e, t=t: e.activation(v[:, t, 0:NB], B[t].ap, ACT.Copy), m, q_moved)
        mv.append(r)
    mk = heads_in(zk, [norm_marks["k", 0], norm_marks["k", 1]], kT, "g_k", 1.0, p.pool_mixed)
    k_moved = p.pe.now()
    m = project(6, B[2:4])
    for t in range(ST):
        B[2 + t].free = r = p.act(lambda e, t=t: e.activation(v[:, t, NB:D], B[2 + t].ap, ACT.Copy), m)
        mv.append(r)
    p.checkpoint("qT", p.f(D_AT, 2048), [p.everyone()])

    gz = F(G_AT, ST, 2048)
    gb = F(Z_AT, NB)
    bias_line = p.newline("gate_bias")

    def gates():
        bias_used = None
        for n in range(4):
            bs = B[2 * (n % 2):2 * (n % 2) + 2]
            gb_in = p.pool.dma(lambda e, n=n: e.dma_start(gb, p.dram["b_gate"][:, n * NB:(n + 1) * NB]), bias_line, bias_used)
            yield from p.gemm("w_gate", n, KD, hT, (0, 1), lambda t, c: bs[t].ap, bs)
            for t in range(ST):
                bs[t].free = bias_used = p.dve(lambda e, t=t, bs=bs, n=n: e.tensor_tensor(
                    gz[:, t, n * NB:(n + 1) * NB], bs[t].ap, gb, ALU.add), p.last_gemm, gb_in, p.pool_mixed)
                p.gz_ready.append(bias_used)

    p.gz_ready = []
    background = gates()
    st = diff_attention(p, qT, kT, v, [mq, mk, mv, p.attn_consts, p.lam_ready], background, k_moved)
    p.attention_done = p.everyone()

    sig = []
    for t in range(ST):
        for c in range(2):
            g = gz[:, t, c * D:(c + 1) * D]
            sig.append(p.act(lambda e, g=g: e.activation(g, g, ACT.Sigmoid), p.gz_ready))
    turned = []
    m = p.run(p.gemm("w_bp", 0, 4, p.ypT, (0, 1), lambda t, c: B[2 * t + c].ap, B[0:4]),
              {2: [lambda: turned.append(turn_attention(p, st))]})
    yaT = turned[0]
    merged = F(B_AT, ST, D)
    part = F(C_AT, ST, D)
    mm = []
    for t in range(ST):
        for c in range(2):
            B[2 * t + c].free = r = p.dve(lambda e, t=t, c=c: e.tensor_tensor(
                merged[:, t, c * NB:(c + 1) * NB], B[2 * t + c].ap, gz[:, t, c * NB:(c + 1) * NB], ALU.mult), m, sig)
            mm.append(r)
    for n in range(2):
        m = p.run(p.gemm("w_ba", n, 4, yaT, (0, 1), lambda t, c: B[4 + 2 * t + c].ap, B[4:8] if n == 0 else [],
                         k0=4 * n, first=(n == 0), last=(n == 1)))
    ready = []
    for c in range(2):
        for t in range(ST):
            pt = part[:, t, c * NB:(c + 1) * NB]
            mg = merged[:, t, c * NB:(c + 1) * NB]
            B[4 + 2 * t + c].free = r = p.dve(lambda e, t=t, c=c, pt=pt: e.tensor_tensor(
                pt, B[4 + 2 * t + c].ap, gz[:, t, D + c * NB:D + (c + 1) * NB], ALU.mult), m, sig, mm)
            ready.append(p.dve(lambda e, pt=pt, mg=mg: e.tensor_tensor(mg, mg, pt, ALU.add), r))
    p.na_bias_free = ready
    mT = p.split_view(0, KD, S)
    p.run(mod_row(p, 1, B[0]))
    mod = mod_row(p, 2, B[0])
    p.transpose_in(lambda t, k: merged[:, t, k * P:(k + 1) * P], ready, KD, ST, mT, B[1:4])
    p.run(mod)
    for n in (1, 2):
        mod_features(p, n, B[1])
    xs = []
    for n in range(2):
        bs = B[4 + 2 * n:6 + 2 * n]
        m = p.run(p.gemm("w_out", n, KD, mT, (0, 1), lambda t, c: bs[t].ap, bs))
        for t in range(ST):
            xx = p.x[:, t, n * NB:(n + 1) * NB]
            bs[t].free = r = p.dve(lambda e, xx=xx, b=bs[t]: e.tensor_tensor(xx, b.ap, xx, ALU.add), m)
            xs.append(r)
    p.checkpoint("x1", p.f(X_AT, 2048), [p.everyone()])

    xn = F(C_AT, ST, D)
    mod = mod_row(p, 4, B[0])
    nrm = p.row_norm(lambda t: p.x[:, t, :], ST, lambda t: xn[:, t, :], lambda t: F(B_AT + t * D, D), xs, p.pe.now(),
                     meanwhile=[lambda: p.run(mod_row(p, 3, B[0]))])
    h2 = p.split_view(0, KD, S)
    p.transpose_in(lambda t, k: xn[:, t, k * P:(k + 1) * P], nrm, KD, ST, h2, B[1:4], scale=lambda k: p.col("g_ffn", k))
    p.run(mod)
    mod_features(p, 3, B[1])
    for n in range(4, 12):
        load_mod_bias(p, n)
    hid = [F(D_AT + 1024 * i, ST, NB) for i in range(2)]
    hidT = [p.split_view(4096 + 2048 * i, 4, S) for i in range(2)]
    state = {"made": [None] * 2, "hid_free": [None] * 2}

    def up(n, between=None):
        bs = B[4:6]
        m = p.run(p.gemm("w_up", n, KD, h2, (0, 1), lambda t, c: bs[t].ap, bs), between)
        h, out = hid[n % 2], []
        for t in range(ST):
            bs[t].free = a = p.act(lambda e, t=t, h=h: e.activation(h[:, t, :], bs[t].ap, ACT.Relu), m, state["hid_free"][n % 2])
            out.append(p.dve(lambda e, t=t, h=h: e.tensor_tensor(h[:, t, :], h[:, t, :], h[:, t, :], ALU.mult), a))
        state["made"][n % 2] = out

    def turn_in(n):
        h = hid[n % 2]
        ht = hidT[n % 2]
        p.transpose_in(lambda t, k: h[:, t, k * P:(k + 1) * P], state["made"][n % 2], 4, ST, ht, B[6:8])
        state["hid_free"][n % 2] = p.pe.now()

    up(0)
    up(1, {1: [lambda: turn_in(0)]})
    over = p.attention_done
    p.late_consts = [p.load(p.k(K_TRI, ST, S), p.dram["tri"], over), p.load(p.k(K_IOTA, P), p.dram["iota"], over),
                     p.load(p.k(K_ROPE, ST, 2, 16), p.dram["rope"], over),
                     p.load(p.k(K_COLMASK, GRID_W), p.dram["col_mask"], over)]
    xc = F(E_AT, ST, D)
    c_in = p.load(xc, p.dram["ctx"].rearrange("(t q) d -> q t d", q=P), over)
    p.ctx_normed = p.row_norm(lambda t: xc[:, t, :], ST, lambda t: xc[:, t, :], lambda t: F(G_AT + t * D, D), c_in, ready)
    p.hc_parts = []
    scale_c, shift_c, m_c = adaln_coefficients(p, 1)
    hc = F(G_AT, KD, S)

    def turn_context(part):
        b = B[6 + part % 2]
        for k in (2 * part, 2 * part + 1):
            for t in range(ST):
                m = p.pe(lambda e, o=b.ap[:, (k % 2) * S + t * P:(k % 2) * S + (t + 1) * P], i=xc[:, t, k * P:(k + 1) * P]:
                         e.transpose(o, i, p.ident), p.ctx_normed, b.free, mark=(k % 2 == 1 and t == 1))
        for k in (2 * part, 2 * part + 1):
            b.free = r = p.dve(lambda e, k=k: e.tensor_scalar(hc[:, k, :], b.ap[:, (k % 2) * S:(k % 2 + 1) * S], scale_c[:, k:k + 1],
                                                              shift_c[:, k:k + 1], ALU.mult, ALU.add), m, m_c)
        p.hc_parts.append(r)

    def context_hi():
        hi = p.r(4096, KD * S)
        for c in range(2):
            p.hc_hi.append(p.act(lambda e, c=c: e.activation(hi[:, c * D:(c + 1) * D], p.f(G_AT + c * D, D), ACT.Copy),
                                 p.hc_parts, down_before))

    p.hc_hi = []
    for n in range(8):
        turning = {1: [lambda: turn_in(n + 1)]}
        m = p.run(p.gemm("w_down", n, 4, hidT[n % 2], (0, 1), lambda t, c: B[2 * t + c].ap,
                         B[0:4] if n == 0 else [], first=(n == 0), last=(n == 7)),
                  {6: turning, 7: {1: [context_hi]}}.get(n))
        down_before = m
        if n + 2 < 8:
            if n >= 2:
                turning[2] = [lambda: turn_context(n - 2)]
            up(n + 2, turning)
    xs = []
    for t in range(ST):
        for c in range(2):
            xx = p.x[:, t, c * NB:(c + 1) * NB]
            B[2 * t + c].free = r = p.dve(lambda e, xx=xx, b=B[2 * t + c]: e.tensor_tensor(xx, b.ap, xx, ALU.add), m)
            xs.append(r)
    p.x_ready = xs
    p.checkpoint("x2", p.f(X_AT, 2048), [p.everyone()])


def pool_mix(p, U, ready, pool_m, grp_w, ins):
    B = p.banks
    mix = p.f(E_AT + 512, 4, S)
    marks = []
    for g in range(4):
        b = B[4 + g // 2]
        for kt in range(ST):
            m = p.pe(lambda e, g=g, kt=kt, b=b: e.matmul(
                b.ap[:, (g % 2) * S:(g % 2 + 1) * S], U[:, kt, g * P:(g + 1) * P], pool_m[:, g, kt, :],
                start=kt == 0, stop=kt == 1), ready, ins, b.free, mark=(kt == 1 and g % 2 == 1))
        if g % 2 == 1:
            d = mix[:, g - 1:g + 1, :].rearrange("p a b -> p (a b)")
            b.free = r = p.dve(lambda e, d=d, b=b: e.tensor_copy(d, b.ap), m)
            marks.append(r)
    yp = p.split_view(8192, 4, S)
    out = []
    for g in range(4):
        b = B[6 + g // 2]
        o = b.ap[:, (g % 2) * S:(g % 2 + 1) * S]
        m = p.pe(lambda e, g=g, o=o: e.matmul(o, grp_w[:, g, :], mix[:, g, :], start=True, stop=True),
                 marks, ins, b.free, mark=g % 2 == 1)
        if g % 2 == 1:
            hs = []
            for q in (g - 1, g):
                oo = b.ap[:, (q % 2) * S:(q % 2 + 1) * S]
                hs.append(p.act(lambda e, q=q, oo=oo: e.activation(yp.hi_span(q, 1), oo, ACT.Copy, scale=p.col("pool_scale", q)), m))
            for q in (g - 1, g):
                oo = b.ap[:, (q % 2) * S:(q % 2 + 1) * S]
                r = p.dve(lambda e, q=q, oo=oo: e.scalar_tensor_tensor(
                    out=yp.lo_span(q, 1), in0=oo, scalar=p.col("pool_scale", q), in1=yp.hi_span(q, 1).bitcast(F32),
                    op0=ALU.mult, op1=ALU.subtract), m, hs)
            b.free = r
            out += [hs, r]
    yp.ready = out
    p.ypT = yp
    p.pool_mixed = [p.pe.now(), out]


def diff_attention(p, qT, kT, v, ready, background, k_moved):
    B = p.banks
    dist, slopes = p.dist, p.slopes
    prob = [p.f(T_AT + 512 * i, 2, S) for i in range(3)]
    prob_free = [None] * 3
    aT = [p.f(T_AT + 1536 + 256 * i, ST, P) for i in range(2)]
    aT_free = [None] * 2
    Oh = p.f(M_AT, 2, NB)
    units = [(t, h) for t in range(ST) for h in range(HEADS)]
    st = {}
    neg_max, sums, inv = p.stat(32), p.stat(32), p.stat(32)
    ssq, rs = p.stat(16), p.stat(16)

    def scores(u):
        t, h = units[u]
        nk = (t + 1) * P
        for i in range(2):
            o = B[4 + i].ap[:, 0:nk]
            p.pe(lambda e, o=o, i=i: e.matmul(o, qT[64 * i:64 * i + 64, h, t * P:(t + 1) * P], kT[64 * i:64 * i + 64, h, 0:nk],
                                              start=True, stop=False), ready, B[4].free, B[5].free, mark=False)
            m = p.pe(lambda e, o=o: e.matmul(o, slopes[:, h, :], dist[:, t, 0:nk], start=False, stop=True), mark=i == 1)
        nm, rs_, iv = (s[:, 2 * u:2 * u + 2] for s in (neg_max, sums, inv))
        both = p.ps[:, 4:6, 0:nk]
        r = p.dve(lambda e: e.tensor_reduce(nm, both, AX.X, ALU.max, negate=True), m)
        w = prob[u % 3]
        ex = []
        for i in range(2):
            ex.append(p.act(lambda e, i=i: e.activation(w[:, i, 0:nk], B[4 + i].ap[:, 0:nk], ACT.Exp, bias=nm[:, i:i + 1],
                                                        accum_out=rs_[:, i:i + 1]), r, prob_free[u % 3]))
        B[4].free = B[5].free = ex
        m = p.dve(lambda e: e.reciprocal(iv, rs_), ex)
        m = p.dve(lambda e: e.tensor_tensor(iv[:, 1:2], iv[:, 1:2], p.neg_lam, ALU.mult), m)
        m2 = p.dve(lambda e: e.tensor_scalar(w[:, 0, 0:nk], w[:, 0, 0:nk], iv[:, 0:1], None, ALU.mult), m, ex)
        st[u] = p.dve(lambda e: e.scalar_tensor_tensor(out=w[:, 0, 0:nk], in0=w[:, 1, 0:nk], scalar=iv[:, 1:2],
                                                       in1=w[:, 0, 0:nk], op0=ALU.mult, op1=ALU.add), m, m2)

    def weigh(u):
        t, h = units[u]
        w, a, b = prob[u % 3], aT[u % 2], B[6]
        for kt in range(t + 1):
            m = p.pe(lambda e, kt=kt: e.transpose(b.ap[:, kt * P:(kt + 1) * P], w[:, 0, kt * P:(kt + 1) * P], p.ident),
                     st[u], b.free, mark=kt == t)
        prob_free[u % 3] = m
        b.free = ev = p.act(lambda e: e.activation(a[:, 0:t + 1, :].rearrange("p a b -> p (a b)"), b.ap[:, 0:(t + 1) * P], ACT.Copy),
                            m, aT_free[u % 2])
        ob = B[7]
        for kt in range(t + 1):
            m = p.pe(lambda e, kt=kt: e.matmul(ob.ap[:, (h % 4) * P:(h % 4 + 1) * P], a[:, kt, :], v[:, kt, h * P:(h + 1) * P],
                                               start=kt == 0, stop=kt == t), ev, ob.free, mark=kt == t)
        aT_free[u % 2] = m
        if h % 4 == 3:
            q = t * 2 + h // 4
            s = ssq[:, 4 * q:4 * q + 4]
            z = p.o_all[:, t, (h // 4) * NB:(h // 4 + 1) * NB]
            a2 = p.act(lambda e: e.activation(z, ob.ap, ACT.Copy), m, p.o_free)
            sq = Oh[:, q % 2, :]
            b2 = p.act(lambda e: e.activation(sq, ob.ap, ACT.Square), m, st.get(("sq", q - 2)))
            ob.free = b2
            r = p.dve(lambda e: e.tensor_reduce(s, sq.rearrange("p (s c) -> p s c", s=4), AX.X, ALU.add), b2)
            st["sq", q] = r
            rm = p.rstd(s, rs[:, 4 * q:4 * q + 4], P, r)
            zz = z.rearrange("p (s c) -> p s c", s=4)
            rb = rs[:, 4 * q:4 * q + 4].unsqueeze(2).to_broadcast([P, 4, P])
            late.append(lambda: st.__setitem__(("o", q), p.dve(lambda e: e.tensor_tensor(zz, zz, rb, ALU.mult), rm, a2)))

    late = []
    p.o_all = p.f(C_AT, ST, D)
    p.o_free = k_moved
    for u in range(len(units) + 2):
        if u < len(units):
            scores(u)
        next(background, None)
        ready_now, late = late, []
        if u >= 2:
            weigh(u - 2)
        for step in ready_now:
            step()
    for _ in background:
        pass
    for step in late:
        step()
    return st


def turn_attention(p, st):
    B = p.banks
    yaT = p.split_view(4096, KD, S)
    p.transpose_in(lambda t, k: p.o_all[:, t, k * P:(k + 1) * P], [[st["o", q] for q in range(4)], p.sub_ready], KD, ST, yaT,
                   [B[4], B[5], B[6]], scale=lambda k: p.sub_gain)
    return yaT


def block_two(p):
    B, F, K = p.banks, p.f, p.k
    x = p.x
    ax, bx, m_x = adaln_coefficients(p, 0)
    tmp = lambda k: F(T_AT + S * (k % 4), S)
    hcT = p.split_view(4096, KD, S)
    xn = F(B_AT, ST, D)
    mod = mod_row(p, 7, B[4])
    nrm = p.row_norm(lambda t: x[:, t, :], ST, lambda t: xn[:, t, :], lambda t: F(G_AT + 2048 + t * D, D), p.x_ready,
                     meanwhile=[lambda: p.run(mod_row(p, 5, B[4])), lambda: p.run(mod_row(p, 6, B[4]))])
    hc_lo = [p.dve(lambda e, c=c: e.tensor_tensor(hcT.lo_span(4 * c, 4), F(G_AT + c * D, D), hcT.hi_span(4 * c, 4).bitcast(F32),
                                                  ALU.subtract), p.hc_parts, p.hc_hi[c], p.pe.now()) for c in range(2)]
    hcT.ready = [p.hc_hi, hc_lo]
    hxT = p.split_view(0, KD, S)
    p.transpose_in(lambda t, k: xn[:, t, k * P:(k + 1) * P], [nrm, m_x], KD, ST, hxT, B[5:8],
                   scale=lambda k: ax[:, k:k + 1], bias=lambda k: bx[:, k:k + 1], tmp=tmp)
    p.run(mod)
    both = Split(lambda k, t: hxT.hi(k, t) if t < ST else hcT.hi(k, t - ST),
                 lambda k, t: hxT.lo(k, t) if t < ST else hcT.lo(k, t - ST))
    both.ready = [hxT.ready, hcT.ready]

    ALL = tuple(range(TT))
    kvl = F(C_AT, TT, KV_LORA + ROPE)
    m = p.run(p.gemm("w_in2kv", 0, KD, both, ALL, lambda t, c: B[t].ap[:, 0:KV_LORA + ROPE], B[0:4]))
    ss_kv, rs_kv = p.stat(TT), p.stat(TT)
    moved, sq = [], []
    for t in ALL:
        a = p.act(lambda e, t=t: e.activation(kvl[:, t, :], B[t].ap[:, 0:KV_LORA + ROPE], ACT.Copy), m)
        B[t].free = b = p.act(lambda e, t=t: e.activation(F(T_AT + 1024 + 256 * (t % 2), KV_LORA), B[t].ap[:, 0:KV_LORA],
                                                          ACT.Square, accum_out=ss_kv[:, t:t + 1]), m, sq[-2:-1])
        moved.append(a)
        sq.append(b)
    rm = p.rstd(ss_kv, rs_kv, KV_LORA, sq)
    kvn = [p.dve(lambda e, t=t: e.tensor_scalar(kvl[:, t, 0:KV_LORA], kvl[:, t, 0:KV_LORA], rs_kv[:, t:t + 1], None, ALU.mult),
                 rm, moved) for t in ALL]

    nk, nkT, nv = F(D_AT, TT, NB), F(E_AT, 4, TT * P), F(G_AT, TT, NB)
    m = p.run(p.gemm("w_in2k", 0, KD, both, ALL, lambda t, c: B[4 + t].ap, B[4:8]))
    nk_in = []
    for t in ALL:
        B[4 + t].free = r = p.act(lambda e, t=t: e.activation(nk[:, t, :], B[4 + t].ap, ACT.Copy), m)
        nk_in.append(r)
    m = p.run(p.gemm("w_in2v", 0, KD, both, ALL, lambda t, c: B[t].ap, B[0:4]))
    nv_in = []
    for t in ALL:
        B[t].free = r = p.act(lambda e, t=t: e.activation(nv[:, t, :], B[t].ap, ACT.Copy), m)
        nv_in.append(r)

    def turn(src, ready, dst, banks, tiles, rows=P):
        b = banks
        for t in range(tiles):
            m = p.pe(lambda e, o=b.ap[0:rows, t * P:(t + 1) * P], i=src(t): e.transpose(o, i, p.ident), ready, b.free,
                     mark=t == tiles - 1)
        b.free = r = p.act(lambda e, o=dst, i=b.ap[0:rows, 0:tiles * P]: e.activation(o, i, ACT.Copy), m)
        return r

    nkT_in = [turn(lambda t, j=j: nk[:, t, j * P:(j + 1) * P], nk_in, nkT[:, j, :], B[4 + j], TT) for j in range(4)]
    kvT = p.split_view(9728, 2, TT * P)
    p.transpose_in(lambda t, k: kvl[:, t, k * P:(k + 1) * P], kvn, 2, TT, kvT, B[4:6], scale=lambda k: p.col("kv_a_g", k))

    zql = F(B_AT, ST, Q_LORA)
    m = p.run(p.gemm("w_in2q", 0, KD, hxT, (0, 1), lambda t, c: B[t].ap[:, 0:Q_LORA], B[0:2]))
    ss_q, rs_q = p.stat(ST), p.stat(ST)
    moved, sq = [], []
    for t in range(ST):
        moved.append(p.act(lambda e, t=t: e.activation(zql[:, t, :], B[t].ap[:, 0:Q_LORA], ACT.Copy), m))
        B[t].free = b = p.act(lambda e, t=t: e.activation(F(T_AT + 1024 + 512 * (t % 2), Q_LORA), B[t].ap[:, 0:Q_LORA],
                                                                 ACT.Square, accum_out=ss_q[:, t:t + 1]), m)
        sq.append(b)
    rm = p.rstd(ss_q, rs_q, Q_LORA, sq)
    qn = [p.dve(lambda e, t=t: e.tensor_scalar(zql[:, t, :], zql[:, t, :], rs_q[:, t:t + 1], None, ALU.mult), rm, moved)
          for t in range(ST)]
    nq, nqT = F(B_AT + 768, ST, NB), F(G_AT + 2048, 4, S)
    m = p.run(p.gemm("w_in2nq", 0, KD, hxT, (0, 1), lambda t, c: B[2 + t].ap, B[2:4]))
    nq_in = []
    for t in range(ST):
        B[2 + t].free = r = p.act(lambda e, t=t: e.activation(nq[:, t, :], B[2 + t].ap, ACT.Copy, scale=64 ** -0.5), m)
        nq_in.append(r)
    nqT_in = [turn(lambda t, j=j: nq[:, t, j * P:(j + 1) * P], nq_in, nqT[:, j, :], B[4 + j], ST) for j in range(4)]
    qlT = p.split_view(8192, 3, S)
    p.transpose_in(lambda t, k: zql[:, t, k * P:(k + 1) * P], qn, 3, ST, qlT, B[0:2], scale=lambda k: p.col("q_a_g", k))

    rope = K(K_ROPE, ST, 2, 16)

    def rotate(z, shape, tables, scratch, ready):
        x1, x2, c, s = z[0], z[1], tables[0], tables[1]
        if shape is not None:
            c, s = (v.unsqueeze(1).to_broadcast(shape) for v in (c, s))
        a, b, c2, d2 = scratch
        ms = [p.dve(lambda e, o=o, i=i, j=j: e.tensor_tensor(o, i, j, ALU.mult), ready, p.late_consts)
              for o, i, j in ((a, x1, c), (b, x2, s), (c2, x1, s), (d2, x2, c))]
        return [p.dve(lambda e: e.tensor_tensor(x1, a, b, ALU.subtract), ms),
                p.dve(lambda e: e.tensor_tensor(x2, c2, d2, ALU.add), ms)]

    kr_ready = []
    for t in range(ST):
        kr = kvl[:, t, KV_LORA:KV_LORA + ROPE]
        sc = [F(T_AT + 64 * t + 16 * i, 16) for i in range(4)]
        kr_ready += rotate((kr[:, 0:16], kr[:, 16:32]), None, (rope[:, t, 0, :], rope[:, t, 1, :]), sc,
                           [moved, p.everyone()] if t == 0 else [])

    mixed = F(B_AT, ST, D)
    bias = [F(G_AT + 3072 + 512 * i, ST, S) for i in range(2)]
    bias_lines = [p.newline(f"window_bias_{i}") for i in range(2)]
    bias_used = [p.na_bias_free, p.na_bias_free]
    col_mask = K(K_COLMASK, GRID_W)
    bias_ready = {}

    def window_bias(h):
        b = bias[h % 2]
        m = p.pool.dma(lambda e, b=b: e.dma_start(b, p.dram["rel_rows"][h]), bias_lines[h % 2], bias_used[h % 2])
        v = b.rearrange("p t (j c) -> p (t j) c", c=GRID_W)
        mask = col_mask.unsqueeze(1).to_broadcast([P, 8, GRID_W])
        bias_ready[h] = p.pool(lambda e, v=v, mask=mask: e.tensor_tensor(v, v, mask, ALU.add), m, p.late_consts)

    def na_scores(h, t, b, after):
        lo = 64 * (h % 2)
        p.pe(lambda e: e.matmul(b.ap, nqT[lo:lo + 64, h // 2, t * P:(t + 1) * P], nkT[lo:lo + 64, h // 2, :],
                                start=True, stop=False), nqT_in, nkT_in, after, mark=False)
        m = p.pe(lambda e: e.matmul(b.ap[:, 0:S], p.ident, bias[h % 2][:, t, :], start=False, stop=True), bias_ready[h])
        if t == ST - 1:
            bias_used[h % 2] = m
            if h + 2 < HEADS:
                window_bias(h + 2)
        return m

    window_bias(0)
    window_bias(1)
    nq_gone = p.pe.now()
    na_done = attend(p, na_scores, 1.0, lambda h, kt: nv[:, kt, h * 64:(h + 1) * 64], nv_in, mixed, 512,
                     iter(()), [nq_gone])

    qm = F(T_AT, ST, HEADS * QK)
    m = p.run(p.gemm("w_uq", 0, 3, qlT, (0, 1), lambda t, c: B[2 * t + c].ap[:, 0:4 * QK], B[0:4]))
    qm_in = []
    for t in range(ST):
        for c in range(2):
            B[2 * t + c].free = r = p.act(lambda e, t=t, c=c: e.activation(
                qm[:, t, c * 4 * QK:(c + 1) * 4 * QK], B[2 * t + c].ap[:, 0:4 * QK], ACT.Copy), m, na_done)
            qm_in.append(r)
    qh = qm.rearrange("p t (h d) -> p t h d", h=HEADS)
    q_ready = []
    for t in range(ST):
        sc = [F(M_AT + 512 * t + 128 * i, HEADS, 16) for i in range(4)]
        q_ready += rotate((qh[:, t, :, NOPE:NOPE + 16], qh[:, t, :, NOPE + 16:QK]), [P, HEADS, 16],
                          (rope[:, t, 0, :], rope[:, t, 1, :]), sc, qm_in)
    vm = F(E_AT, TT, NB)
    kT = F(G_AT, HEADS, TT * P)
    qT = F(D_AT, HEADS, S)
    kt_in, vm_in = [], []
    qT_in = []
    for j in range(0, HEADS, 2):
        b = B[4 + (j // 2) % 2]
        for h in (j, j + 1):
            for t in range(ST):
                m = p.pe(lambda e, o=b.ap[0:QK, (h - j) * S + t * P:(h - j) * S + (t + 1) * P], i=qh[:, t, h, :]:
                         e.transpose(o, i, p.ident), q_ready, b.free, mark=(h == j + 1 and t == 1))
        b.free = r = p.act(lambda e, o=qT[0:QK, j:j + 2, :].rearrange("p a b -> p (a b)"), i=b.ap[0:QK, :]:
                           e.activation(o, i, ACT.Copy), m)
        qT_in.append(r)
    q_gone = p.pe.now()
    kfull = [F(T_AT + 4 * QK * i, 4, QK) for i in range(4)]
    kfree = [None] * 4
    for n in range(2):
        bs = B[0:4]
        m = p.run(p.gemm("w_ukv", n, 2, kvT, ALL, lambda t, c: bs[t].ap, bs))
        for t in ALL:
            src = bs[t].ap.rearrange("p (h d) -> p h d", h=4)
            kd = kfull[t]
            a = p.act(lambda e, o=kd[:, :, 0:NOPE], i=src[:, :, 0:NOPE]: e.activation(o, i, ACT.Copy), m, q_gone, kfree[t])
            vd = vm[:, t, n * 256:(n + 1) * 256].rearrange("p (h d) -> p h d", h=4)
            bs[t].free = r = p.act(lambda e, o=vd, i=src[:, :, NOPE:P]: e.activation(o, i, ACT.Copy), m)
            vm_in.append(r)
            kr = kvl[:, t, KV_LORA:KV_LORA + ROPE].unsqueeze(1).to_broadcast([P, 4, ROPE])
            c = p.dve(lambda e, o=kd[:, :, NOPE:QK], i=kr: e.tensor_copy(o, i), kr_ready, kfree[t], q_gone)
            b = B[4 + t % 2]
            for h in range(4):
                mt = p.pe(lambda e, o=b.ap[0:QK, h * P:(h + 1) * P], i=kd[:, h, :]: e.transpose(o, i, p.ident),
                          a, c, b.free, mark=h == 3)
            kfree[t] = mt
            o = kT[0:QK, 4 * n:4 * n + 4, t * P:(t + 1) * P]
            b.free = r2 = p.dve(lambda e, o=o, i=b.ap[0:QK, :].rearrange("p (h q) -> p h q", h=4): e.tensor_copy(o, i), mt)
            kt_in.append(r2)

    def mla_scores(h, t, b, after):
        return p.pe(lambda e: e.matmul(b.ap, qT[0:QK, h, t * P:(t + 1) * P], kT[0:QK, h, :], start=True, stop=True),
                    qT_in, kt_in, after)

    g1 = F(M_AT, D)
    def mods():
        for n in (8, 9):
            yield from mod_row(p, n, B[4])
            g1_ready.append(mod_spread(p, n - 4, B[5], g1[:, (n - 8) * NB:(n - 7) * NB], after=q_ready))
    g1_ready = []
    bg = mods()
    mla_done = attend(p, mla_scores, float(QK) ** -0.5, lambda h, kt: vm[:, kt, h * 64:(h + 1) * 64], vm_in, mixed, 0,
                      bg, [kfree])
    for _ in bg:
        pass
    p.checkpoint("mixed", p.f(B_AT, 2048), p.everyone())

    mT = p.split_view(0, KD, S)
    p.transpose_in(lambda t, k: mixed[:, t, k * P:(k + 1) * P], [na_done, mla_done], KD, ST, mT, B[0:4])
    shift2, scale2, gain2, g2 = (F(G_AT + D * i, D) for i in range(4))
    gain_in = p.load(gain2, p.dram["norm_ffn_g"], mla_done, lane=p.pool)
    xs = []
    for n in range(2):
        bs = B[4 + 2 * n:6 + 2 * n]
        m = p.run(p.gemm("w_out2", n, KD, mT, (0, 1), lambda t, c: bs[t].ap, bs))
        for t in range(ST):
            tp = F(T_AT + NB * t, NB)
            xx = x[:, t, n * NB:(n + 1) * NB]
            bs[t].free = r = p.dve(lambda e, b=bs[t], tp=tp, g=g1[:, n * NB:(n + 1) * NB]: e.tensor_tensor(tp, b.ap, g, ALU.mult),
                                   m, g1_ready)
            xs.append(p.dve(lambda e, tp=tp, xx=xx: e.tensor_tensor(xx, xx, tp, ALU.add), r))
    mixT_gone = p.pe.now()
    p.checkpoint("x3", p.f(X_AT, 2048), p.everyone())

    h = F(B_AT, ST, D)
    sh_ready, sc_ready = [], []
    mod = mod_row(p, 10, B[0])

    def spread():
        for n in (6, 7):
            sh_ready.append(mod_spread(p, n, B[n - 5], shift2[:, (n - 6) * NB:(n - 5) * NB], after=mla_done))
        for n in (8, 9):
            sc_ready.append(mod_spread(p, n, B[n - 7], scale2[:, (n - 8) * NB:(n - 7) * NB],
                                       gain=gain2[:, (n - 8) * NB:(n - 7) * NB], after=[mla_done, gain_in]))

    nrm = p.row_norm(lambda t: x[:, t, :], ST, lambda t: h[:, t, :], lambda t: F(C_AT + t * D, D), xs, mixT_gone,
                     meanwhile=[lambda: next(mod), spread])
    hs = []
    for t in range(ST):
        a = p.dve(lambda e, t=t: e.tensor_tensor(h[:, t, :], h[:, t, :], scale2, ALU.mult), nrm, sc_ready)
        hs.append(p.dve(lambda e, t=t: e.tensor_tensor(h[:, t, :], h[:, t, :], shift2, ALU.add), a, sh_ready))
    p.checkpoint("hx2", p.f(B_AT, 2048), p.everyone())
    p.run(mod)
    g2_ready = []

    def last_mod():
        yield from mod_row(p, 11, B[2])
        for n in (10, 11):
            g2_ready.append(mod_spread(p, n, B[n - 10], g2[:, (n - 10) * NB:(n - 9) * NB], after=mla_done))
        p.cs_gone = p.pe.now()

    moe(p, h, hs, last_mod(), mixT_gone)
    y, fin = F(T_AT, ST, D), F(D_AT, ST, D)
    gain = F(G_AT, D)
    fg_in = p.load(gain, p.dram["final_g"], hs, lane=p.pool)
    ys = []
    for t in range(ST):
        for c in range(2):
            a = p.dve(lambda e, t=t, c=c, b=p.y_banks[2 * t + c][2]: e.tensor_tensor(
                y[:, t, c * NB:(c + 1) * NB], b.ap, g2[:, c * NB:(c + 1) * NB], ALU.mult), p.y_ready, g2_ready)
        ys.append(p.dve(lambda e, t=t: e.tensor_tensor(y[:, t, :], y[:, t, :], x[:, t, :], ALU.add), a))
    nrm = p.row_norm(lambda t: y[:, t, :], ST, lambda t: fin[:, t, :], lambda t: F(G_AT + (1 + t) * D, D), ys, p.everyone())
    outs = [p.dve(lambda e, t=t: e.tensor_tensor(fin[:, t, :], fin[:, t, :], gain, ALU.mult), nrm, fg_in) for t in range(ST)]
    dst = p.nc.dram_tensor("out", [S, D], F32, kind="ExternalOutput").ap().rearrange("(t q) d -> q t d", q=P)
    for t in range(ST):
        p.load(dst[:, t, :], fin[:, t, :], outs[t], lane=p.sp if t else p.act)
    p.sp.ops.append((p.sp.needed([(l.sem, l.count) for l in p.lines if l.count]), lambda e: e.nop(), None, 0))


def attend(p, scores, scale, values, v_ready, out, col0, background, free):
    B = p.banks
    prob = [p.f(T_AT + 512 * i, NB) for i in range(2)]
    probT = [p.f(T_AT + 1024 + 512 * i, TT, P) for i in range(2)]
    units = [(h, t) for h in range(HEADS) for t in range(ST)]
    peak, neg, sums, inv = p.stat(16), p.stat(16), p.stat(16), p.stat(16)
    prob_free, probT_free, made = [free, free], [free, free], {}
    turned = {}
    acc = B[6:8]

    def first(u):
        h, t = units[u]
        b = B[u % 2]
        at = t * HEADS + h
        m = scores(h, t, b, b.free)
        pk, ng, sm = peak[:, at:at + 1], neg[:, at:at + 1], sums[:, at:at + 1]
        m = p.dve(lambda e: e.tensor_reduce(pk, b.ap, AX.X, ALU.max), m)
        m = p.dve(lambda e: e.tensor_scalar(ng, pk, -scale, None, ALU.mult), m)
        b.free = made[u] = p.act(lambda e, w=prob[u % 2]: e.activation(w, b.ap, ACT.Exp, bias=ng, scale=scale, accum_out=sm),
                                 m, prob_free[u % 2])

    def second(u):
        b, w = B[2 + u % 2], prob[u % 2]
        for kt in range(TT):
            m = p.pe(lambda e, kt=kt: e.transpose(b.ap[:, kt * P:(kt + 1) * P], w[:, kt * P:(kt + 1) * P], p.ident),
                     made[u], b.free, mark=kt == TT - 1)
        prob_free[u % 2] = m
        dst = probT[u % 2].rearrange("p a b -> p (a b)")
        if u % 4 < 3:
            r = p.act(lambda e: e.activation(dst, b.ap, ACT.Copy), m, probT_free[u % 2])
        else:
            r = p.dve(lambda e: e.tensor_copy(dst, b.ap), m, probT_free[u % 2])
        b.free = turned[u] = r

    def third(u):
        h, t = units[u]
        w = probT[u % 2]
        for kt in range(TT):
            m = p.pe(lambda e, kt=kt: e.matmul(acc[t].ap[:, h * 64:(h + 1) * 64], w[:, kt, :], values(h, kt),
                                               start=kt == 0, stop=kt == TT - 1),
                     turned[u], v_ready, acc[t].free, mark=kt == TT - 1)
        probT_free[u % 2] = m
        return m

    for u in range(len(units) + 2):
        if u < len(units):
            first(u)
        next(background, None)
        if 1 <= u <= len(units):
            second(u - 1)
        if u >= 2:
            m = third(u - 2)
    done = []
    r = p.dve(lambda e: e.reciprocal(inv, sums), made[len(units) - 1])
    for t in range(ST):
        o = out[:, t, col0:col0 + NB].rearrange("p (h d) -> p h d", h=HEADS)
        iv = inv[:, t * HEADS:(t + 1) * HEADS].unsqueeze(2).to_broadcast([P, HEADS, 64])
        acc[t].free = r2 = p.dve(lambda e, o=o, iv=iv, i=acc[t].ap.rearrange("p (h d) -> p h d", h=HEADS):
                                 e.tensor_tensor(o, i, iv, ALU.mult), m, r)
        done.append(r2)
    return done


def moe(p, h, h_ready, fill, gone):
    B, F, K = p.banks, p.f, p.k
    H_hi, H_lo = p.r(0, ST, D), p.r(2048, ST, D)
    hT = p.split_view(4096, KD, S)
    p.transpose_in(lambda t, k: h[:, t, k * P:(k + 1) * P], h_ready, KD, ST, hT, B[4:8])
    Hm = []
    for t in range(ST):
        a = p.act(lambda e, t=t: e.activation(H_hi[:, t, :], h[:, t, :], ACT.Copy), h_ready, gone)
        Hm.append(p.dve(lambda e, t=t: e.tensor_tensor(H_lo[:, t, :], h[:, t, :], H_hi[:, t, :].bitcast(F32), ALU.subtract),
                        h_ready, a))
    wr = F(E_AT, KD, 20)
    wr_hi, wr_lo = p.r(10240, KD, 20), p.r(10400, KD, 20)
    wr_in = p.load(wr, p.dram["w_router"], p.attention_done, lane=p.pool)
    br = F(E_AT + 160, 20)
    br_in = p.load(br, p.dram["b_router"], p.attention_done, lane=p.pool)
    a = p.dve(lambda e: e.tensor_copy(wr_hi, wr), wr_in)
    wm = p.dve(lambda e: e.tensor_tensor(wr_lo, wr, wr_hi.bitcast(F32), ALU.subtract), a)
    lg = F(E_AT + 192, ST, 20)
    b = B[3]
    for k in range(KD):
        for i, (l, r) in enumerate(((wr_hi, hT.hi_span(k, 1)), (wr_lo, hT.hi_span(k, 1)), (wr_hi, hT.lo_span(k, 1)))):
            m = p.pe(lambda e, l=l[:, k, :], r=r, s=(k == 0 and i == 0), z=(k == KD - 1 and i == 2):
                     e.matmul(b.ap[0:20, 0:S], l, r, start=s, stop=z), hT.ready, wm, b.free, mark=(k == KD - 1 and i == 2))
    lgT = F(E_AT + 1024, S)
    m = p.dve(lambda e: e.tensor_copy(lgT[0:20, :], b.ap[0:20, 0:S]), m)
    for t in range(ST):
        m = p.pe(lambda e, t=t, m=m: e.transpose(b.ap[:, t * 32:t * 32 + 20], lgT[0:20, t * P:(t + 1) * P], p.ident[0:20, 0:20]),
                 m, mark=t == 1) or m
    bb = br.unsqueeze(1).to_broadcast([P, ST, 20])
    b.free = m = p.dve(lambda e: e.tensor_tensor(lg, b.ap[:, 0:64].rearrange("p (t c) -> p t c", t=ST)[:, :, 0:20], bb, ALU.add), m, br_in)
    p.feed()
    p.hold = True
    for _ in fill:
        pass
    router_gone = p.pe.now()

    at = [E_AT + 256]

    def small(*dims):
        v = F(at[0], *dims)
        at[0] += int(np.prod(dims))
        return v

    def d(fn, *after):
        return p.dve(fn, *after)

    wide = lambda v: v.unsqueeze(2).to_broadcast([P, ST, 4])

    def peak_of(v, m):
        top, eq, cum, first = small(ST), small(ST, 4), small(ST, 5), small(ST, 4)
        m1 = d(lambda e: e.tensor_reduce(top, v, AX.X, ALU.max), m)
        z = d(lambda e: e.memset(cum, 0.0))
        m2 = d(lambda e: e.tensor_tensor(eq, v, wide(top), ALU.is_equal), m1)
        for i in range(4):
            m2 = d(lambda e, i=i: e.tensor_tensor(cum[:, :, i + 1], cum[:, :, i], eq[:, :, i], ALU.max), m2, z)
        return top, first, d(lambda e: e.tensor_tensor(first, cum[:, :, 1:5], cum[:, :, 0:4], ALU.subtract), m2)

    gl = lg[:, :, 0:4]
    gtop, gsel, m1 = peak_of(gl, m)
    diff, ex, gs, gw = small(ST, 4), small(ST, 4), small(ST), small(ST)
    m2 = d(lambda e: e.tensor_tensor(diff, gl, wide(gtop), ALU.subtract), m1)
    m2 = p.act(lambda e: e.activation(ex, diff, ACT.Exp), m2)
    m2 = d(lambda e: e.tensor_reduce(gs, ex, AX.X, ALU.add), m2)
    m2 = d(lambda e: e.reciprocal(gw, gs), m2)
    el = lg[:, :, 4:20].rearrange("p t (g e) -> p t g e", g=4)
    prod, es = small(ST, 4, 4), small(ST, 4)
    gb = gsel.unsqueeze(3).to_broadcast([P, ST, 4, 4])
    m3 = d(lambda e: e.tensor_tensor(prod, el, gb, ALU.mult), m1)
    m3 = d(lambda e: e.tensor_reduce(es, prod.rearrange("p t g e -> p t e g"), AX.X, ALU.add), m3)
    etop, _, m3 = peak_of(es, m3)
    ediff, ee = small(ST, 4), small(ST, 4)
    m3 = d(lambda e: e.tensor_tensor(ediff, es, wide(etop), ALU.subtract), m3)
    m3 = p.act(lambda e: e.activation(ee, ediff, ACT.Exp), m3)
    p1, f1, m4 = peak_of(ee, m3)
    rest = small(ST, 4)
    m4 = d(lambda e: e.scalar_tensor_tensor(out=rest, in0=f1, scalar=-2.0, in1=ee, op0=ALU.mult, op1=ALU.add), m4)
    p2, f2, m5 = peak_of(rest, m4)
    tot, inv, wgt, wi, sel2 = small(ST), small(ST), small(ST), small(ST, 4), small(ST, 4)
    m6 = d(lambda e: e.tensor_tensor(tot, p1, p2, ALU.add), m5)
    m6 = d(lambda e: e.reciprocal(inv, tot), m6)
    m6 = d(lambda e: e.tensor_tensor(wgt, inv, gw, ALU.mult), m6, m2)
    m7 = d(lambda e: e.tensor_tensor(wi, f2, wide(p2), ALU.mult), m5)
    a1 = small(ST, 4)
    m7b = d(lambda e: e.tensor_tensor(a1, f1, wide(p1), ALU.mult), m5)
    m7 = d(lambda e: e.tensor_tensor(wi, wi, a1, ALU.add), m7, m7b)
    m7 = d(lambda e: e.tensor_tensor(wi, wi, wide(wgt), ALU.mult), m7, m6)
    m8 = d(lambda e: e.tensor_tensor(sel2, f1, f2, ALU.add), m5)
    comb, chosen = small(ST, N_EXPERTS), small(ST, N_EXPERTS)
    c4, s4 = (v.rearrange("p t (g e) -> p t g e", g=4) for v in (comb, chosen))
    wb = wi.unsqueeze(2).to_broadcast([P, ST, 4, 4])
    sb2 = sel2.unsqueeze(2).to_broadcast([P, ST, 4, 4])
    comb_ready = d(lambda e: e.tensor_tensor(c4, gb, wb, ALU.mult), m7, m1)
    m8 = d(lambda e: e.tensor_tensor(s4, gb, sb2, ALU.mult), m8, m1)
    tri = K(K_TRI, ST, S)
    for t in range(ST):
        for kt in range(ST):
            m = p.pe(lambda e, t=t, kt=kt: e.matmul(b.ap[:, 64 + t * 16:80 + t * 16], tri[:, kt, t * P:(t + 1) * P], chosen[:, kt, :],
                                                    start=kt == 0, stop=kt == 1), m8, p.late_consts, b.free,
                     mark=(t == 1 and kt == 1))
    slot = small(ST, N_EXPERTS)
    b.free = m = d(lambda e: e.scalar_tensor_tensor(out=slot, in0=b.ap[:, 64:96].rearrange("p (t c) -> p t c", t=ST), scalar=1.0,
                                                    in1=chosen, op0=ALU.add, op1=ALU.mult), m, m8)
    slot_ready = d(lambda e: e.tensor_scalar(slot, slot, -1.0, None, ALU.add), m)
    ones = K(K_ONES, P)
    one = d(lambda e: e.memset(ones, 1.0), p.attention_done)
    for kt in range(ST):
        m = p.pe(lambda e, kt=kt: e.matmul(b.ap[:, 128:128 + N_EXPERTS], ones, chosen[:, kt, :], start=kt == 0, stop=kt == 1),
                 m8, one, b.free, mark=kt == 1)
    most, most_int = small(1), small(1).bitcast(mybir.dt.int32)
    b.free = m = d(lambda e: e.tensor_reduce(most, b.ap[:, 128:128 + N_EXPERTS], AX.X, ALU.max), m)
    flag_ready = d(lambda e: e.tensor_copy(most_int, most), m)
    assert at[0] <= E_AT + 1024

    p.middle_for_splits()
    iota = K(K_IOTA, P)
    Sel = p.r(11264, ST, 2 * P)
    SelT = [[p.r(11776 + 512 * i + 256 * j, ST, P) for j in range(2)] for i in range(2)]
    X = [p.split_view(4096, KD, 2 * P), p.split_view(B_AT, KD, 2 * P, arena=F)]
    Y = [p.r(8192 + D * i, D) for i in range(2)]
    hidT = p.split_view(10240, 4, P)
    silu = [F(D_AT + NB * i, NB) for i in range(2)]
    hid = [F(D_AT + 1024 + NB * i, NB) for i in range(2)]
    weight = p.stat(N_EXPERTS)
    y_banks = [(t, c, B[(2, 3, 6, 7)[2 * t + c]]) for t in range(ST) for c in range(2)]
    sel_free, selT_free, x_free = None, [router_gone] * 2, [router_gone, [router_gone, p.everyone()]]
    silu_free, hid_free, hidT_free, y_free = [None] * 2, [None] * 2, router_gone, router_gone
    sel_ready, x_parts, selT_ready, w_ready, hid_ready, Y_ready = {}, {}, {}, {}, {}, {}

    def choose(pair):
        sel_ready[pair] = [p.dve(lambda e, t=t, j=j: e.tensor_scalar(Sel[:, t, j * P:(j + 1) * P], iota,
                                                                    slot[:, t, 2 * pair + j:2 * pair + j + 1], None, ALU.is_equal),
                                 slot_ready, p.late_consts, sel_free) for t in range(ST) for j in range(2)]

    def gather(pair, part, b):
        x = X[pair % 2]
        for j in range(2):
            k = 2 * part + j
            terms = [(src, t) for src in (H_hi, H_lo) for t in range(ST)]
            for i, (src, t) in enumerate(terms):
                m = p.pe(lambda e, o=b.ap[:, j * 2 * P:(j + 1) * 2 * P], l=src[:, t, k * P:(k + 1) * P], r=Sel[:, t, :], i=i:
                         e.matmul(o, l, r, start=i == 0, stop=i == 3), sel_ready[pair], Hm, b.free, mark=(j == 1 and i == 3))
        hi, lo = x.hi_span(2 * part, 2), x.lo_span(2 * part, 2)
        a = p.act(lambda e: e.activation(hi, b.ap, ACT.Copy), m, x_free[pair % 2])
        b.free = l = p.dve(lambda e: e.tensor_tensor(lo, b.ap, hi.bitcast(F32), ALU.subtract), m, a)
        x_parts.setdefault(pair, []).append([a, l])

    def turn_choice(n, b):
        nonlocal sel_free
        s = Sel[:, :, (n % 2) * P:(n % 2 + 1) * P]
        sT = SelT[n // 2 % 2][n % 2]
        for t in range(ST):
            p.pe(lambda e, t=t: e.transpose(b.ap[:, t * P:(t + 1) * P], s[:, t, :].bitcast(F32), p.ident),
                 sel_ready[n // 2], b.free, mark=False)
        for t in range(ST):
            m = p.pe(lambda e, t=t: e.matmul(b.ap[:, S:S + 1], s[:, t, :].bitcast(F32), comb[:, t, n:n + 1],
                                             start=t == 0, stop=t == 1), comb_ready, mark=t == 1)
        sel_free = m
        w_ready[n] = p.act(lambda e: e.activation(weight[:, n:n + 1], b.ap[:, S:S + 1], ACT.Copy), m)
        b.free = selT_ready[n] = p.act(lambda e: e.activation(sT.rearrange("p a b -> p (a b)"), b.ap[:, 0:S], ACT.Copy),
                                       m, selT_free[n // 2 % 2])

    def turn_hid(n, b):
        h = hid[n % 2]
        p.transpose_in(lambda t, k: h[:, k * P:(k + 1) * P], [hid_ready[n], hidT_free], 4, 1, hidT, [b])
        hid_free[n % 2] = p.pe.now()

    def scatter(n):
        nonlocal y_free
        sT = SelT[n // 2 % 2][n % 2]
        for t, c, b in y_banks:
            for q in range(2):
                m = p.pe(lambda e, b=b, t=t, q=q, c=c: e.matmul(b.ap, sT[:, t, :], Y[q][:, c * NB:(c + 1) * NB],
                                                                start=(n == 0 and q == 0), stop=(n == N_EXPERTS - 1 and q == 1)),
                         selT_ready[n], Y_ready[n], b.free, mark=(b is B[7] and q == 1))
        y_free = m
        if n % 2 == 1:
            selT_free[n // 2 % 2] = m

    def tokens_of(n):
        x = X[n // 2 % 2]
        lhs = Split(lambda k, t: x.hi(k, n % 2), lambda k, t: x.lo(k, n % 2))
        lhs.ready = x_parts[n // 2]
        return lhs

    def down(n, between):
        nonlocal hidT_free
        m = p.run(p.gemm("wd", n, 4, hidT, (0,), lambda t, c: B[4 + c].ap, B[4:6]), between)
        hidT_free = m
        Y_ready[n] = []
        for c in range(2):
            hi, lo = Y[0][:, c * NB:(c + 1) * NB], Y[1][:, c * NB:(c + 1) * NB]
            a = p.act(lambda e, hi=hi, c=c: e.activation(hi, B[4 + c].ap, ACT.Copy), m, y_free)
            B[4 + c].free = l = p.dve(lambda e, hi=hi, lo=lo, c=c: e.tensor_tensor(lo, B[4 + c].ap, hi.bitcast(F32), ALU.subtract),
                                      m, a, y_free)
            Y_ready[n] += [a, l]

    choose(0)
    p.hold = False
    p.feed()
    for part, bank in enumerate((B[4], B[5], B[0], B[1])):
        gather(0, part, bank)
    turn_choice(0, B[4])
    turn_choice(1, B[5])
    for n in range(N_EXPERTS):
        i, pair, odd = n % 2, n // 2 + 1, n % 2
        more = pair < N_EXPERTS // 2
        parts = (2, 3) if odd else (0, 1)
        steps = {j: [] for j in range(12)}
        if n >= 1:
            steps[0].append(lambda: turn_hid(n - 1, B[1]))
        if more and not odd:
            steps[1].append(lambda: choose(pair))
        if n >= 2:
            steps[2].append(lambda: scatter(n - 2))
        if more:
            steps[4].append(lambda: gather(pair, parts[0], B[4]))
            steps[5].append(lambda: gather(pair, parts[1], B[5]))
            if odd:
                steps[9].append(lambda: turn_choice(2 * pair, B[0]))
                steps[10].append(lambda: turn_choice(2 * pair + 1, B[1]))
        part_of = lambda first: {j: steps[first + j] for j in range(4)}
        lhs = tokens_of(n)
        mg = p.run(p.gemm("wg", n, KD, lhs, (0,), lambda t, c: B[0].ap, B[0:1]), part_of(0))
        B[0].free = a = p.act(lambda e, i=i: e.activation(silu[i], B[0].ap, ACT.Silu), mg, silu_free[i])
        mu = p.run(p.gemm("wu", n, KD, lhs, (0,), lambda t, c: B[1].ap, B[1:2]), part_of(4))
        if odd:
            x_free[n // 2 % 2] = mu
        B[1].free = hid_ready[n] = silu_free[i] = p.dve(
            lambda e, i=i, n=n: e.scalar_tensor_tensor(out=hid[i], in0=silu[i], scalar=weight[:, n:n + 1], in1=B[1].ap,
                                                       op0=ALU.mult, op1=ALU.mult), mu, a, w_ready[n], hid_free[i])
        if n >= 1:
            down(n - 1, part_of(8))
    last = N_EXPERTS - 1
    turn_hid(last, B[0])
    down(last, {2: [lambda: scatter(last - 1)]})
    p.y_banks = y_banks
    overflow(p, most_int[0:1, 0:1], flag_ready, H_hi, H_lo, comb, slot, slot_ready)
    scatter(last)
    p.y_ready = [y_free]


def overflow(p, flag, flag_ready, H_hi, H_lo, comb, slot, slot_ready):
    B, F = p.banks, p.f
    sem = lambda n: p.ctx.enter_context(p.nc.semaphore(n))
    pe, dve, act, pool, sp = (Lane(n, sem("over_" + n)) for n in ("pe", "dve", "act", "pool", "sp"))
    lines = [Line(sem(f"over_weights_{i}")) for i in range(3)]
    before = [p.pe.now(), p.dve.now(), p.act.now()]
    slot2 = p.stat(2 * N_EXPERTS).rearrange("p (t e) -> p t e", t=ST)
    weight = p.stat(1)
    X, Y = F(M_AT, KD, P), F(M_AT + D, D)
    sel, selT = F(T_AT, ST, P), F(T_AT + 256, ST, P)
    hid, silu, hidT = F(T_AT + 512, NB), F(T_AT + 1024, NB), F(T_AT + 1536, 4, P)
    raw = [p.raw[:, 0:4096], p.raw[:, 4096:8192]]
    iota = p.k(K_IOTA, P)
    state = {"m": dve(lambda e: e.tensor_scalar(slot2, slot, -float(SLOTS), None, ALU.add), before, slot_ready)}

    def expert(n):
        start = state["m"]
        wg_in = sp.dma(lambda e: e.dma_start(raw[0], p.dram["wg"][n]), lines[0], start)
        wu_in = sp.dma(lambda e: e.dma_start(raw[1], p.dram["wu"][n]), lines[1], start)
        ms = [dve(lambda e, t=t: e.tensor_scalar(sel[:, t, :], iota, slot2[:, t, n:n + 1], None, ALU.is_equal), start)
              for t in range(ST)]
        xs = []
        for half in range(2):
            bank = B[4 + half]
            for k in range(4 * half, 4 * half + 4):
                parts = [(src, t) for src in (H_hi, H_lo) for t in range(ST)]
                for j, (src, t) in enumerate(parts):
                    m = pe(lambda e, o=bank.ap[:, (k % 4) * P:(k % 4 + 1) * P], l=src[:, t, k * P:(k + 1) * P].bitcast(F32),
                           r=sel[:, t, :], j=j: e.matmul(o, l, r, start=j == 0, stop=j == 3), ms, start, mark=(j == 3 and k % 4 == 3))
            xs.append(act(lambda e, o=X[:, 4 * half:4 * half + 4, :].rearrange("p a b -> p (a b)"), i=bank.ap:
                          e.activation(o, i, ACT.Copy), m))
        for t in range(ST):
            pe(lambda e, t=t: e.transpose(B[0].ap[:, t * P:(t + 1) * P], sel[:, t, :], p.ident), mark=False)
        for t in range(ST):
            m = pe(lambda e, t=t: e.matmul(B[0].ap[:, S:S + 1], sel[:, t, :], comb[:, t, n:n + 1], start=t == 0, stop=t == 1),
                   mark=t == 1)
        w = act(lambda e: e.activation(weight, B[0].ap[:, S:S + 1], ACT.Copy), m)
        selT_in = act(lambda e: e.activation(selT.rearrange("p a b -> p (a b)"), B[0].ap[:, 0:S], ACT.Copy), m)
        mg = mu = None
        for k in range(KD):
            mg = pe(lambda e, k=k: e.matmul(B[0].ap, X[:, k, :], raw[0][:, k * NB:(k + 1) * NB], start=k == 0, stop=k == KD - 1),
                    xs, selT_in, wg_in, mark=k == KD - 1)
        for k in range(KD):
            mu = pe(lambda e, k=k: e.matmul(B[1].ap, X[:, k, :], raw[1][:, k * NB:(k + 1) * NB], start=k == 0, stop=k == KD - 1),
                    wu_in, mark=k == KD - 1)
        wd_in = sp.dma(lambda e: e.dma_start(raw[0], p.dram["wd"][n]), lines[2], mg)
        a = act(lambda e: e.activation(silu, B[0].ap, ACT.Silu), mg)
        r = dve(lambda e: e.scalar_tensor_tensor(out=hid, in0=silu, scalar=weight, in1=B[1].ap, op0=ALU.mult, op1=ALU.mult),
                a, w, mu)
        for k in range(4):
            m = pe(lambda e, k=k: e.transpose(B[4].ap[:, k * P:(k + 1) * P], hid[:, k * P:(k + 1) * P], p.ident), r, mark=k == 3)
        a = act(lambda e: e.activation(hidT.rearrange("p a b -> p (a b)"), B[4].ap, ACT.Copy), m)
        for c in range(2):
            for k in range(4):
                m = pe(lambda e, k=k, c=c: e.matmul(B[4 + c].ap, hidT[:, k, :], raw[0][:, (2 * k + c) * NB:(2 * k + c + 1) * NB],
                                                    start=k == 0, stop=k == 3), a, wd_in, mark=k == 3)
        ys = [act(lambda e, c=c: e.activation(Y[:, c * NB:(c + 1) * NB], B[4 + c].ap, ACT.Copy), m) for c in range(2)]
        for t, c, bank in p.y_banks:
            m = pe(lambda e, bank=bank, t=t, c=c: e.matmul(bank.ap, selT[:, t, :], Y[:, c * NB:(c + 1) * NB], start=False, stop=False),
                   ys, selT_in)
        state["m"] = [m, ys]

    for n in range(N_EXPERTS):
        expert(n)
    ends = [pe.now(), dve.now(), act.now()] + [(l.sem, l.count) for l in lines]
    for main, section in ((p.pe, pe), (p.dve, dve), (p.act, act), (p.sp, sp)):
        section.ops.append((section.needed(ends), lambda e: e.nop(), None, 0))
        main.only_if(flag, SLOTS + 1, flag_ready, section)


def shape_constants():
    f = np.float32
    t = np.arange(S)
    q = np.arange(P)
    out = {"ident": np.eye(P, dtype=f)}
    sel = np.zeros((P, 130), f)
    for base in (0, 32, 64):
        sel[[base, base + 1, base + 4], 0:P] = 1.0
        sel[[base, base + 1, base + 4], P] = 1.0
        sel[[base + 2, base + 3, base + 4], P + 1] = 1.0
    out["sel"] = sel
    dist = -np.abs(t[:, None] - t[None, :]).astype(f)
    allowed = (t[None, :] // CHUNK) <= (t[:, None] // CHUNK)
    dist = np.where(allowed, dist, f(BIG)).astype(f)
    out["dist"] = np.ascontiguousarray(dist.reshape(ST, P, S).transpose(1, 0, 2))
    slopes = np.array([2.0 ** (-8.0 * (i + 1) / HEADS) for i in range(HEADS)], dtype=f)
    out["slopes"] = np.ascontiguousarray((np.eye(P, dtype=f)[:, None, :] * slopes[None, :, None]).astype(f))
    m = np.zeros((4, S, S), f)
    for g, w in enumerate(POOL_WINDOWS):
        lo = np.maximum(t + 1 - w, 0)
        for i in t:
            m[g, lo[i]:i + 1, i] = 1.0 / (i + 1 - lo[i])
            m[g, i, i] -= 1.0
    out["pool_m"] = np.ascontiguousarray(m.reshape(4, ST, P, S).transpose(2, 0, 1, 3))
    half = ROPE // 2
    freq = (10000.0 ** (-np.arange(0, half, 2, dtype=f) / half)).astype(f)
    ang = np.concatenate([(t // GRID_W).astype(f)[:, None] * freq, (t % GRID_W).astype(f)[:, None] * freq], axis=-1)
    rope = np.stack([np.cos(ang), np.sin(ang)]).astype(f)
    out["rope"] = np.ascontiguousarray(rope.reshape(2, ST, P, half).transpose(2, 1, 0, 3))
    col = np.arange(GRID_W)
    start = np.clip(col - WIN_W // 2, 0, GRID_W - WIN_W)
    inside = (col[None, :] >= start[:, None]) & (col[None, :] < start[:, None] + WIN_W)
    out["col_mask"] = np.where(inside, f(0), f(BIG))[q % GRID_W].astype(f)
    out["tri"] = np.ascontiguousarray((t[:, None] < t[None, :]).astype(f).reshape(ST, P, S).transpose(1, 0, 2))
    out["iota"] = np.tile(np.arange(P, dtype=f), (P, 1))
    return out


def by_chunk(w, n):
    k, cols = w.shape
    return np.ascontiguousarray(w.reshape(k // P, P, cols // n, n).transpose(2, 1, 0, 3)).reshape(cols // n, P, -1)


def by_rows(w, rows):
    k, cols = w.shape
    return np.ascontiguousarray(w.reshape(k // rows, rows // P, P, cols).transpose(0, 2, 1, 3)).reshape(k // rows, P, -1)


def lay_out(a):
    o = dict(shape_constants())
    o["x"] = a["x"][0]
    col = lambda v: v.reshape(-1, P).T
    vectors = {"g_mix": a["g_mix"][0], "g_ffn": a["g_ffn"][0], "norm_attn_g": a["norm_attn_g_2"][0],
               "pool_scale": a["pool_scale"][0], "g_q": np.concatenate([a["g_q"][0]] * 2), "g_k": np.concatenate([a["g_k"][0]] * 2),
               "g_sub": a["g_sub"][0], "q_a_g": a["q_a_norm_g_2"][0], "kv_a_g": a["kv_a_norm_g_2"][0],
               "c": a["c_2"][0], "c_ctx": a["c_ctx_2"]}
    o["cols"] = np.ascontiguousarray(np.concatenate([col(vectors[n]) for n, _ in COLS], axis=1))
    o["lambda_rows"] = a["lambda_qk"][0].reshape(1, 256)
    o["b_gate"] = a["b_gate"][0].reshape(1, -1)
    o["b_mod"] = a["b_mod_2"][0].reshape(12, NB)
    o["w_grp"] = np.ascontiguousarray(a["w_pool_grp"][0].transpose(1, 0, 2))
    o["w_in"] = by_chunk(a["w_in"][0], 512)
    o["w_gate"] = by_chunk(a["w_gate"][0], 512)
    o["w_bp"] = by_rows(a["w_branch_pool"][0], 512)
    o["w_ba"] = by_rows(a["w_branch_attn"][0], 512)
    o["w_out"] = by_chunk(a["w_out"][0], 512)
    o["w_up"] = by_chunk(a["w_up"][0], 512)
    o["w_down"] = by_rows(a["w_down"][0], 512)
    o["w_mod"] = by_chunk(a["w_mod_2"][0], 512)
    w = a["w_in_2"][0]
    c0 = Q_LORA + 512
    o["w_in2q"] = by_chunk(np.ascontiguousarray(w[:, 0:Q_LORA]), Q_LORA)
    o["w_in2nq"] = by_chunk(np.ascontiguousarray(w[:, Q_LORA:c0]), 512)
    o["w_in2kv"] = by_chunk(np.ascontiguousarray(w[:, c0:c0 + 288]), 288)
    o["w_in2k"] = by_chunk(np.ascontiguousarray(w[:, c0 + 288:c0 + 800]), 512)
    o["w_in2v"] = by_chunk(np.ascontiguousarray(w[:, c0 + 800:c0 + 1312]), 512)
    o["w_uq"] = by_rows(a["w_uq_2"][0], Q_LORA)
    o["w_ukv"] = by_chunk(a["w_ukv_2"][0], 512)
    o["w_out2"] = by_chunk(a["w_out_2"][0], 512)
    wg, wu, wd = a["w_gate_2"][0], a["w_up_2"][0], a["w_down_2"][0]
    o["wg"] = np.stack([by_chunk(wg[e], 512)[0] for e in range(N_EXPERTS)])
    o["wu"] = np.stack([by_chunk(wu[e], 512)[0] for e in range(N_EXPERTS)])
    o["wd"] = np.stack([by_rows(wd[e], 512)[0] for e in range(N_EXPERTS)])
    o["ctx"] = a["ctx_2"][0]
    o["norm_ffn_g"] = a["norm_ffn_g_2"][0].reshape(1, D)
    o["final_g"] = a["final_norm_g_2"].reshape(1, D)
    o["w_router"] = np.ascontiguousarray(np.concatenate([a["w_router_group_2"][0], a["w_router_expert_2"][0]], axis=1)
                                         .reshape(KD, P, 20).transpose(1, 0, 2))
    o["b_router"] = np.concatenate([a["b_router_group_2"][0], a["b_router_expert_2"][0]]).reshape(1, 20)
    rb = a["na_rel_bias_2"][0]
    pad = np.pad(rb, ((0, 0), (0, 0), (48, 48)))
    rows = np.stack([pad[:, :, 63 - q:127 - q] for q in range(GRID_W)], axis=1)
    tiles = [np.concatenate([rows[:, :, 7 - r:11 - r].reshape(HEADS, GRID_W, S) for r in (2 * t, 2 * t + 1)], axis=1)
             for t in range(ST)]
    o["rel_rows"] = np.ascontiguousarray(np.stack(tiles, axis=2))
    return {k: v if v.dtype == np.float32 and v.flags.c_contiguous else np.ascontiguousarray(v) for k, v in o.items()}


BROADCAST = ("lambda_rows", "b_gate", "norm_ffn_g", "final_g", "b_router")


def build(nc, arrays, upto=None):
    dram = {}
    for name, a in arrays.items():
        ap = nc.dram_tensor("in_" + name, list(a.shape), F32, kind="ExternalInput").ap()
        if name in BROADCAST:
            ap = ap.rearrange("a b -> (a b)").partition_broadcast(P)
        dram[name] = ap
    dram["lambda_rows"] = dram["lambda_rows"].rearrange("p (a b) -> p a b", a=4)
    with ExitStack() as ctx:
        p = Program(nc, ctx, dram, upto)
        try:
            begin(p)
            block_one(p)
            block_two(p)
        except Stop:
            ap, marks = p.store
            out = nc.dram_tensor("out", [P, ap.shape[-1]], F32, kind="ExternalOutput").ap()
            p.out_mark = p.load(out, ap, marks, lane=p.act)
            p.act.ops.append((p.act.needed([(l.sem, l.count) for l in p.lines if l.count]), lambda e: e.nop(), None, 0))
        block = ctx.enter_context(nc.Block())

        @block.sync
        def _(eng):
            p.sp.play(eng)

        @block.scalar
        def _(eng):
            p.act.play(eng)

        @block.vector
        def _(eng):
            p.dve.play(eng)

        @block.gpsimd
        def _(eng):
            p.pool.play(eng)

        @block.tensor
        def _(eng):
            p.pe.play(eng)


def kernel(**inputs):
    from concourse import bacc
    from concourse.bass_utils import run_bass_kernel_spmd

    arrays = lay_out({k: np.asarray(v) for k, v in inputs.items()})
    nc = bacc.Bacc("TRN2", target_bir_lowering=False, num_devices=1)
    build(nc, arrays)
    r = run_bass_kernel_spmd(nc, [{"in_" + k: v for k, v in arrays.items()}], core_ids=[0])
    return r.results[0]["out"].reshape(1, S, D)
```
